# Optimizing a Trainium2 kernel written in Bass

```python
import jax, jax.numpy as jnp
from jax import lax
import numpy as np
import math

D_MODEL = 1024
BATCH = 1
SEQ = 256
DEPTH = 2

CHUNK = 64
Q_BLOCK = 128
HEAD_DIM = 64
ATTN_HEADS = D_MODEL // 128
CONV_GROUPS = D_MODEL // 256
HGRN_HEADS = D_MODEL // 256
CONV_WIDTH = 3
ATTN_W = ATTN_HEADS * HEAD_DIM
CONV_C = CONV_GROUPS * HEAD_DIM
HGRN_W = HGRN_HEADS * HEAD_DIM
D_MIX = ATTN_W + CONV_C + HGRN_W
IN_SIZES = (ATTN_W, ATTN_W, ATTN_W, ATTN_HEADS,
            CONV_C, CONV_C, CONV_C,
            HGRN_W, HGRN_W, HGRN_W, HGRN_W)
D_IN = sum(IN_SIZES)
IN_SPLITS = [int(v) for v in np.cumsum(IN_SIZES)[:-1]]
D_FF = (7 * D_MODEL) // 2
N_EXPERTS = 8
TOP_K = 2
N_DENSE = (DEPTH + 1) // 2
N_MOE = DEPTH // 2
EPS = 1e-6
FORGET_BIAS_MEAN = 3.0
MASK_VALUE = -1e30
MASK_LOG_DECAY = -1e4
TINY = 1e-30


def rms(x):
    xf = x.astype(jnp.float32)
    return xf * lax.rsqrt(jnp.mean(xf * xf, axis=-1, keepdims=True) + EPS)

def rms_norm(x, g):
    return (rms(x) * g.astype(jnp.float32)).astype(x.dtype)

def swiglu(x, w_gate, w_up, w_down):
    return (jax.nn.silu(x @ w_gate) * (x @ w_up)) @ w_down

def forgetting_attention(q, k, v, f_logit, g_q, g_k):
    B, S, H, Dh = q.shape
    q = rms(q) * g_q.astype(jnp.float32)
    k = rms(k) * g_k.astype(jnp.float32)
    v = v.astype(jnp.float32)
    dcum = jnp.cumsum(jax.nn.log_sigmoid(f_logit.astype(jnp.float32)), axis=1)
    scale = np.float32(1.0 / np.sqrt(Dh))
    nb = S // Q_BLOCK
    q_blocks = q.reshape(B, nb, Q_BLOCK, H, Dh).transpose(1, 0, 3, 2, 4)
    d_blocks = dcum.reshape(B, nb, Q_BLOCK, H).transpose(1, 0, 3, 2)
    k_t = k.transpose(0, 2, 1, 3)
    v_t = v.transpose(0, 2, 1, 3)
    d_k = dcum.transpose(0, 2, 1)
    k_pos = jnp.arange(S)

    def block(args):
        q_i, d_i, i = args
        q_pos = i * Q_BLOCK + jnp.arange(Q_BLOCK)
        logits = (jnp.einsum('bhqd,bhkd->bhqk', q_i, k_t) * scale
                  + d_i[..., None] - d_k[:, :, None, :])
        mask = k_pos[None, :] <= q_pos[:, None]
        p = jax.nn.softmax(jnp.where(mask, logits, MASK_VALUE), axis=-1)
        return jnp.einsum('bhqk,bhkd->bhqd', p, v_t)

    o = lax.map(block, (q_blocks, d_blocks, jnp.arange(nb)))
    return o.transpose(1, 0, 3, 2, 4).reshape(B, S, H * Dh)

def short_conv(x_in, b_gate, c_gate, w):
    S = x_in.shape[1]
    u = (c_gate * x_in).astype(jnp.float32)
    up = jnp.pad(u, ((0, 0), (CONV_WIDTH - 1, 0), (0, 0)))
    wf = w.astype(jnp.float32)
    y = up[:, 0:S] * wf[0]
    for j in range(1, CONV_WIDTH):
        y = y + up[:, j:j + S] * wf[j]
    return b_gate.astype(jnp.float32) * y

def hgrn2(q, f_logit, i_in, lb):
    B, S, H, d = q.shape
    q = jax.nn.silu(q.astype(jnp.float32))
    z = f_logit.astype(jnp.float32)
    lb = lb.reshape(H, d).astype(jnp.float32)
    f = lb + (1.0 - lb) * jax.nn.sigmoid(z)
    log_f = jnp.log(jnp.maximum(f, TINY))
    k = (1.0 - lb) * jax.nn.sigmoid(-z)
    v = i_in.astype(jnp.float32)
    n_chunks = S // CHUNK

    def to_chunks(t):
        return t.reshape(B, n_chunks, CHUNK, H, d).transpose(1, 0, 3, 2, 4)

    causal = jnp.tril(jnp.ones((CHUNK, CHUNK), dtype=bool))

    def step(state, inp):
        q_c, k_c, v_c, l_c = inp
        c = jnp.cumsum(l_c, axis=2)
        o_inter = jnp.einsum('bhtk,bhkv->bhtv', q_c * jnp.exp(c), state)
        diff = c[:, :, :, None, :] - c[:, :, None, :, :]
        decay = jnp.exp(jnp.where(causal[:, :, None], diff, MASK_LOG_DECAY))
        a = jnp.einsum('bhtk,bhsk,bhtsk->bhts', q_c, k_c, decay)
        o = o_inter + jnp.einsum('bhts,bhsv->bhtv', a, v_c)
        c_last = c[:, :, -1:, :]
        k_dec = k_c * jnp.exp(c_last - c)
        state = (jnp.exp(c_last[:, :, 0, :])[..., None] * state
                 + jnp.einsum('bhsk,bhsv->bhkv', k_dec, v_c))
        return state, o

    state0 = jnp.zeros((B, H, d, d), jnp.float32)
    _, o = lax.scan(step, state0, (to_chunks(q), to_chunks(k), to_chunks(v), to_chunks(log_f)))
    return o.transpose(1, 0, 3, 2, 4).reshape(B, S, H * d)

def moe_swiglu(h, w_router, b_router, w_gate, w_up, w_down):
    B, S, D = h.shape
    t = h.reshape(B * S, D)
    logits = (t @ w_router).astype(jnp.float32) + b_router.astype(jnp.float32)
    top_v, top_i = lax.top_k(logits, TOP_K)
    top_w = jax.nn.softmax(top_v, axis=-1)
    gates = jnp.sum(jax.nn.one_hot(top_i, N_EXPERTS, dtype=jnp.float32) * top_w[..., None], axis=1)
    out = jnp.zeros_like(t)
    for e in range(N_EXPERTS):
        out = out + gates[:, e:e + 1].astype(t.dtype) * swiglu(t, w_gate[e], w_up[e], w_down[e])
    return out.reshape(B, S, D)

def first_inputs(seed: int = 0) -> dict:
    key = jax.random.key(seed)
    ks = jax.random.split(key, 24)
    f32 = jnp.float32
    nrm = lambda k, shape, s: jax.random.normal(k, shape, f32) * s
    return {
        "x": nrm(ks[0], (BATCH, SEQ, D_MODEL), 1.0),
        "norm_mix": 1.0 + nrm(ks[1], (DEPTH, D_MODEL), 0.02),
        "w_in": nrm(ks[2], (DEPTH, D_MODEL, D_IN), D_MODEL ** -0.5),
        "attn_f_bias": FORGET_BIAS_MEAN + nrm(ks[3], (DEPTH, ATTN_HEADS), 0.1),
        "q_norm_gain": 1.0 + nrm(ks[4], (DEPTH, HEAD_DIM), 0.02),
        "k_norm_gain": 1.0 + nrm(ks[5], (DEPTH, HEAD_DIM), 0.02),
        "conv_w": nrm(ks[6], (DEPTH, CONV_WIDTH, CONV_C), CONV_WIDTH ** -0.5),
        "hgrn_lb_logits": nrm(ks[7], (DEPTH, HGRN_W), 0.1),
        "mix_out_gain": 1.0 + nrm(ks[8], (DEPTH, D_MIX), 0.02),
        "w_out": nrm(ks[9], (DEPTH, D_MIX, D_MODEL), D_MIX ** -0.5),
        "norm_ffn": 1.0 + nrm(ks[10], (DEPTH, D_MODEL), 0.02),
        "ffn_w_gate": nrm(ks[11], (N_DENSE, D_MODEL, D_FF), D_MODEL ** -0.5),
        "ffn_w_up": nrm(ks[12], (N_DENSE, D_MODEL, D_FF), D_MODEL ** -0.5),
        "ffn_w_down": nrm(ks[13], (N_DENSE, D_FF, D_MODEL), D_FF ** -0.5),
        "moe_router_w": nrm(ks[14], (N_MOE, D_MODEL, N_EXPERTS), D_MODEL ** -0.5),
        "moe_router_b": nrm(ks[15], (N_MOE, N_EXPERTS), 0.01),
        "moe_w_gate": nrm(ks[16], (N_MOE, N_EXPERTS, D_MODEL, D_FF), D_MODEL ** -0.5),
        "moe_w_up": nrm(ks[17], (N_MOE, N_EXPERTS, D_MODEL, D_FF), D_MODEL ** -0.5),
        "moe_w_down": nrm(ks[18], (N_MOE, N_EXPERTS, D_FF, D_MODEL), D_FF ** -0.5),
    }

def first_block(x, norm_mix, w_in, attn_f_bias, q_norm_gain, k_norm_gain, conv_w,
              hgrn_lb_logits, mix_out_gain, w_out, norm_ffn, ffn_w_gate, ffn_w_up,
              ffn_w_down, moe_router_w, moe_router_b, moe_w_gate, moe_w_up, moe_w_down):
    B, S, _ = x.shape
    dt = x.dtype
    p_lb = jax.nn.softmax(hgrn_lb_logits.astype(jnp.float32), axis=0)
    lb_all = jnp.cumsum(p_lb, axis=0) - p_lb[0]
    for l in range(DEPTH):
        h = rms_norm(x, norm_mix[l])
        z = h @ w_in[l]
        (a_q, a_k, a_v, a_f, c_x, c_b, c_c,
         r_q, r_f, r_i, r_g) = jnp.split(z, IN_SPLITS, axis=-1)
        a_f = a_f + attn_f_bias[l].astype(dt)
        y_a = forgetting_attention(a_q.reshape(B, S, ATTN_HEADS, HEAD_DIM),
                                   a_k.reshape(B, S, ATTN_HEADS, HEAD_DIM),
                                   a_v.reshape(B, S, ATTN_HEADS, HEAD_DIM),
                                   a_f, q_norm_gain[l], k_norm_gain[l])
        y_c = short_conv(c_x, c_b, c_c, conv_w[l])
        y_r = hgrn2(r_q.reshape(B, S, HGRN_HEADS, HEAD_DIM),
                    r_f.reshape(B, S, HGRN_HEADS, HEAD_DIM),
                    r_i.reshape(B, S, HGRN_HEADS, HEAD_DIM), lb_all[l])
        y = jnp.concatenate([y_a, y_c, y_r], axis=-1)
        y = rms(y.reshape(B, S, D_MIX // HEAD_DIM, HEAD_DIM)).reshape(B, S, D_MIX)
        y = y * mix_out_gain[l].astype(jnp.float32)
        y = jnp.concatenate([y[..., :ATTN_W + CONV_C],
                             y[..., ATTN_W + CONV_C:] * jax.nn.silu(r_g.astype(jnp.float32))], axis=-1)
        x = x + y.astype(dt) @ w_out[l]
        h = rms_norm(x, norm_ffn[l])
        if l % 2 == 0:
            j = l // 2
            x = x + swiglu(h, ffn_w_gate[j], ffn_w_up[j], ffn_w_down[j])
        else:
            j = l // 2
            x = x + moe_swiglu(h, moe_router_w[j], moe_router_b[j],
                               moe_w_gate[j], moe_w_up[j], moe_w_down[j])
    return x


GRID_W = 64

A_HEADS = 8
A_KV_HEADS = 2
A_GROUP = A_HEADS // A_KV_HEADS
A_HEAD_DIM = 64
AXIAL_THETA = 10000.0

B_HEADS = 8
B_QK_DIM = 32
B_V_DIM = 2 * B_QK_DIM
B_ROT_DIM = B_QK_DIM // 4
ROPE_THETA = 500000.0

C_HEADS = 8
C_Q_RANK = 384
C_KV_RANK = 256
C_NOPE_DIM = 64
C_ROPE_DIM = 32
C_V_DIM = 64
MLA_THETA = 10000.0

N_BRANCH = 3
BRANCH_W = 512
D_FF_2 = 4 * D_MODEL

A_Q_W = A_HEADS * A_HEAD_DIM
A_KV_W = A_KV_HEADS * A_HEAD_DIM
B_QK_W = B_HEADS * 2 * B_QK_DIM
B_V_W = B_HEADS * B_V_DIM
GATE_W = N_BRANCH * D_MODEL
IN_SIZES_2 = (A_Q_W, A_KV_W, A_KV_W, B_QK_W, B_QK_W, B_V_W, C_Q_RANK, C_KV_RANK, C_ROPE_DIM, GATE_W)
IN_COLS = A_Q_W + 2 * A_KV_W + 2 * B_QK_W + B_V_W + C_Q_RANK + C_KV_RANK + C_ROPE_DIM + GATE_W


def _rms_norm(x, g):
    xf = x.astype(jnp.float32)
    y = xf * lax.rsqrt(jnp.mean(xf * xf, axis=-1, keepdims=True) + EPS)
    return (y * g.astype(jnp.float32)).astype(x.dtype)

def _angles(pos, dim, theta):
    inv_freq = theta ** (-jnp.arange(0, dim, 2, dtype=jnp.float32) / dim)
    return pos.astype(jnp.float32)[:, None] * inv_freq[None, :]

def _rotate(x, ang):
    cos = jnp.cos(ang)[:, None, :].astype(x.dtype)
    sin = jnp.sin(ang)[:, None, :].astype(x.dtype)
    x1, x2 = jnp.split(x, 2, axis=-1)
    return jnp.concatenate([x1 * cos - x2 * sin, x2 * cos + x1 * sin], axis=-1)

def _softmax_f32(s):
    return jax.nn.softmax(s.astype(jnp.float32), axis=-1)

def _sweep_query_blocks(block_fn, *qs):
    b, s = qs[0].shape[:2]
    nb = s // Q_BLOCK
    blocked = tuple(jnp.swapaxes(q.reshape((b, nb, Q_BLOCK) + q.shape[2:]), 0, 1) for q in qs)
    out = lax.map(lambda qb: block_fn(*qb), blocked)
    out = jnp.swapaxes(out, 0, 1)
    return out.reshape((b, s) + out.shape[3:])

def _split_columns(p):
    out, start = [], 0
    for n in IN_SIZES_2:
        out.append(p[..., start:start + n])
        start += n
    return out

def _gqa_axial(q, k, v, q_g, k_g, row_ang, col_ang):
    b, s = q.shape[:2]
    half = A_HEAD_DIM // 2

    def axial(t):
        return jnp.concatenate([_rotate(t[..., :half], row_ang), _rotate(t[..., half:], col_ang)], axis=-1)

    q = axial(_rms_norm(q, q_g)) * (A_HEAD_DIM ** -0.5)
    k = axial(_rms_norm(k, k_g))
    q = q.reshape(b, s, A_KV_HEADS, A_GROUP, A_HEAD_DIM)

    def block(qb):
        sc = jnp.einsum('bqkgd,bskd->bkgqs', qb, k)
        p = _softmax_f32(sc).astype(v.dtype)
        return jnp.einsum('bkgqs,bskd->bqkgd', p, v)

    o = _sweep_query_blocks(block, q)
    return o.reshape(b, s, A_HEADS * A_HEAD_DIM)

def _diff_attention(q, k, v, lam_p, sub_g, lambda_init, rot_ang):
    b, s = q.shape[:2]

    def partial_rot(t):
        t = t.reshape(b, s, B_HEADS * 2, B_QK_DIM)
        t = jnp.concatenate([_rotate(t[..., :B_ROT_DIM], rot_ang), t[..., B_ROT_DIM:]], axis=-1)
        return t.reshape(b, s, B_HEADS, 2, B_QK_DIM)

    q = partial_rot(q) * (B_QK_DIM ** -0.5)
    k = partial_rot(k)
    v = v.reshape(b, s, B_HEADS, B_V_DIM)
    lf = lam_p.astype(jnp.float32)
    lam = jnp.exp(jnp.sum(lf[0] * lf[1])) - jnp.exp(jnp.sum(lf[2] * lf[3])) + lambda_init

    def block(qb):
        sc = jnp.einsum('bqhcd,bshcd->bhcqs', qb, k)
        p = _softmax_f32(sc)
        p = (p[:, :, 0] - lam * p[:, :, 1]).astype(v.dtype)
        return jnp.einsum('bhqs,bshe->bqhe', p, v)

    o = _sweep_query_blocks(block, q)
    o = _rms_norm(o, sub_g) * (1.0 - lambda_init)
    return o.reshape(b, s, B_HEADS * B_V_DIM)

def _mla(c_q, c_kv, k_r, q_g, kv_g, w_uq, w_ukv, ang):
    b, s = c_q.shape[:2]
    q = jnp.einsum('bsr,rn->bsn', _rms_norm(c_q, q_g), w_uq).reshape(b, s, C_HEADS, C_NOPE_DIM + C_ROPE_DIM)
    kv = jnp.einsum('bsr,rn->bsn', _rms_norm(c_kv, kv_g), w_ukv).reshape(b, s, C_HEADS, C_NOPE_DIM + C_V_DIM)
    scale = (C_NOPE_DIM + C_ROPE_DIM) ** -0.5
    q_nope = q[..., :C_NOPE_DIM] * scale
    q_rope = _rotate(q[..., C_NOPE_DIM:], ang) * scale
    k_nope, v = kv[..., :C_NOPE_DIM], kv[..., C_NOPE_DIM:]
    k_rope = _rotate(k_r[:, :, None, :], ang)[:, :, 0]

    def block(qn, qr):
        sc = jnp.einsum('bqhd,bshd->bhqs', qn, k_nope) + jnp.einsum('bqhr,bsr->bhqs', qr, k_rope)
        p = _softmax_f32(sc).astype(v.dtype)
        return jnp.einsum('bhqs,bshe->bqhe', p, v)

    o = _sweep_query_blocks(block, q_nope, q_rope)
    return o.reshape(b, s, C_HEADS * C_V_DIM)

def second_inputs(seed: int = 0) -> dict:
    key = jax.random.key(seed)
    ks = jax.random.split(key, 20)
    f32 = jnp.float32

    def nrm(k, shape, scale):
        return jax.random.normal(k, shape, f32) * scale

    def gain(k, shape):
        return 1.0 + 0.02 * jax.random.normal(k, shape, f32)

    return {
        'x': jax.random.normal(ks[0], (BATCH, SEQ, D_MODEL), f32),
        'ln1_g': gain(ks[1], (DEPTH, D_MODEL)),
        'w_in': nrm(ks[2], (DEPTH, D_MODEL, IN_COLS), D_MODEL ** -0.5),
        'a_q_norm': gain(ks[3], (DEPTH, A_HEAD_DIM)),
        'a_k_norm': gain(ks[4], (DEPTH, A_HEAD_DIM)),
        'b_lambda': nrm(ks[5], (DEPTH, 4, B_QK_DIM), 0.1),
        'b_subln': gain(ks[6], (DEPTH, B_V_DIM)),
        'c_q_norm': gain(ks[7], (DEPTH, C_Q_RANK)),
        'c_kv_norm': gain(ks[8], (DEPTH, C_KV_RANK)),
        'c_w_uq': nrm(ks[9], (DEPTH, C_Q_RANK, C_HEADS * (C_NOPE_DIM + C_ROPE_DIM)), C_Q_RANK ** -0.5),
        'c_w_ukv': nrm(ks[10], (DEPTH, C_KV_RANK, C_HEADS * (C_NOPE_DIM + C_V_DIM)), C_KV_RANK ** -0.5),
        'w_branch': nrm(ks[11], (DEPTH, N_BRANCH, BRANCH_W, D_MODEL), BRANCH_W ** -0.5),
        'w_out': nrm(ks[12], (DEPTH, D_MODEL, D_MODEL), D_MODEL ** -0.5),
        'ln2_g': gain(ks[13], (DEPTH, D_MODEL)),
        'w_ff1': nrm(ks[14], (DEPTH, D_MODEL, D_FF_2), D_MODEL ** -0.5),
        'w_ff2': nrm(ks[15], (DEPTH, D_FF_2, D_MODEL), D_FF_2 ** -0.5),
        'final_g': gain(ks[16], (D_MODEL,)),
    }

def second_block(x, ln1_g, w_in, a_q_norm, a_k_norm, b_lambda, b_subln, c_q_norm, c_kv_norm,
              c_w_uq, c_w_ukv, w_branch, w_out, ln2_g, w_ff1, w_ff2, final_g):
    b, s, d = x.shape
    n_rows = s // GRID_W
    t = jnp.arange(s)
    row_idx = jnp.repeat(jnp.arange(n_rows), GRID_W)
    col_idx = jnp.tile(jnp.arange(GRID_W), n_rows)
    half = A_HEAD_DIM // 2
    row_ang = _angles(row_idx, half, AXIAL_THETA)
    col_ang = _angles(col_idx, half, AXIAL_THETA)
    b_ang = _angles(t, B_ROT_DIM, ROPE_THETA)
    c_ang = _angles(t, C_ROPE_DIM, MLA_THETA)

    for l in range(DEPTH):
        h = _rms_norm(x, ln1_g[l])
        proj = jnp.einsum('bsd,dn->bsn', h, w_in[l])
        (a_q, a_k, a_v, b_q, b_k, b_v, c_cq, c_ckv, c_kr, gate_logits) = _split_columns(proj)

        y_a = _gqa_axial(a_q.reshape(b, s, A_HEADS, A_HEAD_DIM),
                         a_k.reshape(b, s, A_KV_HEADS, A_HEAD_DIM),
                         a_v.reshape(b, s, A_KV_HEADS, A_HEAD_DIM),
                         a_q_norm[l], a_k_norm[l], row_ang, col_ang)
        lambda_init = 0.8 - 0.6 * math.exp(-0.3 * l)
        y_b = _diff_attention(b_q, b_k, b_v, b_lambda[l], b_subln[l], lambda_init, b_ang)
        y_c = _mla(c_cq, c_ckv, c_kr, c_q_norm[l], c_kv_norm[l], c_w_uq[l], c_w_ukv[l], c_ang)

        y = jnp.stack([y_a, y_b, y_c], axis=2)
        gates = jax.nn.sigmoid(gate_logits.reshape(b, s, N_BRANCH, d))
        merged = jnp.sum(gates * jnp.einsum('bsne,ned->bsnd', y, w_branch[l]), axis=2)
        x = x + jnp.einsum('bsd,de->bse', merged, w_out[l])

        h2 = _rms_norm(x, ln2_g[l])
        ff = jnp.square(jax.nn.relu(jnp.einsum('bsd,df->bsf', h2, w_ff1[l])))
        x = x + jnp.einsum('bsf,fd->bsd', ff, w_ff2[l])

    return _rms_norm(x, final_g)


def setup_inputs(seed=0):
    out = dict(first_inputs(seed))
    for name, value in second_inputs(seed + 1).items():
        if name != "x":
            out[name + "_2"] = value
    return out


def reference(
    x, norm_mix, w_in, attn_f_bias, q_norm_gain, k_norm_gain, conv_w, hgrn_lb_logits,
    mix_out_gain, w_out, norm_ffn, ffn_w_gate, ffn_w_up, ffn_w_down, moe_router_w, moe_router_b,
    moe_w_gate, moe_w_up, moe_w_down, ln1_g_2, w_in_2, a_q_norm_2, a_k_norm_2, b_lambda_2,
    b_subln_2, c_q_norm_2, c_kv_norm_2, c_w_uq_2, c_w_ukv_2, w_branch_2, w_out_2, ln2_g_2,
    w_ff1_2, w_ff2_2, final_g_2,
):
    x = first_block(
        x, norm_mix, w_in, attn_f_bias, q_norm_gain, k_norm_gain, conv_w, hgrn_lb_logits,
        mix_out_gain, w_out, norm_ffn, ffn_w_gate, ffn_w_up, ffn_w_down, moe_router_w,
        moe_router_b, moe_w_gate, moe_w_up, moe_w_down,
    )
    return second_block(
        x, ln1_g_2, w_in_2, a_q_norm_2, a_k_norm_2, b_lambda_2, b_subln_2, c_q_norm_2,
        c_kv_norm_2, c_w_uq_2, c_w_ukv_2, w_branch_2, w_out_2, ln2_g_2, w_ff1_2, w_ff2_2,
        final_g_2,
    )


_drawn_inputs = setup_inputs


def setup_inputs(seed=0):
    import zlib

    import numpy as np

    out = dict(_drawn_inputs(seed))
    spreads = {}
    factors = {'hgrn_lb_logits': 6.948,
     'moe_router_b': 4.407,
     'ln1_g_2': 6.103,
     'a_q_norm_2': 8.0,
     'a_k_norm_2': 8.0,
     'b_lambda_2': 5.302,
     'b_subln_2': 8.0,
     'c_q_norm_2': 8.0,
     'c_kv_norm_2': 8.0,
     'ln2_g_2': 3.248,
     'final_g_2': 2.739}
    for name, (base, spread) in spreads.items():
        noise = np.random.default_rng([zlib.crc32(name.encode()), seed]).standard_normal(out[name].shape)
        drawn = base * np.exp(spread * noise) if base else spread * noise
        out[name] = __import__('jax').numpy.asarray(drawn.astype(out[name].dtype))
    for name, factor in factors.items():
        out[name] = (out[name] * factor).astype(out[name].dtype)
    return out
```

```python
from contextlib import ExitStack

import numpy as np

import concourse.bass as bass
from concourse import mybir

F32 = mybir.dt.float32
F32R = mybir.dt.float32r
ACT = mybir.ActivationFunctionType
ALU = mybir.AluOpType
AX = mybir.AxisListType.X

P = 128
S = 256
NT = S // P
D = 1024
DK = D // P
DEPTH = 2
HD = 64
NH = 8
HEAD_AT = [0, 2, 4, 6, 1, 3, 5, 7]
UNIT = 2048
UC = UNIT // DK
RAW, SPLIT = 3, 3
LEAD = 2
EPS = 1e-6
TINY = 1e-30
LN_CUT = 2.0 ** -60
NEG = -1e30

D_FF = 3584
G1 = D_FF // UC
NE = 8
GM = G1 * NE
D_FF2 = 4096
G2 = D_FF2 // UC
LEVELS = 8

U_BLK1 = 2 + 2 + 2 + 3 + 4 + 4
U_FFN = 3 * G1
U_MOE = 3 * GM
U_BLK2 = 2 + 1 + 6 + 3 + 2 + 1 + 12 + 6 + 4 + 2 * G2

LAYER_STEPS = (51, 102, 169)

V1 = dict(norm_mix=(0, 8), norm_ffn=(8, 16), mix_gain=(16, 24), qg=(24, 25), kg=(25, 26),
          conv=(26, 32), fbias=(32, 40), wf=(40, 104))
V1N = 104
V2 = dict(ln1=(0, 8), ln2=(8, 16), aq=(16, 17), ak=(17, 18), bsub=(18, 19), cq=(19, 22),
          ckv=(22, 24), lam=(24, 152), lam_init=(152, 153))
V2N = 153
LAMBDA_INIT = [0.8 - 0.6 * float(np.exp(-0.3 * l)) for l in range(DEPTH)]


class Step:

    def __init__(self, sem, value):
        self.sem, self.value = sem, value


class Lane:

    def __init__(self, engine, sem):
        self.engine, self.sem = engine, sem
        self.base, self.count = 0, 0

    def after(self, *steps):
        for step in steps:
            if step is not None:
                self.engine.wait_ge(step.sem, step.value)

    def now(self):
        return Step(self.sem, self.base + self.count)

    def did(self, instruction):
        instruction.then_inc(self.sem, 1)
        self.count += 1
        return self.now()


class Serial(Lane):

    def next(self, *steps):
        if not (isinstance(self.base, int) and self.base + self.count == 0):
            self.after(self.now())
        self.after(*steps)
        return self.engine


def build(nc, io):
    ctx = ExitStack()
    with ctx:
        def sem(name):
            return ctx.enter_context(nc.semaphore(name))

        pe = Lane(nc.tensor, sem("pe_steps"))
        act = Serial(nc.scalar, sem("act_steps"))
        dve = Serial(nc.vector, sem("dve_steps"))
        raw_landed = [sem(f"raw_landed{i}") for i in range(RAW)]
        hi_ready, lo_ready, unit_used = sem("hi_ready"), sem("lo_ready"), sem("unit_used")
        loaded, stored = sem("small_loaded"), sem("out_stored")

        top = (nc.sbuf_base + 63) // 64 * 64

        def at(name, shape, offset, dtype=F32):
            return nc.alloc_sbuf_tensor_at(name, shape, dtype, offset=offset)

        def rows(shape):
            n = 4
            for x in shape[1:]:
                n *= x
            return (n + 31) // 32 * 32

        def put(name, shape, dtype=F32):
            nonlocal top
            t = at(name, shape, top, dtype)
            top += rows(shape)
            return t

        raw = [put(f"raw{i}", [P, UNIT]) for i in range(RAW)]
        whi = [put(f"whi{i}", [P, UNIT], F32R) for i in range(SPLIT)]
        wlo = [put(f"wlo{i}", [P, UNIT], F32R) for i in range(SPLIT)]
        xT = put("xT", [P, DK, S])
        hT = put("hT", [P, DK, S])
        hhi = put("hhi", [P, DK, S], F32R)
        hlo = put("hlo", [P, DK, S], F32R)
        v1 = put("v1", [P, DEPTH, V1N])
        v2 = put("v2", [P, DEPTH, V2N])
        vx = put("vx", [P, 8 + 64 + 8 + 64])
        selT = put("selT", [16, DK, P])
        ident = put("ident", [P, P])
        ones = put("ones", [P, P])
        zero = put("zero", [P, 512])
        epsc = put("epsc", [P, 1])
        rs = put("rs", [16, S])
        small = put("small", [P, 512])
        arena = top

        class Region:

            def __init__(self, start):
                self.top = start

            def put(self, name, shape, dtype=F32):
                t = at(name, shape, self.top, dtype)
                self.top += rows(shape)
                return t

        PS = ctx.enter_context(nc.psum_tensor("PS", [P, 8, 512], F32))
        emptied = [None] * 8

        def banks(b, n):
            return PS[:, b:b + n, :].rearrange("p b c -> p (b c)")

        def claim(b, n=1):
            for step in {id(s): s for s in emptied[b:b + n] if s is not None}.values():
                pe.after(step)

        def empty(b, n, step):
            for i in range(b, b + n):
                emptied[i] = step
            return step

        stream = dict(base=0, n=0)

        def prepare(u, k):
            r, s = k % RAW, k % SPLIT
            first = isinstance(u, int) and u < RAW
            if not first:
                nc.sync.wait_ge(lo_ready, u - RAW + 1)
            nc.sync.dma_start(raw[r][:], io["ws"][bass.ds(u, 1), :, :].rearrange("a p n -> p (a n)")) \
                .then_inc(raw_landed[r], 16)
            fill = stream["rounds"] + k // RAW + 1
            nc.scalar.wait_ge(raw_landed[r], 16 * fill)
            if not first:
                nc.scalar.wait_ge(unit_used, u - SPLIT + 1)
            nc.scalar.activation(whi[s][:], raw[r][:], ACT.Copy).then_inc(hi_ready, 1)
            nc.vector.wait_ge(hi_ready, u + 1)
            nc.vector.tensor_tensor(wlo[s][:], raw[r][:], whi[s][:].bitcast(F32), ALU.subtract) \
                .then_inc(lo_ready, 1)

        def take():
            n = stream["n"]
            prepare(stream["base"] + n + LEAD, stream["k0"] + n + LEAD)
            nc.tensor.wait_ge(lo_ready, stream["base"] + n + 1)
            stream["n"] = n + 1
            s = (stream["k0"] + n) % SPLIT
            return whi[s], wlo[s]

        stream["k0"] = stream["rounds"] = 0
        for u in range(LEAD):
            prepare(u, u)

        def release(mm):
            mm.then_inc(unit_used, 1)
            return Step(unit_used, stream["base"] + stream["n"])

        class Loop:

            def __init__(self, n, steps, units):
                self.n, self.steps, self.units = n, steps, units

            def __enter__(self):
                assert self.units % RAW == 0 and self.units % SPLIT == 0
                self.old = [(x.base, x.count) for x in (pe, act, dve)]
                self.su = dict(stream)
                self.fori = nc.Fori(0, self.n)
                i = self.fori.__enter__()
                for x, k in zip((pe, act, dve), self.steps):
                    x.base, x.count = i * k + (x.base + x.count), 0
                base = self.su["base"] + self.su["n"]
                stream["base"], stream["n"] = i * self.units + base, 0
                stream["k0"] = (self.su["k0"] + self.su["n"]) % RAW
                stream["rounds"] = i * (self.units // RAW) + \
                    (self.su["rounds"] + (self.su["k0"] + self.su["n"]) // RAW)
                return i

            def __exit__(self, *a):
                got = tuple(x.count for x in (pe, act, dve))
                if a[0] is None:
                    assert got == tuple(self.steps), ("steps of a pass", got)
                    assert stream["n"] == self.units, ("units of a pass", stream["n"])
                self.fori.__exit__(*a)
                for x, (b, c), k in zip((pe, act, dve), self.old, self.steps):
                    x.base, x.count = b, c + self.n * k
                u = self.n * self.units
                stream.update(self.su)
                stream["n"] = self.su["n"] + u

        n_loaded = 0

        def fetch(dst, src):
            nonlocal n_loaded
            nc.gpsimd.dma_start(dst, src).then_inc(loaded, 16)
            n_loaded += 1

        def fetched():
            return Step(loaded, 16 * n_loaded)

        fetch(xT[:], io["xT"])
        fetch(v1[:], io["v1"])
        fetch(v2[:], io["v2"])
        fetch(vx[:], io["vx"])
        fetch(selT[:], io["selT"])
        fetch(ident[:], io["ident"])
        dve.did(dve.next().memset(ones[:], 1.0))
        dve.did(dve.next().memset(zero[:], 0.0))
        dve.did(dve.next().memset(epsc[:], EPS))
        act.after(dve.now())
        pe.after(dve.now())
        start_load = fetched()
        for lane in (pe, act, dve):
            lane.after(start_load)

        def mm3(out, a_hi, a_lo, b_hi, b_lo, start, stop):
            nc.tensor.matmul(out, a_hi, b_hi, start=start, stop=False, skip_group_check=True)
            nc.tensor.matmul(out, a_hi, b_lo, start=False, stop=False, skip_group_check=True)
            return nc.tensor.matmul(out, a_lo, b_hi, start=False, stop=stop, skip_group_check=True)

        def split(hi, lo, src, *after):
            act.did(act.next(*after).activation(hi, src, ACT.Copy))
            return dve.did(dve.next(act.now(), *after).tensor_tensor(lo, src, hi.bitcast(F32), ALU.subtract))

        def unit_T(bank, hi, lo, nk=DK, cols=UC, width=P, *after):
            w_hi, w_lo = take()
            claim(bank)
            pe.after(*after)
            wh = w_hi[:, 0:nk * cols].rearrange("p (k c) -> p k c", k=nk)
            wl = w_lo[:, 0:nk * cols].rearrange("p (k c) -> p k c", k=nk)
            for f in range(2):
                for k in range(nk):
                    mm = mm3(PS[0:width, bank, f * S:(f + 1) * S], wh[:, k, f * width:(f + 1) * width],
                             wl[:, k, f * width:(f + 1) * width], hi[:, k, :], lo[:, k, :],
                             k == 0, k == nk - 1)
            return release(mm)

        def unit_tok(bank, hi, lo, *after):
            w_hi, w_lo = take()
            claim(bank)
            pe.after(*after)
            wh = w_hi[:].rearrange("p (k c) -> p k c", k=DK)
            wl = w_lo[:].rearrange("p (k c) -> p k c", k=DK)
            for t in range(NT):
                for k in range(DK):
                    ts = slice(t * P, (t + 1) * P)
                    mm = mm3(PS[:, bank, t * UC:(t + 1) * UC], hi[:, k, ts], lo[:, k, ts],
                             wh[:, k, :], wl[:, k, :], k == 0, k == DK - 1)
            return release(mm)

        sq_at = None

        def group_rstd(src, nt, whole, width, sq, *after):
            act.did(act.next(*after).activation(sq, src, ACT.Square))
            claim(7)
            pe.after(act.now())
            g = 1 if whole else 2
            if whole:
                for t in range(nt):
                    mm = nc.tensor.matmul(PS[0:1, 7, 0:S], ones[:, 0:1], sq[:, t, :],
                                          start=t == 0, stop=t == nt - 1)
                n = 1
            else:
                for t in range(nt):
                    mm = nc.tensor.matmul(PS[0:16, 7, 0:S], selT_cols(t), sq[:, t, :],
                                          start=t == 0, stop=t == nt - 1)
                n = 16
            pe.did(mm)
            act.did(act.next(pe.now(), dve.now()).activation(rs[0:n, :], PS[0:n, 7, 0:S], ACT.Sqrt,
                                                  bias=epsc[0:n, :], scale=1.0 / width))
            empty(7, 1, act.now())
            return dve.did(dve.next(act.now()).reciprocal(rs[0:n, :], rs[0:n, :]))

        selw = put("selw", [P, DK, 16])
        fetch(selw[:], io["selw"])
        pe.after(fetched())
        arena = top

        def selT_cols(t):
            return selw[:, t, :]

        def spread(t, whole, bank, half):
            n = 1 if whole else 16
            lhs = ones[0:1, :] if whole else selT[:, t, :]
            return nc.tensor.matmul(PS[:, bank, half * S:(half + 1) * S], lhs, rs[0:n, :],
                                    start=True, stop=True)

        def apply_rstd(dst, src, nt, whole, gain, banks4, *after):
            step = dve.now()
            for t0 in range(0, nt, 2):
                b = banks4[(t0 // 2) % len(banks4)]
                claim(b)
                pe.after(step, *after)
                for t in range(t0, min(t0 + 2, nt)):
                    mm = spread(t, whole, b, t - t0)
                pe.did(mm)
                for t in range(t0, min(t0 + 2, nt)):
                    dve.did(dve.next(pe.now(), *after).scalar_tensor_tensor(
                        out=dst[:, t, :], in0=src[:, t, :], scalar=gain(t),
                        in1=PS[:, b, (t - t0) * S:(t - t0 + 1) * S], op0=ALU.mult, op1=ALU.mult))
                empty(b, 1, dve.now())
            return dve.now()

        def norm_to_h(gain):
            group_rstd(xT[:], DK, True, D, hT[:], dve.now(), pe_idle())
            apply_rstd(hT, xT, DK, True, gain, [4, 5, 6, 7])
            pe.after(split(hhi[:], hlo[:], hT[:], dve.now()))

        def pe_idle():
            return Step(unit_used, stream["base"] + stream["n"]) if not (
                isinstance(stream["base"], int) and stream["base"] + stream["n"] == 0) else None

        def add_to_x(tile0, bank, step):
            out = xT[:, tile0:tile0 + 2, :].rearrange("p t s -> p (t s)")
            dve.did(dve.next(step).tensor_tensor(out, out, PS[:, bank, :], ALU.add))
            return empty(bank, 1, dve.now())

        def project_to_x(hi, lo, ready):
            for j in range(DK // 2):
                step = unit_T(4 + j % 4, hi, lo, DK, UC, P, ready)
                add_to_x(2 * j, 4 + j % 4, step)

        def softmax(ps, pb, kw, scale, ready, stat):
            m, z = small[:, stat:stat + NH], small[:, stat + 8:stat + 8 + NH]
            dve.did(dve.next(ready).tensor_reduce(m, ps, AX, ALU.max))
            dve.did(dve.next().tensor_tensor(pb, ps, m.unsqueeze(2).to_broadcast([P, NH, kw]), ALU.subtract))
            sub = dve.now()
            act.did(act.next(sub).activation(pb, pb, ACT.Exp, scale=scale))
            dve.did(dve.next(act.now()).tensor_reduce(z, pb, AX, ALU.add))
            dve.did(dve.next().reciprocal(z, z))
            dve.did(dve.next().tensor_tensor(pb, pb, z.unsqueeze(2).to_broadcast([P, NH, kw]), ALU.mult))
            return sub

        def weigh_values(pb, pt, t, nkb, value, y, tile0, order):
            claim(4, 4)
            pe.after(dve.now(), act.now())
            ptp = banks(4, 4).rearrange("p (h b q) -> p h b q", h=NH, b=NT)
            for h in range(NH):
                for b in range(nkb):
                    mm = nc.tensor.transpose(ptp[:, h, b, :], pb[:, h, b * P:(b + 1) * P], ident[:])
            pe.did(mm)
            act.did(act.next(pe.now()).activation(pt[:, :, 0:nkb, :], ptp[:, :, 0:nkb, :], ACT.Copy))
            empty(4, 4, act.now())
            claim(0)
            pe.after(act.now())
            for i, h in enumerate(order):
                lo = HD * (h % 2)
                for b in range(nkb):
                    mm = nc.tensor.matmul(PS[lo:lo + HD, 0, (h // 2) * P:(h // 2 + 1) * P],
                                          value(h, b), pt[:, i, b, :], start=b == 0, stop=b == nkb - 1,
                                          skip_group_check=True)
            pe.did(mm)
            act.did(act.next(pe.now()).activation(
                y[:, tile0:tile0 + 4, t * P:(t + 1) * P],
                PS[:, 0, :].rearrange("p (t q) -> p t q", t=4), ACT.Copy))
            return empty(0, 1, act.now())

        c1 = Region(arena)
        tri = c1.put("tri", [P, NT, S])
        cmask = c1.put("cmask", [P, NT, S])
        bsum = c1.put("bsum", [P, NT, LEVELS * P])
        lmask = c1.put("lmask", [P, LEVELS, P])
        onehot = c1.put("onehot", [NH, NH, P])
        lbw = c1.put("lbw", [P, DEPTH, S])
        lbl = c1.put("lbl", [P, DEPTH, S])
        gb = c1.put("gb", [P, NE, S])
        yT = c1.put("yT", [P, DK, S])
        rgs = c1.put("rgs", [P, 2, S])
        work1 = c1.top
        ra = Region(work1)
        pb1 = ra.put("pb1", [P, NH, S])
        pt1 = ra.put("pt1", [P, NH, NT, P])
        qT = ra.put("qT", [P, 4, S])
        kT = ra.put("kT", [P, 4, S])
        vtok = ra.put("vtok", [P, NT, 512])
        nd = ra.put("nd", [NH, S])
        lsf = ra.put("lsf", [P, NT, NH])
        dq = ra.put("dq", [P, NT, NH])
        ft = ra.put("ft", [P, 3, NT * NH])
        rc = Region(work1)
        cx = rc.put("cx", [P, 2, S])
        cu = rc.put("cu", [P, 2, S + 2])
        cy = rc.put("cy", [P, 2, S])
        rh = Region(work1)
        E = rh.put("E", [P, 2, LEVELS, P])
        qe = rh.put("qe", [P, 2, LEVELS, P])
        ke = rh.put("ke", [P, 2, 2, LEVELS, P])
        rq = rh.put("rq", [P, 2, S])
        rk = rh.put("rk", [P, 2, S])
        rkt = rh.put("rkt", [P, NT, S])
        lf = rh.put("lf", [P, NT, S])
        lf2 = rh.put("lf2", [P, NT, S])
        ri = rh.put("ri", [P, NT, S])
        aT = rh.put("aT", [P, NT, 512])
        aX = hT[:, 2:4, :].rearrange("p t s -> p (t s)")
        am = hT[:, 0:2, :].rearrange("p t s -> p (t s)")
        ry = Region(work1)
        yhi = ry.put("yhi", [P, DK, S], F32R)
        ylo = ry.put("ylo", [P, DK, S], F32R)
        rf = Region(work1)
        sil = [rf.put(f"sil{i}", [P, 512]) for i in range(2)]
        ahi = [rf.put(f"ahi{i}", [P, 2, S], F32R) for i in range(2)]
        alo = [rf.put(f"alo{i}", [P, 2, S], F32R) for i in range(2)]
        fin = ra.top, rh.top, ry.top
        assert max(fin) <= nc.sbuf_usable_end, (fin, nc.sbuf_usable_end)
        for name in ("tri", "cmask", "bsum", "lmask", "onehot"):
            fetch(dict(tri=tri, cmask=cmask, bsum=bsum, lmask=lmask, onehot=onehot)[name][:], io[name])
        fetch(lbw[:], io["lbw"])
        for lane in (pe, act, dve):
            lane.after(fetched())

        def lower_bounds():
            a, b = lbw[:, 0, :], lbw[:, 1, :]
            m, t = hT[:, 0, :], hT[:, 1, :]
            v = lambda out, x, y, op: dve.did(dve.next().tensor_tensor(out, x, y, op))
            v(m, a, b, ALU.max)
            v(a, a, m, ALU.subtract)
            v(b, b, m, ALU.subtract)
            act.did(act.next(dve.now()).activation(lbw[:], lbw[:], ACT.Exp))
            dve.after(act.now())
            v(t, a, b, ALU.add)
            dve.did(dve.next().reciprocal(t, t))
            v(a, a, t, ALU.mult)
            v(b, b, t, ALU.mult)
            v(lbl[:, 0, :], a, a, ALU.subtract)
            v(t, a, b, ALU.add)
            v(lbl[:, 1, :], t, a, ALU.subtract)
            dve.did(dve.next().tensor_scalar(lbw[:], lbl[:], -1.0, 1.0, ALU.mult, ALU.add))

        lower_bounds()

        def vec1(l, name):
            a, b = V1[name]
            return v1[:, l, a:b]

        def head_norm(buf, nt, gain, sq):
            head_norm_ap(buf[:, 0:nt, :], nt, gain, sq)

        def head_norm_ap(buf, nt, gain, sq):
            group_rstd(buf, nt, False, HD, sq, dve.now())
            apply_rstd(buf, buf, nt, False, gain, [4, 5, 6, 7])

        def evacuate(dst, bank, step):
            act.did(act.next(step, dve.now()).activation(dst, PS[:, bank, :], ACT.Copy))
            return empty(bank, 1, act.now())

        def pair(t, i):
            return t[:, 2 * i:2 * i + 2, :].rearrange("p t s -> p (t s)")

        def forget_decay(l):
            wf = vec1(l, "wf").rearrange("p (k h) -> p k h", k=DK)
            claim(6)
            pe.after(dve.now())
            for t in range(NT):
                for k in range(DK):
                    mm = nc.tensor.matmul(PS[:, 6, t * NH:(t + 1) * NH], hT[:, k, t * P:(t + 1) * P],
                                          wf[:, k, :], start=k == 0, stop=k == DK - 1)
            pe.did(mm)
            z, a, e = (ft[:, i, :].rearrange("p (t h) -> p t h", t=NT) for i in range(3))
            fb = vec1(l, "fbias").unsqueeze(1).to_broadcast([P, NT, NH])
            dve.did(dve.next(pe.now(), act.now()).tensor_tensor(
                z, PS[:, 6, 0:NT * NH].rearrange("p (t h) -> p t h", t=NT), fb, ALU.add))
            empty(6, 1, dve.now())
            act.did(act.next(dve.now()).activation(a, z, ACT.Abs))
            act.did(act.next().activation(e, a, ACT.Exp, scale=-1.0))
            act.did(act.next().activation(a, e, ACT.Ln, bias=1.0))
            dve.did(dve.next(act.now()).scalar_tensor_tensor(
                out=lsf[:], in0=z, scalar=0.0, in1=a, op0=ALU.min, op1=ALU.subtract))
            claim(6)
            claim(7)
            pe.after(dve.now())
            for t in range(NT):
                for b in range(t + 1):
                    nc.tensor.matmul(PS[:, 6, t * NH:(t + 1) * NH], tri[:, b, t * P:(t + 1) * P],
                                     lsf[:, b, :], start=b == 0, stop=b == t)
            for b in range(NT):
                mm = nc.tensor.matmul(PS[0:NH, 7, 0:S], lsf[:, b, :], tri[:, b, :],
                                      start=b == 0, stop=b == NT - 1)
            pe.did(mm)
            act.did(act.next(pe.now()).activation(dq[:], PS[:, 6, 0:NT * NH].rearrange(
                "p (t h) -> p t h", t=NT), ACT.Copy))
            act.did(act.next().activation(nd[:], PS[0:NH, 7, 0:S], ACT.Copy, scale=-1.0))
            empty(6, 2, act.now())

        def forgetting_attention(l):
            for dst in (qT, kT):
                for i in range(2):
                    evacuate(pair(dst, i), 4 + i, unit_T(4 + i, hhi, hlo))
            for i in range(2):
                b = 4 + i
                step = unit_tok(b, hhi, hlo)
                act.did(act.next(step).activation(
                    vtok[:, :, i * UC:(i + 1) * UC], PS[:, b, :].rearrange("p (t c) -> p t c", t=NT), ACT.Copy))
                empty(b, 1, act.now())
            qs = small[:, 500:501]
            dve.did(dve.next().tensor_scalar(qs, vec1(l, "qg"), HD ** -0.5, None, ALU.mult))
            dve.after(act.now())
            head_norm(qT, 4, lambda t: qs, pb1[:, 0:4, :])
            head_norm(kT, 4, lambda t: vec1(l, "kg"), pb1[:, 0:4, :])
            forget_decay(l)
            for t in range(NT):
                kw = (t + 1) * P
                sp = banks(0, 4).rearrange("p (h k) -> p h k", h=NH)[:, :, 0:kw]
                claim(0, 4)
                pe.after(dve.now(), act.now())
                for i, h in enumerate(HEAD_AT):
                    lo = HD * (h % 2)
                    nc.tensor.matmul(sp[:, i, :], qT[lo:lo + HD, h // 2, t * P:(t + 1) * P],
                                     kT[lo:lo + HD, h // 2, 0:kw], start=True, stop=False)
                    mm = nc.tensor.matmul(sp[:, i, :], onehot[:, h, :], nd[:, 0:kw],
                                          start=False, stop=True)
                pe.did(mm)
                dve.after(pe.now(), act.now())
                for i, h in enumerate(HEAD_AT):
                    dve.did(dve.next().scalar_tensor_tensor(
                        out=pb1[:, i, 0:kw], in0=sp[:, i, :], scalar=dq[:, t, h:h + 1],
                        in1=cmask[:, t, 0:kw], op0=ALU.add, op1=ALU.add))
                empty(0, 4, dve.now())
                softmax(pb1[:, :, 0:kw], pb1[:, :, 0:kw], kw, 1.0, dve.now(), 0)
                weigh_values(pb1, pt1, t, t + 1, lambda h, b: vtok[:, b, h * HD:(h + 1) * HD], yT, 0, HEAD_AT)

        def short_conv(l):
            w = vec1(l, "conv").rearrange("p (t j) -> p t j", t=2)
            evacuate(cx[:].rearrange("p t s -> p (t s)"), 4, unit_T(4, hhi, hlo))
            gate_step = unit_T(5, hhi, hlo)
            c_step = unit_T(6, hhi, hlo)
            dve.did(dve.next(act.now()).memset(cu[:, :, 0:2], 0.0))
            dve.did(dve.next(c_step, act.now()).tensor_tensor(
                cu[:, :, 2:2 + S], PS[:, 6, :].rearrange("p (t s) -> p t s", t=2), cx[:], ALU.mult))
            empty(6, 1, dve.now())
            for t in range(2):
                dve.did(dve.next().tensor_scalar(cy[:, t, :], cu[:, t, 0:S], w[:, t, 0:1], None, ALU.mult))
                for j in (1, 2):
                    dve.did(dve.next().scalar_tensor_tensor(
                        out=cy[:, t, :], in0=cu[:, t, j:j + S], scalar=w[:, t, j:j + 1],
                        in1=cy[:, t, :], op0=ALU.mult, op1=ALU.add))
            dve.did(dve.next(gate_step, act.now()).tensor_tensor(
                pair(yT, 2), PS[:, 5, :], cy[:].rearrange("p t s -> p (t s)"), ALU.mult))
            empty(5, 1, dve.now())

        def hgrn(l):
            q_step = unit_T(4, hhi, hlo)
            f_step = unit_tok(5, hhi, hlo)
            i_step = unit_tok(6, hhi, hlo)
            g_step = unit_T(7, hhi, hlo)
            flat = lambda t: t[:].rearrange("p t s -> p (t s)")
            act.after(dve.now())
            act.did(act.next(q_step).activation(flat(rq), PS[:, 4, :], ACT.Silu))
            act.did(act.next(g_step).activation(flat(rgs), PS[:, 7, :], ACT.Silu))
            act.did(act.next(i_step).activation(flat(ri), PS[:, 6, :], ACT.Copy))
            act.did(act.next(f_step).activation(flat(lf), PS[:, 5, :], ACT.Sigmoid))
            act.did(act.next().activation(flat(rkt), PS[:, 5, :], ACT.Sigmoid, scale=-1.0))
            empty(4, 4, act.now())
            lb = lbl[:, l, :].unsqueeze(1).to_broadcast([P, NT, S])
            om = lbw[:, l, :].unsqueeze(1).to_broadcast([P, NT, S])
            dve.did(dve.next(act.now()).tensor_tensor(lf[:], lf[:], om, ALU.mult))
            dve.did(dve.next().tensor_tensor(lf[:], lf[:], lb, ALU.add))
            dve.did(dve.next().tensor_tensor(rkt[:], rkt[:], om, ALU.mult))
            dve.did(dve.next().tensor_scalar(lf2[:], lf[:], TINY, 1.0 / LN_CUT, ALU.max, ALU.mult))
            dve.did(dve.next().tensor_scalar(lf2[:], lf2[:], 1.0, None, ALU.min))
            dve.did(dve.next().tensor_scalar(lf[:], lf[:], LN_CUT, None, ALU.max))
            act.did(act.next(dve.now()).activation(lf[:], lf[:], ACT.Ln))
            act.did(act.next().activation(lf2[:], lf2[:], ACT.Ln))
            dve.did(dve.next(act.now()).tensor_tensor(lf[:], lf[:], lf2[:], ALU.add))
            claim(6)
            pe.after(dve.now())
            kp = PS[:, 6, :].rearrange("p (g s) -> p g s", g=2)
            for g in range(2):
                for t in range(NT):
                    mm = nc.tensor.transpose(kp[:, g, t * P:(t + 1) * P], rkt[:, t, g * P:(g + 1) * P], ident[:])
            pe.did(mm)
            act.did(act.next(pe.now()).activation(flat(rk), PS[:, 6, :], ACT.Copy))
            empty(6, 1, act.now())
            for t in range(NT):
                claim(0, 4)
                pe.after(dve.now())
                for g in range(2):
                    for c in range(2):
                        mm = nc.tensor.matmul(PS[:, 2 * g + c, :], lf[:, t, g * P:(g + 1) * P],
                                              bsum[:, t, c * 512:(c + 1) * 512], start=True, stop=True)
                pe.did(mm)
                act.did(act.next(pe.now(), dve.now()).activation(
                    E[:].rearrange("p g l s -> p (g l s)"), banks(0, 4), ACT.Exp))
                empty(0, 4, act.now())
                for g in range(2):
                    over = lambda x: x[:, g, t * P:(t + 1) * P].unsqueeze(1).to_broadcast([P, LEVELS, P])
                    dve.did(dve.next(act.now(), pe.now()).tensor_tensor(qe[:, g, :, :], E[:, g, :, :], over(rq), ALU.mult))
                    dve.did(dve.next().tensor_tensor(ke[:, t, g, :, :], E[:, g, :, :], over(rk), ALU.mult))
                ready = dve.now()
                for v in range(LEVELS):
                    b = v % 2 * 2
                    claim(b, 2)
                    pe.after(ready)
                    for h in range(4):
                        lo, g = HD * (h % 2), h // 2
                        ks = ke[lo:lo + HD, t, g, v, :] if v < LEVELS - 1 else rk[lo:lo + HD, g, t * P:(t + 1) * P]
                        qs = qe[lo:lo + HD, g, v, :] if v < LEVELS - 1 else rq[lo:lo + HD, g, t * P:(t + 1) * P]
                        mm = nc.tensor.matmul(PS[:, b + h % 2, g * P:(g + 1) * P], ks, qs, start=True, stop=True)
                    pe.did(mm)
                    mask = lmask[:, v, :].unsqueeze(1).unsqueeze(1).to_broadcast([P, 2, 2, P])
                    dst = aT[:, t, :] if v == 0 else am
                    dve.did(dve.next(pe.now()).tensor_tensor(
                        dst.rearrange("p (b g s) -> p b g s", b=2, g=2),
                        PS[:, b:b + 2, 0:2 * P].rearrange("p b (g s) -> p b g s", g=2), mask, ALU.mult))
                    empty(b, 2, dve.now())
                    if v:
                        dve.did(dve.next().tensor_tensor(aT[:, t, :], aT[:, t, :], am[:], ALU.add))
                if t:
                    claim(4, 2)
                    for h in range(4):
                        lo, g = HD * (h % 2), h // 2
                        mm = nc.tensor.matmul(PS[:, 4 + h % 2, g * P:(g + 1) * P], ke[lo:lo + HD, 0, g, LEVELS - 1, :],
                                              qe[lo:lo + HD, g, LEVELS - 1, :], start=True, stop=True)
                    pe.did(mm)
                    act.did(act.next(pe.now()).activation(aX.rearrange("p (b s) -> p b s", b=2),
                                                          PS[:, 4:6, 0:2 * P], ACT.Copy))
                    empty(4, 2, act.now())
            claim(5)
            pe.after(dve.now(), act.now())
            for h in range(4):
                lo = HD * (h % 2)
                for t in range(NT):
                    out = PS[lo:lo + HD, 5, (h // 2) * S + t * P:(h // 2) * S + (t + 1) * P]
                    hs = slice((h % 2 * 2 + h // 2) * P, (h % 2 * 2 + h // 2 + 1) * P)
                    vs = slice(h * HD, (h + 1) * HD)
                    if t:
                        nc.tensor.matmul(out, ri[:, 0, vs], aX[:, hs], start=True, stop=False,
                                         skip_group_check=True)
                    mm = nc.tensor.matmul(out, ri[:, t, vs], aT[:, t, hs], start=t == 0, stop=True,
                                          skip_group_check=True)
            pe.did(mm)
            evacuate(pair(yT, 3), 5, pe.now())

        def mixer_out(l):
            group_rstd(yT[:], DK, False, HD, hT[:], dve.now())
            g = vec1(l, "mix_gain")
            apply_rstd(yT, yT, DK, False, lambda t: g[:, t:t + 1], [4, 5, 6, 7])
            dve.did(dve.next().tensor_tensor(pair(yT, 3), pair(yT, 3), rgs[:].rearrange("p t s -> p (t s)"), ALU.mult))
            ready = split(yhi[:], ylo[:], yT[:], dve.now(), pe.now())
            project_to_x(yhi, ylo, ready)

        def open_sums():
            claim(0, 4)
            for b in range(4):
                mm = nc.tensor.matmul(PS[:, b, :], zero[:, 0:P], zero[:], start=True, stop=False,
                                      skip_group_check=True)
            pe.did(mm)

        def down(a_hi, a_lo, ready):
            w_hi, w_lo = take()
            pe.after(ready)
            for f in range(2):
                for d in range(DK):
                    cs = slice(f * D + d * P, f * D + (d + 1) * P)
                    mm = mm3(PS[:, d // 2, (d % 2) * S:(d % 2 + 1) * S], w_hi[:, cs], w_lo[:, cs],
                             a_hi[:, f, :], a_lo[:, f, :], False, False)
            return release(mm)

        def close_sums(step):
            for b in range(4):
                add_to_x(2 * b, b, step)

        used_a = [None, None, None]

        def swiglu_up(i, gate_of=None):
            bg, bu = 4 + 2 * i, 5 + 2 * i
            g_step = unit_T(bg, hhi, hlo)
            u_step = unit_T(bu, hhi, hlo)
            act.did(act.next(g_step, dve.now()).activation(sil[i][:], PS[:, bg, :], ACT.Silu))
            empty(bg, 1, act.now())
            dve.did(dve.next(u_step, act.now()).tensor_tensor(sil[i][:], sil[i][:], PS[:, bu, :], ALU.mult))
            empty(bu, 1, dve.now())
            if gate_of is not None:
                s2 = sil[i][:].rearrange("p (t s) -> p t s", t=2)
                g = gb[:, bass.ds(gate_of, 1), :].to_broadcast([P, 2, S])
                dve.did(dve.next().tensor_tensor(s2, s2, g, ALU.mult))
            src = sil[i][:].rearrange("p (t s) -> p t s", t=2)
            return split(ahi[i][:], alo[i][:], src, dve.now(), used_a[i])

        def swiglu(groups, steps, gate=lambda g: None):
            open_sums()
            ready = swiglu_up(0, gate(0))
            emptied[4:8] = [emptied[4], emptied[5], None, None]
            n = (groups - 2) // 2
            with Loop(n, steps, 6) as i:
                settled = [pe_idle(), act.now(), dve.now()]
                for b in range(4, 8):
                    emptied[b] = None
                emptied[4] = settled[1]
                emptied[6], emptied[7] = settled[1], settled[2]
                emptied[5] = settled[2]
                used_a[0] = used_a[1] = None
                r1 = swiglu_up(1, gate(i * 2 + 1))
                used_a[0] = down(ahi[0], alo[0], settled[2])
                r0 = swiglu_up(0, gate(i * 2 + 2))
                used_a[1] = down(ahi[1], alo[1], r1)
            done = pe_idle()
            used_a[0] = used_a[1] = done
            for b in range(4, 8):
                emptied[b] = dve.now()
            r1 = swiglu_up(1, gate(groups - 1))
            down(ahi[0], alo[0], dve_settled(r1))
            close_sums(down(ahi[1], alo[1], r1))

        def dve_settled(step):
            return step

        def router():
            wr = vx[:, 8:72].rearrange("p (k e) -> p k e", k=DK)
            claim(4)
            pe.after(dve.now())
            for t in range(NT):
                for k in range(DK):
                    mm = nc.tensor.matmul(PS[:, 4, t * NE:(t + 1) * NE], hT[:, k, t * P:(t + 1) * P],
                                          wr[:, k, :], start=k == 0, stop=k == DK - 1)
            pe.did(mm)
            lg = small[:, 0:16].rearrange("p (t e) -> p t e", t=NT)
            m = small[:, 16:18]
            ex = small[:, 32:48].rearrange("p (t e) -> p t e", t=NT)
            rank = small[:, 48:64].rearrange("p (t e) -> p t e", t=NT)
            gt = small[:, 64:192].rearrange("p (t e j) -> p t e j", t=NT, e=NE)
            eq = small[:, 192:320].rearrange("p (t e j) -> p t e j", t=NT, e=NE)
            before = vx[:, 80:144].rearrange("p (e j) -> p e j", e=NE)
            vv = lambda *a: dve.did(dve.next().tensor_tensor(*a))
            rb = vx[:, 72:80].unsqueeze(1).to_broadcast([P, NT, NE])
            dve.after(pe.now())
            vv(lg, PS[:, 4, 0:16].rearrange("p (t e) -> p t e", t=NT), rb, ALU.add)
            empty(4, 1, dve.now())
            for t in range(NT):
                mine = lg[:, t, :].unsqueeze(2).to_broadcast([P, NE, NE])
                other = lg[:, t, :].unsqueeze(1).to_broadcast([P, NE, NE])
                vv(gt[:, t], other, mine, ALU.is_gt)
                vv(eq[:, t], other, mine, ALU.is_equal)
                vv(eq[:, t], eq[:, t], before, ALU.mult)
                vv(gt[:, t], gt[:, t], eq[:, t], ALU.add)
            dve.did(dve.next().tensor_reduce(rank, gt, AX, ALU.add))
            dve.did(dve.next().tensor_scalar(rank, rank, 1.5, None, ALU.is_lt))
            dve.did(dve.next().tensor_reduce(m, lg, AX, ALU.max))
            vv(ex, lg, m.unsqueeze(2).to_broadcast([P, NT, NE]), ALU.subtract)
            act.did(act.next(dve.now()).activation(ex, ex, ACT.Exp))
            dve.after(act.now())
            vv(ex, ex, rank, ALU.mult)
            dve.did(dve.next().tensor_reduce(m, ex, AX, ALU.add))
            dve.did(dve.next().reciprocal(m, m))
            vv(ex, ex, m.unsqueeze(2).to_broadcast([P, NT, NE]), ALU.mult)
            claim(5)
            pe.after(dve.now())
            for t in range(NT):
                mm = nc.tensor.transpose(PS[0:NE, 5, t * P:(t + 1) * P], ex[:, t, :], ident[:])
            pe.did(mm)
            act.did(act.next(pe.now()).activation(rs[0:NE, :], PS[0:NE, 5, 0:S], ACT.Copy))
            empty(5, 1, act.now())
            claim(0, 4)
            pe.after(act.now())
            for e in range(NE):
                mm = nc.tensor.matmul(banks(0, 4)[:, e * S:(e + 1) * S], onehot[:, e, :], rs[0:NE, :],
                                      start=True, stop=True)
            pe.did(mm)
            act.did(act.next(pe.now()).activation(gb[:].rearrange("p e s -> p (e s)"), banks(0, 4), ACT.Copy))
            empty(0, 4, act.now())
            dve.after(act.now())

        def vec1_of(l, name):
            g = vec1(l, name)
            return lambda t: g[:, t:t + 1]

        for l in range(1 if io.get("stop") == 1 else DEPTH):
            norm_to_h(vec1_of(l, "norm_mix"))
            pe.after(dve.now())
            forgetting_attention(l)
            pe.after(act.now(), dve.now())
            act.after(pe.now())
            dve.after(pe.now(), act.now())
            short_conv(l)
            act.after(dve.now())
            hgrn(l)
            dve.after(act.now())
            mixer_out(l)
            act.after(dve.now())
            norm_to_h(vec1_of(l, "norm_ffn"))
            pe.after(dve.now())
            if l % 2 == 0:
                swiglu(G1, (0, 4, 4))
            else:
                router()
                swiglu(GM, (0, 4, 6), lambda g: g % NE)

        if io.get("stop") in (1, 2):
            nc.sync.wait_ge(dve.sem, dve.base + dve.count)
            nc.sync.dma_start(io["out"], xT[:]).then_inc(stored, 16)
            nc.sync.wait_ge(stored, 16)
            return

        def settle():
            steps = [x.now() for x in (pe, act, dve)] + [pe_idle()]
            for lane in (pe, act, dve):
                lane.after(*steps)
            for b in range(8):
                emptied[b] = None

        settle()
        nc.gpsimd.wait_ge(act.sem, act.base + act.count)
        nc.gpsimd.wait_ge(dve.sem, dve.base + dve.count)
        c2 = Region(arena)
        rope_in = {n: c2.put(n, io[n].shape) for n in ("cosA", "sinA", "rotA", "cosB", "sinB", "rotB",
                                                        "cosC", "sinC", "rotC")}
        vl = c2.put("vl", [P, V2N])
        nlam = c2.put("nlam", [P, 4])
        y2 = c2.put("y2", [P, 12, S])
        soft = c2.top
        rp = Region(soft)
        pb2 = [rp.put(f"pb2{i}", [P, NH, S]) for i in range(2)]
        pt2 = rp.put("pt2", [P, NH, NT, P])
        r = Region(soft)
        chi = r.put("chi", [P, 5, S], F32R)
        clo = r.put("clo", [P, 5, S], F32R)
        r = Region(soft)
        y2hi = r.put("y2hi", [P, 12, S], F32R)
        y2lo = r.put("y2lo", [P, 12, S], F32R)
        qk = rp.top
        r = Region(qk)
        qa = r.put("qa", [P, 4, S])
        kva = r.put("kva", [P, 2, S])
        va = r.put("va", [P, NT, P])
        r = Region(qk)
        qb = r.put("qb", [P, 4, S])
        kb = r.put("kb", [P, 4, S])
        vb = r.put("vb", [P, NT, 512])
        r = Region(qk)
        cc = r.put("cc", [P, 6, S])
        qc = r.put("qc", [P, NH, S])
        kc = r.put("kc", [P, NH, S])
        vc = r.put("vc", [P, NT, 512])
        end2 = r.top
        r = Region(qk)
        mg = r.put("mg", [P, DK, S])
        mhi = r.put("mhi", [P, DK, S], F32R)
        mlo = r.put("mlo", [P, DK, S], F32R)
        gs = [r.put(f"gs{i}", [P, 512]) for i in range(2)]
        end2 = max(end2, r.top)
        r = Region(soft)
        rl = [r.put(f"rl{i}", [P, 512]) for i in range(3)]
        bhi = [r.put(f"bhi{i}", [P, 2, S], F32R) for i in range(3)]
        blo = [r.put(f"blo{i}", [P, 2, S], F32R) for i in range(3)]
        assert max(end2, r.top) <= nc.sbuf_usable_end, (end2, r.top)
        loaded2 = sem("second_loaded")
        for n, t in rope_in.items():
            nc.gpsimd.dma_start(t[:], io[n]).then_inc(loaded2, 16)
        for lane in (pe, dve):
            lane.after(Step(loaded2, 16 * len(rope_in)))

        def vec2(name):
            return vl[:, V2[name][0]:V2[name][1]]

        def column(name, n=1):
            return lambda t: vec2(name)[:, (t if n > 1 else 0):(t if n > 1 else 0) + 1]

        def rope(buf, nt, n, which, tmp):
            rot, cos, sin = (rope_in[x + which] for x in ("rot", "cos", "sin"))
            k = (nt + 1) // 2
            claim(4, k)
            pe.after(dve.now(), act.now())
            out = banks(4, k).rearrange("p (t s) -> p t s", s=S)
            for t in range(nt):
                mm = nc.tensor.matmul(out[0:n, t, :], rot[0:n, 0:n], buf[:, t, :], start=True, stop=True)
            pe.did(mm)
            wide = lambda x: x[0:n, :].unsqueeze(1).to_broadcast([n, nt, S])
            dve.did(dve.next(pe.now()).tensor_tensor(tmp, out[0:n, 0:nt, :], wide(sin), ALU.mult))
            empty(4, k, dve.now())
            dve.did(dve.next().tensor_tensor(buf, buf, wide(cos), ALU.mult))
            dve.did(dve.next().tensor_tensor(buf, buf, tmp, ALU.add))

        def scores(parts, pb, scale):
            sp = banks(0, 4).rearrange("p (h k) -> p h k", h=NH)
            claim(0, 4)
            pe.after(dve.now(), act.now())
            for i in range(NH):
                q, k = parts(i)
                mm = nc.tensor.matmul(sp[:, i, :], q, k, start=True, stop=True)
            pe.did(mm)
            dve.after(act.now())
            empty(0, 4, softmax(sp, pb[:], S, scale, pe.now(), 0))

        def branch_a():
            for i in range(2):
                evacuate(pair(qa, i), 4 + i, unit_T(4 + i, hhi, hlo))
            evacuate(pair(kva, 0), 6, unit_T(6, hhi, hlo))
            head_norm(qa, 4, column("aq"), hT[:, 0:4, :])
            kv1 = kva[:, 0:1, :]
            head_norm_ap(kv1, 1, column("ak"), hT[:, 0:1, :])
            rope(qa[:], 4, P, "A", hT[:, 0:4, :])
            rope(kv1, 1, P, "A", hT[:, 0:1, :])
            claim(4)
            pe.after(act.now(), dve.now())
            for t in range(NT):
                mm = nc.tensor.transpose(PS[:, 4, t * P:(t + 1) * P], kva[:, 1, t * P:(t + 1) * P], ident[:])
            pe.did(mm)
            act.did(act.next(pe.now()).activation(va[:].rearrange("p t c -> p (t c)"), PS[:, 4, 0:S], ACT.Copy))
            empty(4, 1, act.now())
            for t in range(NT):
                def parts(h):
                    lo = HD * (h // 4)
                    return qa[lo:lo + HD, h % 4, t * P:(t + 1) * P], kva[lo:lo + HD, 0, :]
                scores(parts, pb2[0], HD ** -0.5)
                weigh_values(pb2[0], pt2, t, NT, lambda h, b: va[:, b, h // 4 * HD:(h // 4 + 1) * HD],
                             y2, 0, range(NH))

        def branch_b():
            for dst in (qb, kb):
                for i in range(2):
                    evacuate(pair(dst, i), 4 + i, unit_T(4 + i, hhi, hlo))
            for i in range(2):
                step = unit_tok(6 + i, hhi, hlo)
                act.did(act.next(step).activation(
                    vb[:, :, i * UC:(i + 1) * UC], PS[:, 6 + i, :].rearrange("p (t c) -> p t c", t=NT), ACT.Copy))
                empty(6 + i, 1, act.now())
            dve.after(act.now())
            rope(qb[:], 4, P, "B", hT[:, 0:4, :])
            rope(kb[:], 4, P, "B", hT[:, 0:4, :])
            lam = vec2("lam").rearrange("p (a b d) -> p a b d", a=2, b=2)
            pr = small[:, 64:128].rearrange("p (a d) -> p a d", a=2)
            dve.did(dve.next().tensor_tensor(pr, lam[:, :, 0, :], lam[:, :, 1, :], ALU.mult))
            dve.did(dve.next().tensor_reduce(nlam[:, 0:2], pr, AX, ALU.add))
            act.did(act.next(dve.now()).activation(nlam[:, 0:2], nlam[:, 0:2], ACT.Exp))
            dve.did(dve.next(act.now()).tensor_tensor(nlam[:, 2:3], nlam[:, 1:2], nlam[:, 0:1], ALU.subtract))
            dve.did(dve.next().tensor_tensor(nlam[:, 2:3], nlam[:, 2:3], vec2("lam_init"), ALU.subtract))
            for t in range(NT):
                for c in range(2):
                    def parts(i):
                        h = HEAD_AT[i]
                        lo = HD * (h % 2) + 32 * c
                        return qb[lo:lo + 32, h // 2, t * P:(t + 1) * P], kb[lo:lo + 32, h // 2, :]
                    scores(parts, pb2[c], 32 ** -0.5)
                dve.did(dve.next().scalar_tensor_tensor(
                    out=pb2[0][:], in0=pb2[1][:], scalar=nlam[:, 2:3], in1=pb2[0][:],
                    op0=ALU.mult, op1=ALU.add))
                weigh_values(pb2[0], pt2, t, NT, lambda h, b: vb[:, b, h * HD:(h + 1) * HD],
                             y2, 4, HEAD_AT)
            g = nlam[:, 3:4]
            dve.did(dve.next(act.now()).tensor_scalar(g, vec2("lam_init"), -1.0, 1.0, ALU.mult, ALU.add))
            dve.did(dve.next().tensor_tensor(g, g, vec2("bsub"), ALU.mult))
            head_norm_ap(y2[:, 4:8, :], 4, lambda t: g, hT[:, 0:4, :])

        NOPE, ROT = 64, 32
        QW = NOPE + ROT

        def branch_c():
            for i in range(3):
                evacuate(pair(cc, i), 4 + i, unit_T(4 + i, hhi, hlo))
            dve.after(act.now())
            for a, n, gain in ((0, 3, "cq"), (3, 2, "ckv")):
                src = cc[:, a:a + n, :]
                group_rstd(src, n, True, n * P, hT[:, 0:n, :], dve.now())
                apply_rstd(src, src, n, True, column(gain, n), [4, 5])
            ready = split(chi[:], clo[:], cc[:, 0:5, :], dve.now())
            rope(cc[0:QW, 5:6, :], 1, QW, "C", hT[0:QW, 0:1, :])
            act.did(act.next(dve.now()).activation(
                kc[NOPE:QW, :, :], cc[NOPE:QW, 5:6, :].to_broadcast([ROT, NH, S]), ACT.Copy))
            for i in range(2):
                w_hi, w_lo = take()
                claim(4 + 2 * i, 2)
                pe.after(ready)
                wh, wl = (w[:, 0:3 * 4 * QW].rearrange("p (k c) -> p k c", k=3) for w in (w_hi, w_lo))
                out = banks(4 + 2 * i, 2).rearrange("p (h s) -> p h s", s=S)
                for h in range(4):
                    cs = slice(h * QW, (h + 1) * QW)
                    for k in range(3):
                        mm = mm3(out[0:QW, h, :], wh[:, k, cs], wl[:, k, cs], chi[:, k, :], clo[:, k, :],
                                 k == 0, k == 2)
                step = release(mm)
                act.did(act.next(step).activation(qc[0:QW, 4 * i:4 * i + 4, :], out[0:QW, :, :], ACT.Copy))
                empty(4 + 2 * i, 2, act.now())
            w_hi, w_lo = take()
            wh, wl = (w[:].rearrange("p (k c) -> p k c", k=2) for w in (w_hi, w_lo))
            claim(0, 8)
            out = banks(4, 4).rearrange("p (h s) -> p h s", s=S)
            for h in range(NH):
                for k in range(2):
                    mm3(out[:, h, :], wh[:, k, h * P:(h + 1) * P], wl[:, k, h * P:(h + 1) * P],
                        chi[:, 3 + k, :], clo[:, 3 + k, :], k == 0, k == 1)
            for t in range(NT):
                ts = slice(t * P, (t + 1) * P)
                for k in range(2):
                    vh, vl_ = (w[:, k, :].rearrange("p (h c) -> p h c", h=NH)[:, :, NOPE:] for w in (wh, wl))
                    mm = mm3(PS[:, t, :], chi[:, 3 + k, ts], clo[:, 3 + k, ts], vh, vl_, k == 0, k == 1)
            step = release(mm)
            act.did(act.next(step).activation(kc[0:NOPE, :, :], out[0:NOPE, :, :], ACT.Copy))
            act.did(act.next().activation(vc[:].rearrange("p t c -> p (t c)"), banks(0, 2), ACT.Copy))
            empty(0, 8, act.now())
            dve.after(act.now())
            rope(qc[0:QW, :, :], NH, QW, "C", hT[0:QW, :, :])
            for t in range(NT):
                scores(lambda h: (qc[0:QW, h, t * P:(t + 1) * P], kc[0:QW, h, :]), pb2[0], QW ** -0.5)
                weigh_values(pb2[0], pt2, t, NT, lambda h, b: vc[:, b, h * HD:(h + 1) * HD],
                             y2, 8, range(NH))

        def merge():
            ready = split(y2hi[:], y2lo[:], y2[:], act.now(), pe.now())
            for jj in range(2):
                for n in range(3):
                    for i in range(2):
                        step = unit_T(4 + i, hhi, hlo)
                        act.did(act.next(step, dve.now()).activation(gs[i][:], PS[:, 4 + i, :], ACT.Sigmoid))
                        empty(4 + i, 1, act.now())
                    w_hi, w_lo = take()
                    claim(6, 2)
                    pe.after(ready)
                    wh, wl = (w[:].rearrange("p (k c) -> p k c", k=4) for w in (w_hi, w_lo))
                    for f in range(4):
                        for k in range(4):
                            mm = mm3(PS[:, 6 + f // 2, f % 2 * S:(f % 2 + 1) * S],
                                     wh[:, k, f * P:(f + 1) * P], wl[:, k, f * P:(f + 1) * P],
                                     y2hi[:, 4 * n + k, :], y2lo[:, 4 * n + k, :], k == 0, k == 3)
                    step = release(mm)
                    for i in range(2):
                        dst = pair(mg, 2 * jj + i)
                        dve.did(dve.next(step, act.now()).tensor_tensor(
                            dst if n == 0 else gs[i][:], gs[i][:], PS[:, 6 + i, :], ALU.mult))
                        empty(6 + i, 1, dve.now())
                        if n:
                            dve.did(dve.next().tensor_tensor(dst, dst, gs[i][:], ALU.add))
            project_to_x(mhi, mlo, split(mhi[:], mlo[:], mg[:], dve.now(), pe.now()))

        used_b = [None] * 3

        def relu_up(i):
            step = unit_T(4 + i, hhi, hlo)
            act.did(act.next(step, dve.now()).activation(rl[i][:], PS[:, 4 + i, :], ACT.Relu))
            empty(4 + i, 1, act.now())
            dve.did(dve.next(act.now()).tensor_tensor(rl[i][:], rl[i][:], rl[i][:], ALU.mult))
            return split(bhi[i][:], blo[i][:], rl[i][:].rearrange("p (t s) -> p t s", t=2), dve.now(), used_b[i])

        def relu_ffn(steps):
            open_sums()
            ready = relu_up(0)
            with Loop((G2 - 1) // 3, steps, 6):
                before_act, before_dve = act.now(), dve.now()
                for b in range(4, 7):
                    emptied[b] = before_act
                for j in range(3):
                    used_b[j] = None
                r = before_dve
                for j in range(3):
                    r2 = relu_up((j + 1) % 3)
                    used_b[j] = down(bhi[j], blo[j], r)
                    r = r2
            close_sums(down(bhi[0], blo[0], dve.now()))

        def layer2(l):
            settle()
            src = v2[:, bass.ds(l, 1), :].rearrange("p a c -> p (a c)")
            dve.did(dve.next().tensor_copy(vl[:], src))
            norm_to_h(column("ln1", 8))
            branch_a()
            settle()
            branch_b()
            settle()
            branch_c()
            settle()
            merge()
            settle()
            norm_to_h(column("ln2", 8))
            settle()
            relu_ffn((0, 6, 6))

        if io.get("stop") == 3:
            layer2(0)
            final = xT
        else:
            with Loop(DEPTH, LAYER_STEPS, U_BLK2) as l:
                layer2(l)
            settle()
            group_rstd(xT[:], DK, True, D, hT[:], dve.now())
            apply_rstd(hT, xT, DK, True, lambda t: vx[:, t:t + 1], [4, 5, 6, 7])
            final = hT
        nc.sync.wait_ge(dve.sem, dve.base + dve.count)
        nc.sync.dma_start(io["out"], final[:]).then_inc(stored, 16)
        nc.sync.wait_ge(stored, 16)


def constants():
    f = np.float32
    s, t = np.arange(P)[:, None], np.arange(S)[None, :]
    c = {}
    c["tri"] = np.stack([(s + b * P <= t) for b in range(NT)], 1).astype(f)
    c["cmask"] = np.stack([np.where(t <= s + b * P, 0.0, NEG) for b in range(NT)], 1).astype(f)
    tt = np.arange(P)[None, :]
    bsum = np.zeros((P, NT, LEVELS, P), f)
    lmask = np.zeros((P, LEVELS, P), f)
    for v in range(LEVELS - 1):
        n = 1 << v
        mid = tt // (2 * n) * (2 * n) + n - 1
        m = np.where(tt > mid, (s > mid) & (s <= tt), (s > tt) & (s <= mid))
        bsum[:, :, v, :] = m[:, None, :]
        lmask[:, v, :] = (s // (2 * n) == tt // (2 * n)) & (s // n % 2 == 0) & (tt // n % 2 == 1)
    bsum[:, 0, LEVELS - 1, :] = s > tt
    bsum[:, 1, LEVELS - 1, :] = s <= tt
    lmask[:, LEVELS - 1, :] = s == tt
    c["bsum"], c["lmask"] = bsum.reshape(P, NT, -1), lmask
    def angles(pos, dim, theta):
        inv = (f(theta) ** (-np.arange(0, dim, 2, dtype=f) / f(dim))).astype(f)
        return (pos.astype(f)[:, None] * inv[None, :]).astype(f).T

    def rotary(n, spans):
        cos, sin, rot = np.ones((n, S), f), np.zeros((n, S), f), np.zeros((n, n), f)
        for a, ang in spans:
            h = len(ang)
            for i in (0, h):
                cos[a + i:a + i + h], sin[a + i:a + i + h] = np.cos(ang), np.sin(ang)
            for i in range(h):
                rot[a + h + i, a + i], rot[a + i, a + h + i] = -1, 1
        return cos, sin, rot

    pos = np.arange(S)
    row, col = angles(pos // 64, 32, 10000.0), angles(pos % 64, 32, 10000.0)
    spans = dict(A=(P, [(a + o, g) for a in (0, 64) for o, g in ((0, row), (32, col))]),
                 B=(P, [(a, angles(pos, 8, 500000.0)) for a in range(0, P, 32)]),
                 C=(96, [(64, angles(pos, 32, 10000.0))]))
    for which, (n, sp) in spans.items():
        c["cos" + which], c["sin" + which], c["rot" + which] = rotary(n, sp)
    c["onehot"] = np.repeat(np.eye(NH, dtype=f)[:, :, None], P, 2)
    c["ident"] = np.eye(P, dtype=f)
    half = np.arange(P) // HD
    selw = np.zeros((P, DK, 16), f)
    for k in range(DK):
        selw[np.arange(P), k, 2 * k + half] = 1
    c["selw"] = selw
    c["selT"] = np.ascontiguousarray(selw.transpose(2, 1, 0))
    return c


def by_part(v):
    return np.moveaxis(v.reshape(*v.shape[:-1], -1, P), -1, 0)


def k_units(w, cols=UC):
    K, N = w.shape
    return w.reshape(K // P, P, N // cols, cols).transpose(2, 1, 0, 3).reshape(N // cols, P, -1)


def down_units(w):
    return w.reshape(-1, 2, P, w.shape[1]).transpose(0, 2, 1, 3).reshape(-1, P, 2 * w.shape[1])


def pipelined(up, dn):
    out = [up[0]]
    for g in range(len(up) - 1):
        out += [up[g + 1], dn[g:g + 1]]
    return out + [dn[-1:]]


def pack(inp):
    f = np.float32
    units = []
    w_in, w_out = inp["w_in"], inp["w_out"]
    for l in range(DEPTH):
        w = w_in[l]
        units.append(k_units(w[:, 0:1536]))
        units.append(k_units(w[:, 1544:1544 + 1792]))
        units.append(k_units(w_out[l]))
        if l == 0:
            a = np.stack([k_units(inp["ffn_w_gate"][0]), k_units(inp["ffn_w_up"][0])], 1)
            units += pipelined(a, down_units(inp["ffn_w_down"][0]))
        else:
            g = np.stack([k_units(inp["moe_w_gate"][0][e]) for e in range(NE)], 1).reshape(GM, P, UNIT)
            u = np.stack([k_units(inp["moe_w_up"][0][e]) for e in range(NE)], 1).reshape(GM, P, UNIT)
            d = np.stack([down_units(inp["moe_w_down"][0][e]) for e in range(NE)], 1).reshape(GM, P, UNIT)
            units += pipelined(np.stack([g, u], 1), d)
            del g, u, d
    for l in range(DEPTH):
        w = inp["w_in_2"][l]
        perm = [h * HD + d for t in range(4) for h in (t, t + 4) for d in range(HD)]
        units.append(k_units(w[:, 0:512][:, perm]))
        units.append(k_units(w[:, 512:768]))
        units.append(k_units(w[:, 768:2304]))
        lat = np.zeros((D, 768), f)
        lat[:, 0:640] = w[:, 2304:2944]
        lat[:, 640 + 64:640 + 96] = w[:, 2944:2976]
        units.append(k_units(lat))
        uq = k_units(inp["c_w_uq_2"][l], 384)
        units.append(np.concatenate([uq, np.zeros((2, P, UNIT - uq.shape[2]), f)], 2))
        units.append(k_units(inp["c_w_ukv_2"][l], 1024))
        gates = w[:, 2976:].reshape(D, 3, D)
        for jj in range(2):
            for n in range(3):
                units.append(k_units(gates[:, n, jj * 512:(jj + 1) * 512]))
                units.append(k_units(inp["w_branch_2"][l][n][:, jj * 512:(jj + 1) * 512], 512))
        units.append(k_units(inp["w_out_2"][l]))
        units += pipelined(k_units(inp["w_ff1_2"][l])[:, None], down_units(inp["w_ff2_2"][l]))
    units.append(np.zeros((LEAD, P, UNIT), f))
    arrays = {"ws": np.concatenate(units, 0)}
    arrays["xT"] = by_part(np.ascontiguousarray(inp["x"][0])).transpose(0, 2, 1)
    rep = lambda v: np.broadcast_to(v, (P,) + v.shape)
    two = lambda v: np.concatenate([v, v])[:, None]
    v1 = []
    for l in range(DEPTH):
        wf = w_in[l][:, 1536:1544].reshape(DK, P, NH).transpose(1, 0, 2).reshape(P, -1)
        conv = inp["conv_w"][l].reshape(3, 2, P).transpose(2, 1, 0).reshape(P, 6)
        v1.append(np.concatenate([by_part(inp["norm_mix"][l]), by_part(inp["norm_ffn"][l]),
                                  by_part(inp["mix_out_gain"][l]), two(inp["q_norm_gain"][l]),
                                  two(inp["k_norm_gain"][l]), conv, rep(inp["attn_f_bias"][l]), wf], 1))
    arrays["v1"] = np.stack(v1, 1)
    v2 = []
    for l in range(DEPTH):
        v2.append(np.concatenate([by_part(inp["ln1_g_2"][l]), by_part(inp["ln2_g_2"][l]),
                                  two(inp["a_q_norm_2"][l]), two(inp["a_k_norm_2"][l]),
                                  two(inp["b_subln_2"][l]), by_part(inp["c_q_norm_2"][l]),
                                  by_part(inp["c_kv_norm_2"][l]), rep(inp["b_lambda_2"][l].reshape(-1)),
                                  np.full((P, 1), LAMBDA_INIT[l], f)], 1))
    arrays["v2"] = np.stack(v2, 1)
    wr = inp["moe_router_w"][0].reshape(DK, P, NE).transpose(1, 0, 2).reshape(P, -1)
    arrays["vx"] = np.concatenate([by_part(inp["final_g_2"]), wr, rep(inp["moe_router_b"][0]),
                                   rep(np.tril(np.ones((NE, NE), np.float32), -1).reshape(-1))], 1)
    arrays["lbw"] = rep(inp["hgrn_lb_logits"])
    arrays.update(constants())
    return {k: np.ascontiguousarray(v) for k, v in arrays.items()}


def kernel(_stop=0, **inputs):
    import concourse.bacc as bacc
    from concourse.bass_utils import run_bass_kernel_spmd as run

    arrays = pack({k: np.asarray(v) for k, v in inputs.items()})
    nc = bacc.Bacc("TRN2", target_bir_lowering=False, num_devices=1)
    io = {k: nc.dram_tensor(f"in_{k}", a.shape, F32, kind="ExternalInput").ap() for k, a in arrays.items()}
    io["out"] = nc.dram_tensor("out_T", (P, DK, S), F32, kind="ExternalOutput").ap()
    if _stop:
        io["stop"] = _stop
    build(nc, io)
    r = run(nc, [{f"in_{k}": a for k, a in arrays.items()}], core_ids=[0])
    out = r.results[0]["out_T"]
    return np.ascontiguousarray(out.transpose(2, 1, 0)).reshape(1, S, D)
```

```python
from contextlib import ExitStack

import numpy as np

import concourse.bass as bass
from concourse import mybir

F32 = mybir.dt.float32
F32R = mybir.dt.float32r
ACT = mybir.ActivationFunctionType
ALU = mybir.AluOpType
AX = mybir.AxisListType.X

P = 128
S = 256
NT = S // P
D = 1024
DK = D // P
DEPTH = 2
HD = 64
NH = 8
HEAD_AT = [0, 2, 4, 6, 1, 3, 5, 7]
UNIT = 2048
UC = UNIT // DK
RAW, SPLIT = 3, 3
LEAD = 2
EPS = 1e-6
TINY = 1e-30
LN_CUT = 2.0 ** -60
NEG = -1e30

D_FF = 3584
G1 = D_FF // UC
NE = 8
D_FF2 = 4096
G2 = D_FF2 // UC
LEVELS = 8

U_BLK1 = 2 + 2 + 2 + 3 + 4 + 4
U_FFN = 3 * G1
U_BLK2 = 2 + 1 + 6 + 3 + 2 + 1 + 12 + 6 + 4 + 2 * G2

EXPERT_STEPS = (11, 17, 21)
LAYER_STEPS = (51, 102, 169)

V1 = dict(norm_mix=(0, 8), norm_ffn=(8, 16), mix_gain=(16, 24), qg=(24, 25), kg=(25, 26),
          conv=(26, 32), fbias=(32, 40), wf=(40, 104))
V1N = 104
V2 = dict(ln1=(0, 8), ln2=(8, 16), aq=(16, 17), ak=(17, 18), bsub=(18, 19), cq=(19, 22),
          ckv=(22, 24), lam=(24, 152), lam_init=(152, 153))
V2N = 153
LAMBDA_INIT = [0.8 - 0.6 * float(np.exp(-0.3 * l)) for l in range(DEPTH)]


class Step:

    def __init__(self, sem, value):
        self.sem, self.value = sem, value


class Lane:

    def __init__(self, engine, sem):
        self.engine, self.sem = engine, sem
        self.base, self.count = 0, 0

    def after(self, *steps):
        for step in steps:
            if step is not None:
                self.engine.wait_ge(step.sem, step.value)

    def now(self):
        return Step(self.sem, self.base + self.count)

    def did(self, instruction):
        instruction.then_inc(self.sem, 1)
        self.count += 1
        return self.now()


class Serial(Lane):

    def next(self, *steps):
        if not (isinstance(self.base, int) and self.base + self.count == 0):
            self.after(self.now())
        self.after(*steps)
        return self.engine


def build(nc, io):
    ctx = ExitStack()
    with ctx:
        def sem(name):
            return ctx.enter_context(nc.semaphore(name))

        pe = Lane(nc.tensor, sem("pe_steps"))
        act = Serial(nc.scalar, sem("act_steps"))
        dve = Serial(nc.vector, sem("dve_steps"))
        raw_landed = [sem(f"raw_landed{i}") for i in range(RAW)]
        hi_ready, lo_ready, unit_used = sem("hi_ready"), sem("lo_ready"), sem("unit_used")
        loaded, stored = sem("small_loaded"), sem("out_stored")

        top = (nc.sbuf_base + 63) // 64 * 64

        def at(name, shape, offset, dtype=F32):
            return nc.alloc_sbuf_tensor_at(name, shape, dtype, offset=offset)

        def rows(shape):
            n = 4
            for x in shape[1:]:
                n *= x
            return (n + 31) // 32 * 32

        def put(name, shape, dtype=F32):
            nonlocal top
            t = at(name, shape, top, dtype)
            top += rows(shape)
            return t

        raw = [put(f"raw{i}", [P, UNIT]) for i in range(RAW)]
        whi = [put(f"whi{i}", [P, UNIT], F32R) for i in range(SPLIT)]
        wlo = [put(f"wlo{i}", [P, UNIT], F32R) for i in range(SPLIT)]
        xT = put("xT", [P, DK, S])
        slow_raw = at("slow_raw", [P, UNIT], top)
        hT = put("hT", [P, DK, S])
        at_hhi, at_hlo = top, top + rows([P, DK, S])
        hhi = put("hhi", [P, DK, S], F32R)
        hlo = put("hlo", [P, DK, S], F32R)
        v1 = put("v1", [P, DEPTH, V1N])
        v2 = put("v2", [P, DEPTH, V2N])
        vx = put("vx", [P, 8 + 64 + 8 + 64])
        selT = put("selT", [16, DK, P])
        ident = put("ident", [P, P])
        ones = put("ones", [P, P])
        zero = put("zero", [P, 512])
        epsc = put("epsc", [P, 1])
        rs = put("rs", [16, S])
        small = put("small", [P, 512])
        selw = put("selw", [P, DK, 16])
        at_overflow = put("overflow", [1, 1], mybir.dt.int32)
        at_pms = put("pms", [P, S], F32R)
        iota = put("iota", [P, P])
        arena = top

        class Region:

            def __init__(self, start):
                self.top = start

            def put(self, name, shape, dtype=F32):
                t = at(name, shape, self.top, dtype)
                self.top += rows(shape)
                return t

        PS = ctx.enter_context(nc.psum_tensor("PS", [P, 8, 512], F32))
        emptied = [None] * 8

        def banks(b, n):
            return PS[:, b:b + n, :].rearrange("p b c -> p (b c)")

        def claim(b, n=1):
            for step in {id(s): s for s in emptied[b:b + n] if s is not None}.values():
                pe.after(step)

        def empty(b, n, step):
            for i in range(b, b + n):
                emptied[i] = step
            return step

        class Stream:

            def __init__(self, raw, lead, raw_landed, used, first_unit=0, used0=0):
                self.raw, self.lead, self.raw_landed, self.used = raw, lead, raw_landed, used
                self.first_unit, self.used0 = first_unit, used0
                self.base = self.n = self.k0 = self.rounds = 0

            def load(self, u, k):
                r = k % len(self.raw)
                nc.sync.dma_start(self.raw[r][:], io["ws"][bass.ds(u + self.first_unit, 1), :, :].rearrange(
                    "a p n -> p (a n)")).then_inc(self.raw_landed[r], 16)
                return self.raw_landed[r], 16 * (self.rounds + k // len(self.raw) + 1)

            def at(self):
                return self.base + self.n

            def taken(self):
                return Step(self.used, self.at() + self.used0)

        class Split(Stream):

            def prepare(self, u, k):
                s = k % SPLIT
                first = isinstance(u, int) and u < RAW
                if not first:
                    nc.sync.wait_ge(lo_ready, u - RAW + 1)
                landed, count = self.load(u, k)
                nc.scalar.wait_ge(landed, count)
                if not first:
                    nc.scalar.wait_ge(unit_used, u - SPLIT + 1)
                nc.scalar.activation(whi[s][:], self.raw[k % RAW][:], ACT.Copy).then_inc(hi_ready, 1)
                nc.vector.wait_ge(hi_ready, u + 1)
                nc.vector.tensor_tensor(wlo[s][:], self.raw[k % RAW][:], whi[s][:].bitcast(F32),
                                        ALU.subtract).then_inc(lo_ready, 1)

            def take(self):
                self.prepare(self.at() + LEAD, self.k0 + self.n + LEAD)
                nc.tensor.wait_ge(lo_ready, self.at() + 1)
                self.n += 1
                s = (self.k0 + self.n - 1) % SPLIT
                return whi[s], wlo[s]

        class Whole(Stream):

            def take(self):
                nc.sync.wait_ge(self.used, self.at() + self.used0)
                landed, count = self.load(self.at(), self.k0 + self.n)
                nc.tensor.wait_ge(landed, count)
                self.n += 1
                return self.raw[0], None

        stream = main = Split(raw, LEAD, raw_landed, unit_used)

        def take():
            return stream.take()

        def release(mm):
            mm.then_inc(stream.used, 1)
            return stream.taken()

        class Loop:

            def __init__(self, n, steps, units):
                self.n, self.steps, self.units = n, steps, units

            def __enter__(self):
                ring = len(stream.raw)
                assert self.units % RAW == 0 and self.units % SPLIT == 0
                self.old = [(x.base, x.count) for x in (pe, act, dve)]
                self.at = stream.base, stream.n, stream.k0, stream.rounds
                self.fori = nc.Fori(0, self.n)
                i = self.fori.__enter__()
                for x, k in zip((pe, act, dve), self.steps):
                    x.base, x.count = i * k + (x.base + x.count), 0
                rounds, k = divmod(stream.k0 + stream.n, ring)
                stream.rounds = i * (self.units // ring) + (stream.rounds + rounds)
                stream.base, stream.n, stream.k0 = i * self.units + stream.at(), 0, k
                return i

            def __exit__(self, *a):
                got = tuple(x.count for x in (pe, act, dve)) + (stream.n,)
                if a[0] is None:
                    assert got == tuple(self.steps) + (self.units,), ("steps and units of a pass", got)
                self.fori.__exit__(*a)
                for x, (b, c), k in zip((pe, act, dve), self.old, self.steps):
                    x.base, x.count = b, c + self.n * k
                stream.base, stream.n, stream.k0, stream.rounds = self.at
                stream.n += self.n * self.units

        n_loaded = 0

        def fetch(dst, src):
            nonlocal n_loaded
            nc.sync.dma_start(dst, src).then_inc(loaded, 16)
            n_loaded += 1

        def fetched():
            return Step(loaded, 16 * n_loaded)

        fetch(xT[:], io["xT"])
        fetch(v1[:], io["v1"])
        fetch(v2[:], io["v2"])
        fetch(vx[:], io["vx"])
        fetch(selT[:], io["selT"])
        fetch(ident[:], io["ident"])
        fetch(selw[:], io["selw"])
        fetch(iota[:], io["iota"])
        dve.did(dve.next().memset(ones[:], 1.0))
        dve.did(dve.next().memset(zero[:], 0.0))
        dve.did(dve.next().memset(epsc[:], EPS))
        act.after(dve.now())
        pe.after(dve.now())
        start_load = fetched()
        for u in range(LEAD):
            main.prepare(u, u)
        for lane in (pe, act, dve):
            lane.after(start_load)

        def mm3(out, a_hi, a_lo, b_hi, b_lo, start, stop):
            if b_lo is None:
                nc.tensor.matmul(out, a_hi.bitcast(F32), b_hi, start=start, stop=False, skip_group_check=True)
                return nc.tensor.matmul(out, a_lo.bitcast(F32), b_hi, start=False, stop=stop,
                                        skip_group_check=True)
            nc.tensor.matmul(out, a_hi, b_hi, start=start, stop=False, skip_group_check=True)
            nc.tensor.matmul(out, a_hi, b_lo, start=False, stop=False, skip_group_check=True)
            return nc.tensor.matmul(out, a_lo, b_hi, start=False, stop=stop, skip_group_check=True)

        def split(hi, lo, src, *after):
            act.did(act.next(*after).activation(hi, src, ACT.Copy))
            return dve.did(dve.next(act.now(), *after).tensor_tensor(lo, src, hi.bitcast(F32), ALU.subtract))

        def unit_T(bank, hi, lo, nk=DK, cols=UC, width=P, *after):
            w_hi, w_lo = take()
            claim(bank)
            pe.after(*after)
            wh = w_hi[:, 0:nk * cols].rearrange("p (k c) -> p k c", k=nk)
            wl = w_lo[:, 0:nk * cols].rearrange("p (k c) -> p k c", k=nk)
            for f in range(2):
                for k in range(nk):
                    mm = mm3(PS[0:width, bank, f * S:(f + 1) * S], wh[:, k, f * width:(f + 1) * width],
                             wl[:, k, f * width:(f + 1) * width], hi[:, k, :], lo[:, k, :],
                             k == 0, k == nk - 1)
            return release(mm)

        def unit_tok(bank, hi, lo, *after):
            w_hi, w_lo = take()
            claim(bank)
            pe.after(*after)
            wh = w_hi[:].rearrange("p (k c) -> p k c", k=DK)
            wl = w_lo[:].rearrange("p (k c) -> p k c", k=DK)
            for t in range(NT):
                for k in range(DK):
                    ts = slice(t * P, (t + 1) * P)
                    mm = mm3(PS[:, bank, t * UC:(t + 1) * UC], hi[:, k, ts], lo[:, k, ts],
                             wh[:, k, :], wl[:, k, :], k == 0, k == DK - 1)
            return release(mm)

        sq_at = None

        def group_rstd(src, nt, whole, width, sq, *after):
            act.did(act.next(*after).activation(sq, src, ACT.Square))
            claim(7)
            pe.after(act.now())
            g = 1 if whole else 2
            if whole:
                for t in range(nt):
                    mm = nc.tensor.matmul(PS[0:1, 7, 0:S], ones[:, 0:1], sq[:, t, :],
                                          start=t == 0, stop=t == nt - 1)
                n = 1
            else:
                for t in range(nt):
                    mm = nc.tensor.matmul(PS[0:16, 7, 0:S], selT_cols(t), sq[:, t, :],
                                          start=t == 0, stop=t == nt - 1)
                n = 16
            pe.did(mm)
            act.did(act.next(pe.now(), dve.now()).activation(rs[0:n, :], PS[0:n, 7, 0:S], ACT.Sqrt,
                                                  bias=epsc[0:n, :], scale=1.0 / width))
            empty(7, 1, act.now())
            return dve.did(dve.next(act.now()).reciprocal(rs[0:n, :], rs[0:n, :]))


        def selT_cols(t):
            return selw[:, t, :]

        def spread(t, whole, bank, half):
            n = 1 if whole else 16
            lhs = ones[0:1, :] if whole else selT[:, t, :]
            return nc.tensor.matmul(PS[:, bank, half * S:(half + 1) * S], lhs, rs[0:n, :],
                                    start=True, stop=True)

        def apply_rstd(dst, src, nt, whole, gain, banks4, *after):
            step = dve.now()
            for t0 in range(0, nt, 2):
                b = banks4[(t0 // 2) % len(banks4)]
                claim(b)
                pe.after(step, *after)
                for t in range(t0, min(t0 + 2, nt)):
                    mm = spread(t, whole, b, t - t0)
                pe.did(mm)
                for t in range(t0, min(t0 + 2, nt)):
                    dve.did(dve.next(pe.now(), *after).scalar_tensor_tensor(
                        out=dst[:, t, :], in0=src[:, t, :], scalar=gain(t),
                        in1=PS[:, b, (t - t0) * S:(t - t0 + 1) * S], op0=ALU.mult, op1=ALU.mult))
                empty(b, 1, dve.now())
            return dve.now()

        def norm_to_h(gain):
            group_rstd(xT[:], DK, True, D, hT[:], dve.now(), pe_idle())
            apply_rstd(hT, xT, DK, True, gain, [4, 5, 6, 7])
            pe.after(split(hhi[:], hlo[:], hT[:], dve.now()))

        def pe_idle():
            return None if isinstance(stream.at(), int) and stream.at() == 0 else stream.taken()

        def settle():
            steps = [x.now() for x in (pe, act, dve)] + [pe_idle()]
            for lane in (pe, act, dve):
                lane.after(*steps)
            for b in range(8):
                emptied[b] = None

        def add_to_x(tile0, bank, step):
            out = xT[:, tile0:tile0 + 2, :].rearrange("p t s -> p (t s)")
            dve.did(dve.next(step).tensor_tensor(out, out, PS[:, bank, :], ALU.add))
            return empty(bank, 1, dve.now())

        def project_to_x(hi, lo, ready):
            for j in range(DK // 2):
                step = unit_T(4 + j % 4, hi, lo, DK, UC, P, ready)
                add_to_x(2 * j, 4 + j % 4, step)

        def softmax(ps, pb, kw, scale, ready, stat):
            m, z = small[:, stat:stat + NH], small[:, stat + 8:stat + 8 + NH]
            dve.did(dve.next(ready).tensor_reduce(m, ps, AX, ALU.max))
            dve.did(dve.next().tensor_tensor(pb, ps, m.unsqueeze(2).to_broadcast([P, NH, kw]), ALU.subtract))
            sub = dve.now()
            act.did(act.next(sub).activation(pb, pb, ACT.Exp, scale=scale))
            dve.did(dve.next(act.now()).tensor_reduce(z, pb, AX, ALU.add))
            dve.did(dve.next().reciprocal(z, z))
            dve.did(dve.next().tensor_tensor(pb, pb, z.unsqueeze(2).to_broadcast([P, NH, kw]), ALU.mult))
            return sub

        def weigh_values(pb, pt, t, nkb, value, y, tile0, order):
            claim(4, 4)
            pe.after(dve.now(), act.now())
            ptp = banks(4, 4).rearrange("p (h b q) -> p h b q", h=NH, b=NT)
            for h in range(NH):
                for b in range(nkb):
                    mm = nc.tensor.transpose(ptp[:, h, b, :], pb[:, h, b * P:(b + 1) * P], ident[:])
            pe.did(mm)
            act.did(act.next(pe.now()).activation(pt[:, :, 0:nkb, :], ptp[:, :, 0:nkb, :], ACT.Copy))
            empty(4, 4, act.now())
            claim(0)
            pe.after(act.now())
            for i, h in enumerate(order):
                lo = HD * (h % 2)
                for b in range(nkb):
                    mm = nc.tensor.matmul(PS[lo:lo + HD, 0, (h // 2) * P:(h // 2 + 1) * P],
                                          value(h, b), pt[:, i, b, :], start=b == 0, stop=b == nkb - 1,
                                          skip_group_check=True)
            pe.did(mm)
            act.did(act.next(pe.now()).activation(
                y[:, tile0:tile0 + 4, t * P:(t + 1) * P],
                PS[:, 0, :].rearrange("p (t q) -> p t q", t=4), ACT.Copy))
            return empty(0, 1, act.now())

        c1 = Region(arena)
        tri = c1.put("tri", [P, NT, S])
        cmask = c1.put("cmask", [P, NT, S])
        bsum = c1.put("bsum", [P, NT, LEVELS * P])
        lmask = c1.put("lmask", [P, LEVELS, P])
        onehot = c1.put("onehot", [NH, NH, P])
        lbw = c1.put("lbw", [P, DEPTH, S])
        lbl = c1.put("lbl", [P, DEPTH, S])
        yT = c1.put("yT", [P, DK, S])
        rgs = c1.put("rgs", [P, 2, S])
        work1 = c1.top
        ra = Region(work1)
        pb1 = ra.put("pb1", [P, NH, S])
        pt1 = ra.put("pt1", [P, NH, NT, P])
        qT = ra.put("qT", [P, 4, S])
        kT = ra.put("kT", [P, 4, S])
        vtok = ra.put("vtok", [P, NT, 512])
        nd = ra.put("nd", [NH, S])
        lsf = ra.put("lsf", [P, NT, NH])
        dq = ra.put("dq", [P, NT, NH])
        ft = ra.put("ft", [P, 3, NT * NH])
        rc = Region(work1)
        cx = rc.put("cx", [P, 2, S])
        cu = rc.put("cu", [P, 2, S + 2])
        cy = rc.put("cy", [P, 2, S])
        rh = Region(work1)
        E = rh.put("E", [P, 2, LEVELS, P])
        qe = rh.put("qe", [P, 2, LEVELS, P])
        ke = rh.put("ke", [P, 2, 2, LEVELS, P])
        rq = rh.put("rq", [P, 2, S])
        rk = rh.put("rk", [P, 2, S])
        rkt = rh.put("rkt", [P, NT, S])
        lf = rh.put("lf", [P, NT, S])
        lf2 = rh.put("lf2", [P, NT, S])
        ri = rh.put("ri", [P, NT, S])
        aT = rh.put("aT", [P, NT, 512])
        aX = hT[:, 2:4, :].rearrange("p t s -> p (t s)")
        am = hT[:, 0:2, :].rearrange("p t s -> p (t s)")
        ry = Region(work1)
        yhi = ry.put("yhi", [P, DK, S], F32R)
        ylo = ry.put("ylo", [P, DK, S], F32R)
        rf = Region(work1)
        sil = [rf.put(f"sil{i}", [P, 512]) for i in range(2)]
        ahi = [rf.put(f"ahi{i}", [P, 2, S], F32R) for i in range(2)]
        alo = [rf.put(f"alo{i}", [P, 2, S], F32R) for i in range(2)]
        fin = ra.top, rh.top, ry.top
        assert max(fin) <= nc.sbuf_usable_end, (fin, nc.sbuf_usable_end)
        for name in ("tri", "cmask", "bsum", "lmask", "onehot"):
            fetch(dict(tri=tri, cmask=cmask, bsum=bsum, lmask=lmask, onehot=onehot)[name][:], io[name])
        fetch(lbw[:], io["lbw"])
        for lane in (pe, act, dve):
            lane.after(fetched())

        def lower_bounds():
            a, b = lbw[:, 0, :], lbw[:, 1, :]
            m, t = hT[:, 0, :], hT[:, 1, :]
            v = lambda out, x, y, op: dve.did(dve.next().tensor_tensor(out, x, y, op))
            v(m, a, b, ALU.max)
            v(a, a, m, ALU.subtract)
            v(b, b, m, ALU.subtract)
            act.did(act.next(dve.now()).activation(lbw[:], lbw[:], ACT.Exp))
            dve.after(act.now())
            v(t, a, b, ALU.add)
            dve.did(dve.next().reciprocal(t, t))
            v(a, a, t, ALU.mult)
            v(b, b, t, ALU.mult)
            v(lbl[:, 0, :], a, a, ALU.subtract)
            v(t, a, b, ALU.add)
            v(lbl[:, 1, :], t, a, ALU.subtract)
            dve.did(dve.next().tensor_scalar(lbw[:], lbl[:], -1.0, 1.0, ALU.mult, ALU.add))

        lower_bounds()

        def vec1(l, name):
            a, b = V1[name]
            return v1[:, l, a:b]

        def head_norm(buf, nt, gain, sq):
            head_norm_ap(buf[:, 0:nt, :], nt, gain, sq)

        def head_norm_ap(buf, nt, gain, sq):
            group_rstd(buf, nt, False, HD, sq, dve.now())
            apply_rstd(buf, buf, nt, False, gain, [4, 5, 6, 7])

        def evacuate(dst, bank, step):
            act.did(act.next(step, dve.now()).activation(dst, PS[:, bank, :], ACT.Copy))
            return empty(bank, 1, act.now())

        def pair(t, i):
            return t[:, 2 * i:2 * i + 2, :].rearrange("p t s -> p (t s)")

        def forget_decay(l):
            wf = vec1(l, "wf").rearrange("p (k h) -> p k h", k=DK)
            claim(6)
            pe.after(dve.now())
            for t in range(NT):
                for k in range(DK):
                    mm = nc.tensor.matmul(PS[:, 6, t * NH:(t + 1) * NH], hT[:, k, t * P:(t + 1) * P],
                                          wf[:, k, :], start=k == 0, stop=k == DK - 1)
            pe.did(mm)
            z, a, e = (ft[:, i, :].rearrange("p (t h) -> p t h", t=NT) for i in range(3))
            fb = vec1(l, "fbias").unsqueeze(1).to_broadcast([P, NT, NH])
            dve.did(dve.next(pe.now(), act.now()).tensor_tensor(
                z, PS[:, 6, 0:NT * NH].rearrange("p (t h) -> p t h", t=NT), fb, ALU.add))
            empty(6, 1, dve.now())
            act.did(act.next(dve.now()).activation(a, z, ACT.Abs))
            act.did(act.next().activation(e, a, ACT.Exp, scale=-1.0))
            act.did(act.next().activation(a, e, ACT.Ln, bias=1.0))
            dve.did(dve.next(act.now()).scalar_tensor_tensor(
                out=lsf[:], in0=z, scalar=0.0, in1=a, op0=ALU.min, op1=ALU.subtract))
            claim(6)
            claim(7)
            pe.after(dve.now())
            for t in range(NT):
                for b in range(t + 1):
                    nc.tensor.matmul(PS[:, 6, t * NH:(t + 1) * NH], tri[:, b, t * P:(t + 1) * P],
                                     lsf[:, b, :], start=b == 0, stop=b == t)
            for b in range(NT):
                mm = nc.tensor.matmul(PS[0:NH, 7, 0:S], lsf[:, b, :], tri[:, b, :],
                                      start=b == 0, stop=b == NT - 1)
            pe.did(mm)
            act.did(act.next(pe.now()).activation(dq[:], PS[:, 6, 0:NT * NH].rearrange(
                "p (t h) -> p t h", t=NT), ACT.Copy))
            act.did(act.next().activation(nd[:], PS[0:NH, 7, 0:S], ACT.Copy, scale=-1.0))
            empty(6, 2, act.now())

        def forgetting_attention(l):
            for dst in (qT, kT):
                for i in range(2):
                    evacuate(pair(dst, i), 4 + i, unit_T(4 + i, hhi, hlo))
            for i in range(2):
                b = 4 + i
                step = unit_tok(b, hhi, hlo)
                act.did(act.next(step).activation(
                    vtok[:, :, i * UC:(i + 1) * UC], PS[:, b, :].rearrange("p (t c) -> p t c", t=NT), ACT.Copy))
                empty(b, 1, act.now())
            qs = small[:, 500:501]
            dve.did(dve.next().tensor_scalar(qs, vec1(l, "qg"), HD ** -0.5, None, ALU.mult))
            dve.after(act.now())
            head_norm(qT, 4, lambda t: qs, pb1[:, 0:4, :])
            head_norm(kT, 4, lambda t: vec1(l, "kg"), pb1[:, 0:4, :])
            forget_decay(l)
            for t in range(NT):
                kw = (t + 1) * P
                sp = banks(0, 4).rearrange("p (h k) -> p h k", h=NH)[:, :, 0:kw]
                claim(0, 4)
                pe.after(dve.now(), act.now())
                for i, h in enumerate(HEAD_AT):
                    lo = HD * (h % 2)
                    nc.tensor.matmul(sp[:, i, :], qT[lo:lo + HD, h // 2, t * P:(t + 1) * P],
                                     kT[lo:lo + HD, h // 2, 0:kw], start=True, stop=False)
                    mm = nc.tensor.matmul(sp[:, i, :], onehot[:, h, :], nd[:, 0:kw],
                                          start=False, stop=True)
                pe.did(mm)
                dve.after(pe.now(), act.now())
                for i, h in enumerate(HEAD_AT):
                    dve.did(dve.next().scalar_tensor_tensor(
                        out=pb1[:, i, 0:kw], in0=sp[:, i, :], scalar=dq[:, t, h:h + 1],
                        in1=cmask[:, t, 0:kw], op0=ALU.add, op1=ALU.add))
                empty(0, 4, dve.now())
                softmax(pb1[:, :, 0:kw], pb1[:, :, 0:kw], kw, 1.0, dve.now(), 0)
                weigh_values(pb1, pt1, t, t + 1, lambda h, b: vtok[:, b, h * HD:(h + 1) * HD], yT, 0, HEAD_AT)

        def short_conv(l):
            w = vec1(l, "conv").rearrange("p (t j) -> p t j", t=2)
            evacuate(cx[:].rearrange("p t s -> p (t s)"), 4, unit_T(4, hhi, hlo))
            gate_step = unit_T(5, hhi, hlo)
            c_step = unit_T(6, hhi, hlo)
            dve.did(dve.next(act.now()).memset(cu[:, :, 0:2], 0.0))
            dve.did(dve.next(c_step, act.now()).tensor_tensor(
                cu[:, :, 2:2 + S], PS[:, 6, :].rearrange("p (t s) -> p t s", t=2), cx[:], ALU.mult))
            empty(6, 1, dve.now())
            for t in range(2):
                dve.did(dve.next().tensor_scalar(cy[:, t, :], cu[:, t, 0:S], w[:, t, 0:1], None, ALU.mult))
                for j in (1, 2):
                    dve.did(dve.next().scalar_tensor_tensor(
                        out=cy[:, t, :], in0=cu[:, t, j:j + S], scalar=w[:, t, j:j + 1],
                        in1=cy[:, t, :], op0=ALU.mult, op1=ALU.add))
            dve.did(dve.next(gate_step, act.now()).tensor_tensor(
                pair(yT, 2), PS[:, 5, :], cy[:].rearrange("p t s -> p (t s)"), ALU.mult))
            empty(5, 1, dve.now())

        def hgrn(l):
            q_step = unit_T(4, hhi, hlo)
            f_step = unit_tok(5, hhi, hlo)
            i_step = unit_tok(6, hhi, hlo)
            g_step = unit_T(7, hhi, hlo)
            flat = lambda t: t[:].rearrange("p t s -> p (t s)")
            act.after(dve.now())
            act.did(act.next(q_step).activation(flat(rq), PS[:, 4, :], ACT.Silu))
            act.did(act.next(g_step).activation(flat(rgs), PS[:, 7, :], ACT.Silu))
            act.did(act.next(i_step).activation(flat(ri), PS[:, 6, :], ACT.Copy))
            act.did(act.next(f_step).activation(flat(lf), PS[:, 5, :], ACT.Sigmoid))
            act.did(act.next().activation(flat(rkt), PS[:, 5, :], ACT.Sigmoid, scale=-1.0))
            empty(4, 4, act.now())
            lb = lbl[:, l, :].unsqueeze(1).to_broadcast([P, NT, S])
            om = lbw[:, l, :].unsqueeze(1).to_broadcast([P, NT, S])
            dve.did(dve.next(act.now()).tensor_tensor(lf[:], lf[:], om, ALU.mult))
            dve.did(dve.next().tensor_tensor(lf[:], lf[:], lb, ALU.add))
            dve.did(dve.next().tensor_tensor(rkt[:], rkt[:], om, ALU.mult))
            dve.did(dve.next().tensor_scalar(lf2[:], lf[:], TINY, 1.0 / LN_CUT, ALU.max, ALU.mult))
            dve.did(dve.next().tensor_scalar(lf2[:], lf2[:], 1.0, None, ALU.min))
            dve.did(dve.next().tensor_scalar(lf[:], lf[:], LN_CUT, None, ALU.max))
            act.did(act.next(dve.now()).activation(lf[:], lf[:], ACT.Ln))
            act.did(act.next().activation(lf2[:], lf2[:], ACT.Ln))
            dve.did(dve.next(act.now()).tensor_tensor(lf[:], lf[:], lf2[:], ALU.add))
            claim(6)
            pe.after(dve.now())
            kp = PS[:, 6, :].rearrange("p (g s) -> p g s", g=2)
            for g in range(2):
                for t in range(NT):
                    mm = nc.tensor.transpose(kp[:, g, t * P:(t + 1) * P], rkt[:, t, g * P:(g + 1) * P], ident[:])
            pe.did(mm)
            act.did(act.next(pe.now()).activation(flat(rk), PS[:, 6, :], ACT.Copy))
            empty(6, 1, act.now())
            for t in range(NT):
                claim(0, 4)
                pe.after(dve.now())
                for g in range(2):
                    for c in range(2):
                        mm = nc.tensor.matmul(PS[:, 2 * g + c, :], lf[:, t, g * P:(g + 1) * P],
                                              bsum[:, t, c * 512:(c + 1) * 512], start=True, stop=True)
                pe.did(mm)
                act.did(act.next(pe.now(), dve.now()).activation(
                    E[:].rearrange("p g l s -> p (g l s)"), banks(0, 4), ACT.Exp))
                empty(0, 4, act.now())
                for g in range(2):
                    over = lambda x: x[:, g, t * P:(t + 1) * P].unsqueeze(1).to_broadcast([P, LEVELS, P])
                    dve.did(dve.next(act.now(), pe.now()).tensor_tensor(qe[:, g, :, :], E[:, g, :, :], over(rq), ALU.mult))
                    dve.did(dve.next().tensor_tensor(ke[:, t, g, :, :], E[:, g, :, :], over(rk), ALU.mult))
                ready = dve.now()
                for v in range(LEVELS):
                    b = v % 2 * 2
                    claim(b, 2)
                    pe.after(ready)
                    for h in range(4):
                        lo, g = HD * (h % 2), h // 2
                        ks = ke[lo:lo + HD, t, g, v, :] if v < LEVELS - 1 else rk[lo:lo + HD, g, t * P:(t + 1) * P]
                        qs = qe[lo:lo + HD, g, v, :] if v < LEVELS - 1 else rq[lo:lo + HD, g, t * P:(t + 1) * P]
                        mm = nc.tensor.matmul(PS[:, b + h % 2, g * P:(g + 1) * P], ks, qs, start=True, stop=True)
                    pe.did(mm)
                    mask = lmask[:, v, :].unsqueeze(1).unsqueeze(1).to_broadcast([P, 2, 2, P])
                    dst = aT[:, t, :] if v == 0 else am
                    dve.did(dve.next(pe.now()).tensor_tensor(
                        dst.rearrange("p (b g s) -> p b g s", b=2, g=2),
                        PS[:, b:b + 2, 0:2 * P].rearrange("p b (g s) -> p b g s", g=2), mask, ALU.mult))
                    empty(b, 2, dve.now())
                    if v:
                        dve.did(dve.next().tensor_tensor(aT[:, t, :], aT[:, t, :], am[:], ALU.add))
                if t:
                    claim(4, 2)
                    for h in range(4):
                        lo, g = HD * (h % 2), h // 2
                        mm = nc.tensor.matmul(PS[:, 4 + h % 2, g * P:(g + 1) * P], ke[lo:lo + HD, 0, g, LEVELS - 1, :],
                                              qe[lo:lo + HD, g, LEVELS - 1, :], start=True, stop=True)
                    pe.did(mm)
                    act.did(act.next(pe.now()).activation(aX.rearrange("p (b s) -> p b s", b=2),
                                                          PS[:, 4:6, 0:2 * P], ACT.Copy))
                    empty(4, 2, act.now())
            claim(5)
            pe.after(dve.now(), act.now())
            for h in range(4):
                lo = HD * (h % 2)
                for t in range(NT):
                    out = PS[lo:lo + HD, 5, (h // 2) * S + t * P:(h // 2) * S + (t + 1) * P]
                    hs = slice((h % 2 * 2 + h // 2) * P, (h % 2 * 2 + h // 2 + 1) * P)
                    vs = slice(h * HD, (h + 1) * HD)
                    if t:
                        nc.tensor.matmul(out, ri[:, 0, vs], aX[:, hs], start=True, stop=False,
                                         skip_group_check=True)
                    mm = nc.tensor.matmul(out, ri[:, t, vs], aT[:, t, hs], start=t == 0, stop=True,
                                          skip_group_check=True)
            pe.did(mm)
            evacuate(pair(yT, 3), 5, pe.now())

        def mixer_out(l):
            group_rstd(yT[:], DK, False, HD, hT[:], dve.now())
            g = vec1(l, "mix_gain")
            apply_rstd(yT, yT, DK, False, lambda t: g[:, t:t + 1], [4, 5, 6, 7])
            dve.did(dve.next().tensor_tensor(pair(yT, 3), pair(yT, 3), rgs[:].rearrange("p t s -> p (t s)"), ALU.mult))
            ready = split(yhi[:], ylo[:], yT[:], dve.now(), pe.now())
            project_to_x(yhi, ylo, ready)

        def open_sums():
            claim(0, 4)
            for b in range(4):
                mm = nc.tensor.matmul(PS[:, b, :], zero[:, 0:P], zero[:], start=True, stop=False,
                                      skip_group_check=True)
            pe.did(mm)

        def down(a_hi, a_lo, ready):
            w_hi, w_lo = take()
            pe.after(ready)
            for f in range(2):
                for d in range(DK):
                    cs = slice(f * D + d * P, f * D + (d + 1) * P)
                    mm = mm3(PS[:, d // 2, (d % 2) * S:(d % 2 + 1) * S], w_hi[:, cs], w_lo[:, cs],
                             a_hi[:, f, :], a_lo[:, f, :], False, False)
            return release(mm)

        def close_sums(step):
            for b in range(4):
                add_to_x(2 * b, b, step)

        used_a = [None, None, None]

        def swiglu_up(i):
            bg, bu = 4 + 2 * i, 5 + 2 * i
            g_step = unit_T(bg, hhi, hlo)
            u_step = unit_T(bu, hhi, hlo)
            act.did(act.next(g_step, dve.now()).activation(sil[i][:], PS[:, bg, :], ACT.Silu))
            empty(bg, 1, act.now())
            dve.did(dve.next(u_step, act.now()).tensor_tensor(sil[i][:], sil[i][:], PS[:, bu, :], ALU.mult))
            empty(bu, 1, dve.now())
            src = sil[i][:].rearrange("p (t s) -> p t s", t=2)
            return split(ahi[i][:], alo[i][:], src, dve.now(), used_a[i])

        def swiglu(groups, steps):
            open_sums()
            ready = swiglu_up(0)
            emptied[4:8] = [emptied[4], emptied[5], None, None]
            n = (groups - 2) // 2
            with Loop(n, steps, 6) as i:
                settled = [pe_idle(), act.now(), dve.now()]
                for b in range(4, 8):
                    emptied[b] = None
                emptied[4] = settled[1]
                emptied[6], emptied[7] = settled[1], settled[2]
                emptied[5] = settled[2]
                used_a[0] = used_a[1] = None
                r1 = swiglu_up(1)
                used_a[0] = down(ahi[0], alo[0], settled[2])
                r0 = swiglu_up(0)
                used_a[1] = down(ahi[1], alo[1], r1)
            done = pe_idle()
            used_a[0] = used_a[1] = done
            for b in range(4, 8):
                emptied[b] = dve.now()
            r1 = swiglu_up(1)
            down(ahi[0], alo[0], dve_settled(r1))
            close_sums(down(ahi[1], alo[1], r1))

        def dve_settled(step):
            return step

        def router():
            wr = vx[:, 8:72].rearrange("p (k e) -> p k e", k=DK)
            claim(4)
            pe.after(dve.now())
            for t in range(NT):
                for k in range(DK):
                    mm = nc.tensor.matmul(PS[:, 4, t * NE:(t + 1) * NE], hT[:, k, t * P:(t + 1) * P],
                                          wr[:, k, :], start=k == 0, stop=k == DK - 1)
            pe.did(mm)
            lg = small[:, 0:16].rearrange("p (t e) -> p t e", t=NT)
            m = small[:, 16:18]
            ex = small[:, 32:48].rearrange("p (t e) -> p t e", t=NT)
            rank = small[:, 48:64].rearrange("p (t e) -> p t e", t=NT)
            gt = small[:, 64:192].rearrange("p (t e j) -> p t e j", t=NT, e=NE)
            eq = small[:, 192:320].rearrange("p (t e j) -> p t e j", t=NT, e=NE)
            before = vx[:, 80:144].rearrange("p (e j) -> p e j", e=NE)
            vv = lambda *a: dve.did(dve.next().tensor_tensor(*a))
            rb = vx[:, 72:80].unsqueeze(1).to_broadcast([P, NT, NE])
            dve.after(pe.now())
            vv(lg, PS[:, 4, 0:16].rearrange("p (t e) -> p t e", t=NT), rb, ALU.add)
            empty(4, 1, dve.now())
            for t in range(NT):
                mine = lg[:, t, :].unsqueeze(2).to_broadcast([P, NE, NE])
                other = lg[:, t, :].unsqueeze(1).to_broadcast([P, NE, NE])
                vv(gt[:, t], other, mine, ALU.is_gt)
                vv(eq[:, t], other, mine, ALU.is_equal)
                vv(eq[:, t], eq[:, t], before, ALU.mult)
                vv(gt[:, t], gt[:, t], eq[:, t], ALU.add)
            dve.did(dve.next().tensor_reduce(rank, gt, AX, ALU.add))
            dve.did(dve.next().tensor_scalar(rank, rank, 1.5, None, ALU.is_lt))
            dve.did(dve.next().tensor_reduce(m, lg, AX, ALU.max))
            vv(ex, lg, m.unsqueeze(2).to_broadcast([P, NT, NE]), ALU.subtract)
            act.did(act.next(dve.now()).activation(ex, ex, ACT.Exp))
            dve.after(act.now())
            vv(ex, ex, rank, ALU.mult)
            dve.did(dve.next().tensor_reduce(m, ex, AX, ALU.add))
            dve.did(dve.next().reciprocal(m, m))
            vv(ex, ex, m.unsqueeze(2).to_broadcast([P, NT, NE]), ALU.mult)
            claim(5)
            pe.after(dve.now())
            for t in range(NT):
                for b in range(t + 1):
                    nc.tensor.matmul(PS[:, 5, t * NE:(t + 1) * NE], tri[:, b, t * P:(t + 1) * P],
                                     rank[:, b, :], start=b == 0, stop=b == t)
            for t in range(NT):
                mm = nc.tensor.matmul(PS[0:1, 5, 32:32 + NE], ones[:, 0:1], rank[:, t, :],
                                      start=t == 0, stop=t == NT - 1)
            pe.did(mm)
            cnt = PS[:, 5, 0:NT * NE].rearrange("p (t e) -> p t e", t=NT)
            dve.after(pe.now())
            vv(slots.rearrange("p (t e) -> p t e", t=NT), cnt, rank, ALU.mult)
            dve.did(dve.next().tensor_scalar(slots, slots, -1.0, None, ALU.add))
            dve.did(dve.next().tensor_reduce(m[0:1, 0:1], PS[0:1, 5, 32:32 + NE], AX, ALU.max))
            dve.did(dve.next().tensor_scalar(overflow[:], m[0:1, 0:1], float(P), None, ALU.is_gt))
            empty(5, 1, dve.now())

        slots = small[:, 384:400]
        gates = small[:, 32:48]
        GF = 512
        GE = D_FF // GF
        overflow = at_overflow
        rm = Region(arena)
        xghi = rm.put("xghi", [P, NE, DK, P], F32R)
        xglo = rm.put("xglo", [P, NE, DK, P], F32R)
        pm = rm.put("pm", [P, NE, S], F32R)
        xshi = rm.put("xshi", [P, DK, P], F32R)
        xslo = rm.put("xslo", [P, DK, P], F32R)
        msil = rm.put("msil", [P, GF])
        mact = rm.put("mact", [P, GF])
        mahi = rm.put("mahi", [P, GF // P, P], F32R)
        malo = rm.put("malo", [P, GF // P, P], F32R)
        at_pt = rm.top
        pt = rm.put("pt", [P, NT, NE, P], F32R)
        r = Region(at_pt)
        ohi = r.put("ohi", [P, D], F32R)
        olo = r.put("olo", [P, D], F32R)
        assert rm.top <= nc.sbuf_usable_end, (rm.top, nc.sbuf_usable_end)
        htkhi = at("htkhi", [P, NT, D], at_hhi, F32R)
        htklo = at("htklo", [P, NT, D], at_hlo, F32R)
        pms = at_pms
        gsl = small[:, 400:408]
        gs1 = small[:, 408:409]
        big = NE * P

        def tokens_to_rows():
            for src, dst, b, lane in ((hhi, htkhi, 0, act), (hlo, htklo, 4, dve)):
                claim(b, 4)
                pe.after(dve.now(), act.now())
                for t in range(NT):
                    for k in range(DK):
                        mm = nc.tensor.transpose(banks(b, 4)[:, t * D + k * P:t * D + (k + 1) * P],
                                                 src[:, k, t * P:(t + 1) * P].bitcast(F32), ident[:])
                pe.did(mm)
            act.did(act.next(pe.now()).activation(htkhi[:].rearrange("p t d -> p (t d)"), banks(0, 4), ACT.Copy))
            dve.did(dve.next(pe.now()).tensor_copy(htklo[:].rearrange("p t d -> p (t d)"), banks(4, 4)))
            empty(0, 4, act.now())
            empty(4, 4, dve.now())

        def gather(r):
            sl = small[:, 416:432]
            dve.did(dve.next(act.now(), pe.now()).tensor_scalar(sl, slots, float(-P * r), None, ALU.add))
            dve.did(dve.next().tensor_tensor(
                pt[:].rearrange("p t e s -> p (t e) s"), iota[:].unsqueeze(1).to_broadcast([P, NT * NE, P]),
                sl.unsqueeze(2).to_broadcast([P, NT * NE, P]), ALU.is_equal))
            pe.after(dve.now(), act.now())
            i = 0
            for half in range(2):
                es = slice(4 * half, 4 * half + 4)
                for k in range(DK):
                    b = i % 4 * 2
                    claim(b, 2)
                    for j, src in enumerate((htkhi, htklo)):
                        for t in range(NT):
                            mm = nc.tensor.matmul(PS[:, b + j, :], src[:, t, k * P:(k + 1) * P],
                                                  pt[:, t, es, :], start=t == 0, stop=t == NT - 1)
                    pe.did(mm)
                    v = PS[:, b:b + 2, :].rearrange("p b (e s) -> p b e s", e=4)
                    act.did(act.next(pe.now()).activation(xghi[:, es, k, :], v[:, 0], ACT.Copy))
                    dve.did(dve.next(pe.now()).tensor_copy(xglo[:, es, k, :], v[:, 1]))
                    empty(b, 1, act.now())
                    empty(b + 1, 1, dve.now())
                    i += 1
            claim(0, 5)
            for e in range(NE):
                for t in range(NT):
                    nc.tensor.transpose(banks(0, 4)[:, e * S + t * P:e * S + (t + 1) * P],
                                        pt[:, t, e, :].bitcast(F32), ident[:])
                for t in range(NT):
                    mm = nc.tensor.matmul(PS[:, 4, e:e + 1], pt[:, t, e, :].bitcast(F32),
                                          gates[:, t * NE + e:t * NE + e + 1], start=t == 0, stop=t == NT - 1)
            pe.did(mm)
            act.did(act.next(pe.now()).activation(pm[:].rearrange("p e s -> p (e s)"), banks(0, 4), ACT.Copy))
            dve.did(dve.next(pe.now()).tensor_copy(gsl, PS[:, 4, 0:NE]))
            empty(0, 4, act.now())
            empty(4, 1, dve.now())

        ACC, GATE, UP, TURN, OUT = 0, 4, 5, 6, 2

        def expert_tokens(e):
            flat = lambda x: x.rearrange("p a k s -> p (a k s)")
            act.did(act.next(pe.now(), pe_idle(), dve.now()).activation(
                xshi[:].rearrange("p k s -> p (k s)"), flat(xghi[:, bass.ds(e, 1), :, :]).bitcast(F32), ACT.Copy))
            dve.did(dve.next(pe.now(), pe_idle()).tensor_copy(
                xslo[:].rearrange("p k s -> p (k s)"), flat(xglo[:, bass.ds(e, 1), :, :]).bitcast(F32)))
            dve.did(dve.next().tensor_copy(gs1, gsl[:, bass.ds(e, 1)]))

        def expert_places(e):
            act.did(act.next(pe.now(), pe_idle()).activation(
                pms[:], pm[:, bass.ds(e, 1), :].rearrange("p a s -> p (a s)").bitcast(F32), ACT.Copy))

        def group_up(gate_free, up_free, sil_free):
            steps = []
            for b, free in ((GATE, gate_free), (UP, up_free)):
                for half in range(2):
                    w_hi, w_lo = take()
                    if half == 0:
                        pe.after(free)
                    for k in range(4):
                        cs = slice(k * GF, (k + 1) * GF)
                        kk = 4 * half + k
                        mm = mm3(PS[:, b, :], xshi[:, kk, :], xslo[:, kk, :], w_hi[:, cs],
                                 None if w_lo is None else w_lo[:, cs], kk == 0, kk == 7)
                    step = release(mm)
                steps.append(step)
            act.did(act.next(steps[0], sil_free).activation(msil[:], PS[:, GATE, :], ACT.Silu))
            dve.did(dve.next(act.now(), steps[1]).scalar_tensor_tensor(
                out=mact[:], in0=msil[:], scalar=gs1, in1=PS[:, UP, :], op0=ALU.mult, op1=ALU.mult))

        def group_turn():
            pe.after(dve.now())
            for f in range(GF // P):
                mm = nc.tensor.transpose(PS[:, TURN, f * P:(f + 1) * P], mact[:, f * P:(f + 1) * P], ident[:])
            pe.did(mm)
            src = PS[:, TURN, :].rearrange("p (f s) -> p f s", s=P)
            act.did(act.next(pe.now()).activation(mahi[:], src, ACT.Copy))
            dve.did(dve.next(act.now(), pe.now()).tensor_tensor(malo[:], src, mahi[:].bitcast(F32), ALU.subtract))

        def group_down(ready_act, ready_dve):
            for half in range(2):
                w_hi, w_lo = take()
                if half == 0:
                    pe.after(ready_act, ready_dve)
                for f in range(2):
                    for c in range(2):
                        cs = slice(f * D + c * 512, f * D + (c + 1) * 512)
                        mm = mm3(PS[:, ACC + c, :], mahi[:, 2 * half + f, :], malo[:, 2 * half + f, :],
                                 w_hi[:, cs], None if w_lo is None else w_lo[:, cs], False, False)
                step = release(mm)
            return step

        def open_acc():
            for c in range(2):
                mm = nc.tensor.matmul(PS[:, ACC + c, :], zero[:, 0:P].bitcast(F32R), zero[:].bitcast(F32R),
                                      start=True, stop=False, skip_group_check=True)
            return mm

        def take_out(step):
            act.did(act.next(step).activation(ohi[:], banks(ACC, 2), ACT.Copy))
            dve.did(dve.next(act.now(), step).tensor_tensor(olo[:], banks(ACC, 2), ohi[:].bitcast(F32), ALU.subtract))

        def scatter(out_act, out_dve):
            pe.after(out_act, out_dve)
            free = [None, None]
            for q in range(4):
                b = OUT + q % 2
                pe.after(free[q % 2])
                for f in range(2):
                    cs = slice((2 * q + f) * P, (2 * q + f + 1) * P)
                    out = PS[:, b, f * S:(f + 1) * S]
                    nc.tensor.matmul(out, ohi[:, cs], pms[:], start=True, stop=False)
                    mm = nc.tensor.matmul(out, olo[:, cs], pms[:], start=False, stop=True)
                pe.did(mm)
                dst = xT[:, 2 * q:2 * q + 2, :].rearrange("p t s -> p (t s)")
                dve.did(dve.next(pe.now()).tensor_tensor(dst, dst, PS[:, b, :], ALU.add))
                free[q % 2] = dve.now()

        def back(lane, n):
            return Step(lane.sem, lane.base + lane.count - n)

        def groups_of_expert():
            with Loop(GE - 1, (1, 2, 2), 6):
                ready = act.now(), dve.now()
                group_up(back(act, 1), back(dve, 1), dve.now())
                group_down(*ready)
                group_turn()

        def experts():
            expert_tokens(0)
            expert_places(0)
            pe.after(act.now(), dve.now())
            pe.did(open_acc())
            group_up(None, None, None)
            group_turn()
            with Loop(NE - 1, EXPERT_STEPS, 6 * (GE - 1) + 6) as e:
                groups_of_expert()
                expert_tokens(e + 1)
                tokens = act.now(), dve.now()
                step = group_down(act.now(), dve.now())
                take_out(step)
                out = act.now(), dve.now()
                pe.after(*tokens)
                group_up(None, None, out[1])
                scatter(*out)
                expert_places(e + 1)
                open_acc()
                pe.after(act.now())
                group_turn()
            groups_of_expert()
            take_out(group_down(act.now(), dve.now()))
            scatter(act.now(), dve.now())

        def routed_ffn():
            nonlocal stream
            settle()
            tokens_to_rows()
            gather(0)
            moe_start = main.at()
            experts()
            settle()
            for engine in (nc.sync, nc.gpsimd):
                engine.wait_ge(dve.sem, dve.base + dve.count)
            flag = nc.values_load(overflow[0:1, 0:1], min_val=0, max_val=1,
                                  skip_runtime_bounds_check_because="it is the result of a comparison")
            with nc.If(flag > 0):
                kept = [(x.sem, x.base, x.count) for x in (pe, act, dve)]
                for x, name in zip((pe, act, dve), ("pe", "act", "dve")):
                    x.sem, x.base, x.count = sem(f"overflow_{name}_steps"), 0, 0
                stream = Whole([slow_raw], 0, [sem("overflow_landed")], sem("overflow_used"),
                               first_unit=moe_start, used0=1)
                open_acc().then_inc(stream.used, 1)
                pe.did(open_acc())
                act.did(act.next(pe.now()).activation(small[:, 440:441], gates[:, 0:1], ACT.Copy))
                dve.did(dve.next(act.now()).tensor_copy(small[:, 441:442], gates[:, 0:1]))
                gather(1)
                experts()
                settle()
                nc.sync.wait_ge(dve.sem, dve.base + dve.count)
                stream = main
                for x, (a, b, c) in zip((pe, act, dve), kept):
                    x.sem, x.base, x.count = a, b, c
            settle()

        def vec1_of(l, name):
            g = vec1(l, name)
            return lambda t: g[:, t:t + 1]

        for l in range(1 if io.get("stop") == 1 else DEPTH):
            norm_to_h(vec1_of(l, "norm_mix"))
            pe.after(dve.now())
            forgetting_attention(l)
            pe.after(act.now(), dve.now())
            act.after(pe.now())
            dve.after(pe.now(), act.now())
            short_conv(l)
            act.after(dve.now())
            hgrn(l)
            dve.after(act.now())
            mixer_out(l)
            act.after(dve.now())
            norm_to_h(vec1_of(l, "norm_ffn"))
            pe.after(dve.now())
            if l % 2 == 0:
                swiglu(G1, (0, 4, 4))
            else:
                router()
                routed_ffn()

        if io.get("stop") in (1, 2):
            nc.sync.wait_ge(dve.sem, dve.base + dve.count)
            nc.sync.dma_start(io["out"], xT[:]).then_inc(stored, 16)
            nc.sync.wait_ge(stored, 16)
            return

        settle()
        c2 = Region(arena)
        rope_in = {n: c2.put(n, io[n].shape) for n in ("cosA", "sinA", "rotA", "cosB", "sinB", "rotB",
                                                        "cosC", "sinC", "rotC")}
        vl = c2.put("vl", [P, V2N])
        nlam = c2.put("nlam", [P, 4])
        y2 = c2.put("y2", [P, 12, S])
        soft = c2.top
        rp = Region(soft)
        pb2 = [rp.put(f"pb2{i}", [P, NH, S]) for i in range(2)]
        pt2 = rp.put("pt2", [P, NH, NT, P])
        r = Region(soft)
        chi = r.put("chi", [P, 5, S], F32R)
        clo = r.put("clo", [P, 5, S], F32R)
        r = Region(soft)
        y2hi = r.put("y2hi", [P, 12, S], F32R)
        y2lo = r.put("y2lo", [P, 12, S], F32R)
        qk = rp.top
        r = Region(qk)
        qa = r.put("qa", [P, 4, S])
        kva = r.put("kva", [P, 2, S])
        va = r.put("va", [P, NT, P])
        r = Region(qk)
        qb = r.put("qb", [P, 4, S])
        kb = r.put("kb", [P, 4, S])
        vb = r.put("vb", [P, NT, 512])
        r = Region(qk)
        cc = r.put("cc", [P, 6, S])
        qc = r.put("qc", [P, NH, S])
        kc = r.put("kc", [P, NH, S])
        vc = r.put("vc", [P, NT, 512])
        end2 = r.top
        r = Region(qk)
        mg = r.put("mg", [P, DK, S])
        mhi = r.put("mhi", [P, DK, S], F32R)
        mlo = r.put("mlo", [P, DK, S], F32R)
        gs = [r.put(f"gs{i}", [P, 512]) for i in range(2)]
        end2 = max(end2, r.top)
        r = Region(soft)
        rl = [r.put(f"rl{i}", [P, 512]) for i in range(3)]
        bhi = [r.put(f"bhi{i}", [P, 2, S], F32R) for i in range(3)]
        blo = [r.put(f"blo{i}", [P, 2, S], F32R) for i in range(3)]
        assert max(end2, r.top) <= nc.sbuf_usable_end, (end2, r.top)
        loaded2 = sem("second_loaded")
        for n, t in rope_in.items():
            nc.scalar.dma_start(t[:], io[n]).then_inc(loaded2, 16)
        for lane in (pe, dve):
            lane.after(Step(loaded2, 16 * len(rope_in)))

        def vec2(name):
            return vl[:, V2[name][0]:V2[name][1]]

        def column(name, n=1):
            return lambda t: vec2(name)[:, (t if n > 1 else 0):(t if n > 1 else 0) + 1]

        def rope(buf, nt, n, which, tmp):
            rot, cos, sin = (rope_in[x + which] for x in ("rot", "cos", "sin"))
            k = (nt + 1) // 2
            claim(4, k)
            pe.after(dve.now(), act.now())
            out = banks(4, k).rearrange("p (t s) -> p t s", s=S)
            for t in range(nt):
                mm = nc.tensor.matmul(out[0:n, t, :], rot[0:n, 0:n], buf[:, t, :], start=True, stop=True)
            pe.did(mm)
            wide = lambda x: x[0:n, :].unsqueeze(1).to_broadcast([n, nt, S])
            dve.did(dve.next(pe.now()).tensor_tensor(tmp, out[0:n, 0:nt, :], wide(sin), ALU.mult))
            empty(4, k, dve.now())
            dve.did(dve.next().tensor_tensor(buf, buf, wide(cos), ALU.mult))
            dve.did(dve.next().tensor_tensor(buf, buf, tmp, ALU.add))

        def scores(parts, pb, scale):
            sp = banks(0, 4).rearrange("p (h k) -> p h k", h=NH)
            claim(0, 4)
            pe.after(dve.now(), act.now())
            for i in range(NH):
                q, k = parts(i)
                mm = nc.tensor.matmul(sp[:, i, :], q, k, start=True, stop=True)
            pe.did(mm)
            dve.after(act.now())
            empty(0, 4, softmax(sp, pb[:], S, scale, pe.now(), 0))

        def branch_a():
            for i in range(2):
                evacuate(pair(qa, i), 4 + i, unit_T(4 + i, hhi, hlo))
            evacuate(pair(kva, 0), 6, unit_T(6, hhi, hlo))
            head_norm(qa, 4, column("aq"), hT[:, 0:4, :])
            kv1 = kva[:, 0:1, :]
            head_norm_ap(kv1, 1, column("ak"), hT[:, 0:1, :])
            rope(qa[:], 4, P, "A", hT[:, 0:4, :])
            rope(kv1, 1, P, "A", hT[:, 0:1, :])
            claim(4)
            pe.after(act.now(), dve.now())
            for t in range(NT):
                mm = nc.tensor.transpose(PS[:, 4, t * P:(t + 1) * P], kva[:, 1, t * P:(t + 1) * P], ident[:])
            pe.did(mm)
            act.did(act.next(pe.now()).activation(va[:].rearrange("p t c -> p (t c)"), PS[:, 4, 0:S], ACT.Copy))
            empty(4, 1, act.now())
            for t in range(NT):
                def parts(h):
                    lo = HD * (h // 4)
                    return qa[lo:lo + HD, h % 4, t * P:(t + 1) * P], kva[lo:lo + HD, 0, :]
                scores(parts, pb2[0], HD ** -0.5)
                weigh_values(pb2[0], pt2, t, NT, lambda h, b: va[:, b, h // 4 * HD:(h // 4 + 1) * HD],
                             y2, 0, range(NH))

        def branch_b():
            for dst in (qb, kb):
                for i in range(2):
                    evacuate(pair(dst, i), 4 + i, unit_T(4 + i, hhi, hlo))
            for i in range(2):
                step = unit_tok(6 + i, hhi, hlo)
                act.did(act.next(step).activation(
                    vb[:, :, i * UC:(i + 1) * UC], PS[:, 6 + i, :].rearrange("p (t c) -> p t c", t=NT), ACT.Copy))
                empty(6 + i, 1, act.now())
            dve.after(act.now())
            rope(qb[:], 4, P, "B", hT[:, 0:4, :])
            rope(kb[:], 4, P, "B", hT[:, 0:4, :])
            lam = vec2("lam").rearrange("p (a b d) -> p a b d", a=2, b=2)
            pr = small[:, 64:128].rearrange("p (a d) -> p a d", a=2)
            dve.did(dve.next().tensor_tensor(pr, lam[:, :, 0, :], lam[:, :, 1, :], ALU.mult))
            dve.did(dve.next().tensor_reduce(nlam[:, 0:2], pr, AX, ALU.add))
            act.did(act.next(dve.now()).activation(nlam[:, 0:2], nlam[:, 0:2], ACT.Exp))
            dve.did(dve.next(act.now()).tensor_tensor(nlam[:, 2:3], nlam[:, 1:2], nlam[:, 0:1], ALU.subtract))
            dve.did(dve.next().tensor_tensor(nlam[:, 2:3], nlam[:, 2:3], vec2("lam_init"), ALU.subtract))
            for t in range(NT):
                for c in range(2):
                    def parts(i):
                        h = HEAD_AT[i]
                        lo = HD * (h % 2) + 32 * c
                        return qb[lo:lo + 32, h // 2, t * P:(t + 1) * P], kb[lo:lo + 32, h // 2, :]
                    scores(parts, pb2[c], 32 ** -0.5)
                dve.did(dve.next().scalar_tensor_tensor(
                    out=pb2[0][:], in0=pb2[1][:], scalar=nlam[:, 2:3], in1=pb2[0][:],
                    op0=ALU.mult, op1=ALU.add))
                weigh_values(pb2[0], pt2, t, NT, lambda h, b: vb[:, b, h * HD:(h + 1) * HD],
                             y2, 4, HEAD_AT)
            g = nlam[:, 3:4]
            dve.did(dve.next(act.now()).tensor_scalar(g, vec2("lam_init"), -1.0, 1.0, ALU.mult, ALU.add))
            dve.did(dve.next().tensor_tensor(g, g, vec2("bsub"), ALU.mult))
            head_norm_ap(y2[:, 4:8, :], 4, lambda t: g, hT[:, 0:4, :])

        NOPE, ROT = 64, 32
        QW = NOPE + ROT

        def branch_c():
            for i in range(3):
                evacuate(pair(cc, i), 4 + i, unit_T(4 + i, hhi, hlo))
            dve.after(act.now())
            for a, n, gain in ((0, 3, "cq"), (3, 2, "ckv")):
                src = cc[:, a:a + n, :]
                group_rstd(src, n, True, n * P, hT[:, 0:n, :], dve.now())
                apply_rstd(src, src, n, True, column(gain, n), [4, 5])
            ready = split(chi[:], clo[:], cc[:, 0:5, :], dve.now())
            rope(cc[0:QW, 5:6, :], 1, QW, "C", hT[0:QW, 0:1, :])
            act.did(act.next(dve.now()).activation(
                kc[NOPE:QW, :, :], cc[NOPE:QW, 5:6, :].to_broadcast([ROT, NH, S]), ACT.Copy))
            for i in range(2):
                w_hi, w_lo = take()
                claim(4 + 2 * i, 2)
                pe.after(ready)
                wh, wl = (w[:, 0:3 * 4 * QW].rearrange("p (k c) -> p k c", k=3) for w in (w_hi, w_lo))
                out = banks(4 + 2 * i, 2).rearrange("p (h s) -> p h s", s=S)
                for h in range(4):
                    cs = slice(h * QW, (h + 1) * QW)
                    for k in range(3):
                        mm = mm3(out[0:QW, h, :], wh[:, k, cs], wl[:, k, cs], chi[:, k, :], clo[:, k, :],
                                 k == 0, k == 2)
                step = release(mm)
                act.did(act.next(step).activation(qc[0:QW, 4 * i:4 * i + 4, :], out[0:QW, :, :], ACT.Copy))
                empty(4 + 2 * i, 2, act.now())
            w_hi, w_lo = take()
            wh, wl = (w[:].rearrange("p (k c) -> p k c", k=2) for w in (w_hi, w_lo))
            claim(0, 8)
            out = banks(4, 4).rearrange("p (h s) -> p h s", s=S)
            for h in range(NH):
                for k in range(2):
                    mm3(out[:, h, :], wh[:, k, h * P:(h + 1) * P], wl[:, k, h * P:(h + 1) * P],
                        chi[:, 3 + k, :], clo[:, 3 + k, :], k == 0, k == 1)
            for t in range(NT):
                ts = slice(t * P, (t + 1) * P)
                for k in range(2):
                    vh, vl_ = (w[:, k, :].rearrange("p (h c) -> p h c", h=NH)[:, :, NOPE:] for w in (wh, wl))
                    mm = mm3(PS[:, t, :], chi[:, 3 + k, ts], clo[:, 3 + k, ts], vh, vl_, k == 0, k == 1)
            step = release(mm)
            act.did(act.next(step).activation(kc[0:NOPE, :, :], out[0:NOPE, :, :], ACT.Copy))
            act.did(act.next().activation(vc[:].rearrange("p t c -> p (t c)"), banks(0, 2), ACT.Copy))
            empty(0, 8, act.now())
            dve.after(act.now())
            rope(qc[0:QW, :, :], NH, QW, "C", hT[0:QW, :, :])
            for t in range(NT):
                scores(lambda h: (qc[0:QW, h, t * P:(t + 1) * P], kc[0:QW, h, :]), pb2[0], QW ** -0.5)
                weigh_values(pb2[0], pt2, t, NT, lambda h, b: vc[:, b, h * HD:(h + 1) * HD],
                             y2, 8, range(NH))

        def merge():
            ready = split(y2hi[:], y2lo[:], y2[:], act.now(), pe.now())
            for jj in range(2):
                for n in range(3):
                    for i in range(2):
                        step = unit_T(4 + i, hhi, hlo)
                        act.did(act.next(step, dve.now()).activation(gs[i][:], PS[:, 4 + i, :], ACT.Sigmoid))
                        empty(4 + i, 1, act.now())
                    w_hi, w_lo = take()
                    claim(6, 2)
                    pe.after(ready)
                    wh, wl = (w[:].rearrange("p (k c) -> p k c", k=4) for w in (w_hi, w_lo))
                    for f in range(4):
                        for k in range(4):
                            mm = mm3(PS[:, 6 + f // 2, f % 2 * S:(f % 2 + 1) * S],
                                     wh[:, k, f * P:(f + 1) * P], wl[:, k, f * P:(f + 1) * P],
                                     y2hi[:, 4 * n + k, :], y2lo[:, 4 * n + k, :], k == 0, k == 3)
                    step = release(mm)
                    for i in range(2):
                        dst = pair(mg, 2 * jj + i)
                        dve.did(dve.next(step, act.now()).tensor_tensor(
                            dst if n == 0 else gs[i][:], gs[i][:], PS[:, 6 + i, :], ALU.mult))
                        empty(6 + i, 1, dve.now())
                        if n:
                            dve.did(dve.next().tensor_tensor(dst, dst, gs[i][:], ALU.add))
            project_to_x(mhi, mlo, split(mhi[:], mlo[:], mg[:], dve.now(), pe.now()))

        used_b = [None] * 3

        def relu_up(i):
            step = unit_T(4 + i, hhi, hlo)
            act.did(act.next(step, dve.now()).activation(rl[i][:], PS[:, 4 + i, :], ACT.Relu))
            empty(4 + i, 1, act.now())
            dve.did(dve.next(act.now()).tensor_tensor(rl[i][:], rl[i][:], rl[i][:], ALU.mult))
            return split(bhi[i][:], blo[i][:], rl[i][:].rearrange("p (t s) -> p t s", t=2), dve.now(), used_b[i])

        def relu_ffn(steps):
            open_sums()
            ready = relu_up(0)
            with Loop((G2 - 1) // 3, steps, 6):
                before_act, before_dve = act.now(), dve.now()
                for b in range(4, 7):
                    emptied[b] = before_act
                for j in range(3):
                    used_b[j] = None
                r = before_dve
                for j in range(3):
                    r2 = relu_up((j + 1) % 3)
                    used_b[j] = down(bhi[j], blo[j], r)
                    r = r2
            close_sums(down(bhi[0], blo[0], dve.now()))

        def layer2(l):
            settle()
            src = v2[:, bass.ds(l, 1), :].rearrange("p a c -> p (a c)")
            dve.did(dve.next().tensor_copy(vl[:], src))
            norm_to_h(column("ln1", 8))
            branch_a()
            settle()
            branch_b()
            settle()
            branch_c()
            settle()
            merge()
            settle()
            norm_to_h(column("ln2", 8))
            settle()
            relu_ffn((0, 6, 6))

        if io.get("stop") == 3:
            layer2(0)
            final = xT
        else:
            with Loop(DEPTH, LAYER_STEPS, U_BLK2) as l:
                layer2(l)
            settle()
            group_rstd(xT[:], DK, True, D, hT[:], dve.now())
            apply_rstd(hT, xT, DK, True, lambda t: vx[:, t:t + 1], [4, 5, 6, 7])
            final = hT
        nc.sync.wait_ge(dve.sem, dve.base + dve.count)
        nc.sync.dma_start(io["out"], final[:]).then_inc(stored, 16)
        nc.sync.wait_ge(stored, 16)


def constants():
    f = np.float32
    s, t = np.arange(P)[:, None], np.arange(S)[None, :]
    c = {}
    c["tri"] = np.stack([(s + b * P <= t) for b in range(NT)], 1).astype(f)
    c["cmask"] = np.stack([np.where(t <= s + b * P, 0.0, NEG) for b in range(NT)], 1).astype(f)
    tt = np.arange(P)[None, :]
    bsum = np.zeros((P, NT, LEVELS, P), f)
    lmask = np.zeros((P, LEVELS, P), f)
    for v in range(LEVELS - 1):
        n = 1 << v
        mid = tt // (2 * n) * (2 * n) + n - 1
        m = np.where(tt > mid, (s > mid) & (s <= tt), (s > tt) & (s <= mid))
        bsum[:, :, v, :] = m[:, None, :]
        lmask[:, v, :] = (s // (2 * n) == tt // (2 * n)) & (s // n % 2 == 0) & (tt // n % 2 == 1)
    bsum[:, 0, LEVELS - 1, :] = s > tt
    bsum[:, 1, LEVELS - 1, :] = s <= tt
    lmask[:, LEVELS - 1, :] = s == tt
    c["bsum"], c["lmask"] = bsum.reshape(P, NT, -1), lmask
    def angles(pos, dim, theta):
        inv = (f(theta) ** (-np.arange(0, dim, 2, dtype=f) / f(dim))).astype(f)
        return (pos.astype(f)[:, None] * inv[None, :]).astype(f).T

    def rotary(n, spans):
        cos, sin, rot = np.ones((n, S), f), np.zeros((n, S), f), np.zeros((n, n), f)
        for a, ang in spans:
            h = len(ang)
            for i in (0, h):
                cos[a + i:a + i + h], sin[a + i:a + i + h] = np.cos(ang), np.sin(ang)
            for i in range(h):
                rot[a + h + i, a + i], rot[a + i, a + h + i] = -1, 1
        return cos, sin, rot

    pos = np.arange(S)
    row, col = angles(pos // 64, 32, 10000.0), angles(pos % 64, 32, 10000.0)
    spans = dict(A=(P, [(a + o, g) for a in (0, 64) for o, g in ((0, row), (32, col))]),
                 B=(P, [(a, angles(pos, 8, 500000.0)) for a in range(0, P, 32)]),
                 C=(96, [(64, angles(pos, 32, 10000.0))]))
    for which, (n, sp) in spans.items():
        c["cos" + which], c["sin" + which], c["rot" + which] = rotary(n, sp)
    c["onehot"] = np.repeat(np.eye(NH, dtype=f)[:, :, None], P, 2)
    c["ident"] = np.eye(P, dtype=f)
    c["iota"] = np.broadcast_to(np.arange(P, dtype=f), (P, P)).copy()
    half = np.arange(P) // HD
    selw = np.zeros((P, DK, 16), f)
    for k in range(DK):
        selw[np.arange(P), k, 2 * k + half] = 1
    c["selw"] = selw
    c["selT"] = np.ascontiguousarray(selw.transpose(2, 1, 0))
    return c


def by_part(v):
    return np.moveaxis(v.reshape(*v.shape[:-1], -1, P), -1, 0)


def k_units(w, cols=UC):
    K, N = w.shape
    return w.reshape(K // P, P, N // cols, cols).transpose(2, 1, 0, 3).reshape(N // cols, P, -1)


def down_units(w):
    return w.reshape(-1, 2, P, w.shape[1]).transpose(0, 2, 1, 3).reshape(-1, P, 2 * w.shape[1])


def pipelined(up, dn):
    out = [up[0]]
    for g in range(len(up) - 1):
        out += [up[g + 1], dn[g:g + 1]]
    return out + [dn[-1:]]


def pack(inp):
    f = np.float32
    units = []
    w_in, w_out = inp["w_in"], inp["w_out"]
    for l in range(DEPTH):
        w = w_in[l]
        units.append(k_units(w[:, 0:1536]))
        units.append(k_units(w[:, 1544:1544 + 1792]))
        units.append(k_units(w_out[l]))
        if l == 0:
            a = np.stack([k_units(inp["ffn_w_gate"][0]), k_units(inp["ffn_w_up"][0])], 1)
            units += pipelined(a, down_units(inp["ffn_w_down"][0]))
        else:
            wide = lambda w: w.reshape(NE, 2, 4, P, 7, 512).transpose(0, 4, 1, 3, 2, 5).reshape(NE, 7, 2, P, UNIT)
            gu = np.concatenate([wide(inp["moe_w_gate"][0]), wide(inp["moe_w_up"][0])], 2)
            dn = inp["moe_w_down"][0].reshape(NE, 7, 2, 2, P, D).transpose(0, 1, 2, 4, 3, 5).reshape(NE, 7, 2, P, UNIT)
            units.append(gu[0, 0])
            for e in range(NE):
                for g in range(6):
                    units += [gu[e, g + 1], dn[e, g]]
                units.append(dn[e, 6])
                if e + 1 < NE:
                    units.append(gu[e + 1, 0])
            del gu, dn
    for l in range(DEPTH):
        w = inp["w_in_2"][l]
        perm = [h * HD + d for t in range(4) for h in (t, t + 4) for d in range(HD)]
        units.append(k_units(w[:, 0:512][:, perm]))
        units.append(k_units(w[:, 512:768]))
        units.append(k_units(w[:, 768:2304]))
        lat = np.zeros((D, 768), f)
        lat[:, 0:640] = w[:, 2304:2944]
        lat[:, 640 + 64:640 + 96] = w[:, 2944:2976]
        units.append(k_units(lat))
        uq = k_units(inp["c_w_uq_2"][l], 384)
        units.append(np.concatenate([uq, np.zeros((2, P, UNIT - uq.shape[2]), f)], 2))
        units.append(k_units(inp["c_w_ukv_2"][l], 1024))
        gates = w[:, 2976:].reshape(D, 3, D)
        for jj in range(2):
            for n in range(3):
                units.append(k_units(gates[:, n, jj * 512:(jj + 1) * 512]))
                units.append(k_units(inp["w_branch_2"][l][n][:, jj * 512:(jj + 1) * 512], 512))
        units.append(k_units(inp["w_out_2"][l]))
        units += pipelined(k_units(inp["w_ff1_2"][l])[:, None], down_units(inp["w_ff2_2"][l]))
    units.append(np.zeros((LEAD, P, UNIT), f))
    arrays = {"ws": np.concatenate(units, 0)}
    arrays["xT"] = by_part(np.ascontiguousarray(inp["x"][0])).transpose(0, 2, 1)
    rep = lambda v: np.broadcast_to(v, (P,) + v.shape)
    two = lambda v: np.concatenate([v, v])[:, None]
    v1 = []
    for l in range(DEPTH):
        wf = w_in[l][:, 1536:1544].reshape(DK, P, NH).transpose(1, 0, 2).reshape(P, -1)
        conv = inp["conv_w"][l].reshape(3, 2, P).transpose(2, 1, 0).reshape(P, 6)
        v1.append(np.concatenate([by_part(inp["norm_mix"][l]), by_part(inp["norm_ffn"][l]),
                                  by_part(inp["mix_out_gain"][l]), two(inp["q_norm_gain"][l]),
                                  two(inp["k_norm_gain"][l]), conv, rep(inp["attn_f_bias"][l]), wf], 1))
    arrays["v1"] = np.stack(v1, 1)
    v2 = []
    for l in range(DEPTH):
        v2.append(np.concatenate([by_part(inp["ln1_g_2"][l]), by_part(inp["ln2_g_2"][l]),
                                  two(inp["a_q_norm_2"][l]), two(inp["a_k_norm_2"][l]),
                                  two(inp["b_subln_2"][l]), by_part(inp["c_q_norm_2"][l]),
                                  by_part(inp["c_kv_norm_2"][l]), rep(inp["b_lambda_2"][l].reshape(-1)),
                                  np.full((P, 1), LAMBDA_INIT[l], f)], 1))
    arrays["v2"] = np.stack(v2, 1)
    wr = inp["moe_router_w"][0].reshape(DK, P, NE).transpose(1, 0, 2).reshape(P, -1)
    arrays["vx"] = np.concatenate([by_part(inp["final_g_2"]), wr, rep(inp["moe_router_b"][0]),
                                   rep(np.tril(np.ones((NE, NE), np.float32), -1).reshape(-1))], 1)
    arrays["lbw"] = rep(inp["hgrn_lb_logits"])
    arrays.update(constants())
    return {k: np.ascontiguousarray(v) for k, v in arrays.items()}


def kernel(_stop=0, **inputs):
    import concourse.bacc as bacc
    from concourse.bass_utils import run_bass_kernel_spmd as run

    arrays = pack({k: np.asarray(v) for k, v in inputs.items()})
    nc = bacc.Bacc("TRN2", target_bir_lowering=False, num_devices=1, dynamic_dma_scratch_size=1024)
    io = {k: nc.dram_tensor(f"in_{k}", a.shape, F32, kind="ExternalInput").ap() for k, a in arrays.items()}
    io["out"] = nc.dram_tensor("out_T", (P, DK, S), F32, kind="ExternalOutput").ap()
    if _stop:
        io["stop"] = _stop
    build(nc, io)
    r = run(nc, [{f"in_{k}": a for k, a in arrays.items()}], core_ids=[0])
    out = r.results[0]["out_T"]
    return np.ascontiguousarray(out.transpose(2, 1, 0)).reshape(1, S, D)
```

```python
from contextlib import ExitStack

import numpy as np

import concourse.bass as bass
from concourse import mybir

F32 = mybir.dt.float32
F32R = mybir.dt.float32r
ACT = mybir.ActivationFunctionType
ALU = mybir.AluOpType
AX = mybir.AxisListType.X

P = 128
S = 256
NT = S // P
D = 1024
DK = D // P
DEPTH = 2
HD = 64
NH = 8
SLOT = [0, 2, 1, 3]
UNIT = 2048
UC = UNIT // DK
RAW, SPLIT = 3, 3
LEAD = 2
EPS = 1e-6
TINY = 1e-30
LN_CUT = 2.0 ** -60
NEG = -1e30

D_FF = 3584
G1 = D_FF // UC
NE = 8
D_FF2 = 4096
G2 = D_FF2 // UC
LEVELS = 8

U_BLK2 = 2 + 1 + 6 + 3 + 2 + 1 + 12 + 6 + 4 + 2 * G2

EXPERT_STEPS = (11, 17, 21)
LAYER_STEPS = (59, 130, 170)

V1 = dict(norm_mix=(0, 8), norm_ffn=(8, 16), mix_gain=(16, 24), qg=(24, 25), kg=(25, 26),
          conv=(26, 32), fbias=(32, 40), wf=(40, 104))
V1N = 104
V2 = dict(ln1=(0, 8), ln2=(8, 16), aq=(16, 17), ak=(17, 18), bsub=(18, 19), cq=(19, 22),
          ckv=(22, 24), lam=(24, 152), lam_init=(152, 153))
V2N = 153
LAMBDA_INIT = [0.8 - 0.6 * float(np.exp(-0.3 * l)) for l in range(DEPTH)]


class Step:

    def __init__(self, sem, value):
        self.sem, self.value = sem, value


class Lane:

    def __init__(self, engine, sem):
        self.engine, self.sem = engine, sem
        self.base, self.count = 0, 0

    def after(self, *steps):
        for step in steps:
            if step is not None:
                self.engine.wait_ge(step.sem, step.value)

    def now(self):
        return Step(self.sem, self.base + self.count)

    def when(self, *steps):
        self.after(*steps)
        return self.engine

    def did(self, instruction):
        instruction.then_inc(self.sem, 1)
        self.count += 1
        return self.now()


class Serial(Lane):

    def next(self, *steps):
        if not (isinstance(self.base, int) and self.base + self.count == 0):
            self.after(self.now())
        self.after(*steps)
        return self.engine


def build(nc, io):
    ctx = ExitStack()
    with ctx:
        def sem(name):
            return ctx.enter_context(nc.semaphore(name))

        pe = Lane(nc.tensor, sem("pe_steps"))
        act = Serial(nc.scalar, sem("act_steps"))
        dve = Serial(nc.vector, sem("dve_steps"))
        raw_landed = [sem(f"raw_landed{i}") for i in range(RAW)]
        hi_ready, lo_ready, unit_used = sem("hi_ready"), sem("lo_ready"), sem("unit_used")
        loaded, stored = sem("small_loaded"), sem("out_stored")

        top = (nc.sbuf_base + 63) // 64 * 64

        def at(name, shape, offset, dtype=F32):
            return nc.alloc_sbuf_tensor_at(name, shape, dtype, offset=offset)

        def rows(shape):
            n = 4
            for x in shape[1:]:
                n *= x
            return (n + 31) // 32 * 32

        def put(name, shape, dtype=F32):
            nonlocal top
            t = at(name, shape, top, dtype)
            top += rows(shape)
            return t

        raw = [put(f"raw{i}", [P, UNIT]) for i in range(RAW)]
        whi = [put(f"whi{i}", [P, UNIT], F32R) for i in range(SPLIT)]
        wlo = [put(f"wlo{i}", [P, UNIT], F32R) for i in range(SPLIT)]
        xT = put("xT", [P, DK, S])
        slow_raw = at("slow_raw", [P, UNIT], top)
        hT = put("hT", [P, DK, S])
        at_hhi, at_hlo = top, top + rows([P, DK, S])
        hhi = put("hhi", [P, DK, S], F32R)
        hlo = put("hlo", [P, DK, S], F32R)
        v1 = put("v1", [P, DEPTH, V1N])
        v2 = put("v2", [P, DEPTH, V2N])
        vx = put("vx", [P, 8 + 64 + 8 + 64])
        selT = put("selT", [16, DK, P])
        ident = put("ident", [P, P])
        ones = put("ones", [P, P])
        zero = put("zero", [P, 512])
        epsc = put("epsc", [P, 1])
        rs = put("rs", [16, S])
        small = put("small", [P, 512])
        rstd = small[:, 0:S]
        selw = put("selw", [P, DK, 16])
        stat = put("stat", [P, 4, 8])
        overflow = put("overflow", [1, 1], mybir.dt.int32)
        pms = put("pms", [P, S], F32R)
        iota = put("iota", [P, P])
        arena = top

        class Region:

            def __init__(self, start):
                self.top = start

            def put(self, name, shape, dtype=F32):
                t = at(name, shape, self.top, dtype)
                self.top += rows(shape)
                return t

        PS = ctx.enter_context(nc.psum_tensor("PS", [P, 8, 512], F32))
        emptied = [None] * 8

        def banks(b, n):
            return PS[:, b:b + n, :].rearrange("p b c -> p (b c)")

        def claim(b, n=1):
            for step in {id(s): s for s in emptied[b:b + n] if s is not None}.values():
                pe.after(step)

        def empty(b, n, step):
            for i in range(b, b + n):
                emptied[i] = step
            return step

        class Stream:

            def __init__(self, raw, lead, raw_landed, used, first_unit=0, used0=0):
                self.raw, self.lead, self.raw_landed, self.used = raw, lead, raw_landed, used
                self.first_unit, self.used0 = first_unit, used0
                self.base = self.n = self.k0 = self.rounds = 0

            def load(self, u, k):
                r = k % len(self.raw)
                nc.sync.dma_start(self.raw[r][:], io["ws"][bass.ds(u + self.first_unit, 1), :, :].rearrange(
                    "a p n -> p (a n)")).then_inc(self.raw_landed[r], 16)
                return self.raw_landed[r], 16 * (self.rounds + k // len(self.raw) + 1)

            def at(self):
                return self.base + self.n

            def taken(self):
                return Step(self.used, self.at() + self.used0)

        class Split(Stream):

            def prepare(self, u, k):
                s = k % SPLIT
                first = isinstance(u, int) and u < RAW
                if not first:
                    nc.sync.wait_ge(lo_ready, u - RAW + 1)
                landed, count = self.load(u, k)
                nc.scalar.wait_ge(landed, count)
                if not first:
                    nc.scalar.wait_ge(unit_used, u - SPLIT + 1)
                nc.scalar.activation(whi[s][:], self.raw[k % RAW][:], ACT.Copy).then_inc(hi_ready, 1)
                nc.vector.wait_ge(hi_ready, u + 1)
                nc.vector.tensor_tensor(wlo[s][:], self.raw[k % RAW][:], whi[s][:].bitcast(F32),
                                        ALU.subtract).then_inc(lo_ready, 1)

            def take(self):
                self.prepare(self.at() + LEAD, self.k0 + self.n + LEAD)
                nc.tensor.wait_ge(lo_ready, self.at() + 1)
                self.n += 1
                s = (self.k0 + self.n - 1) % SPLIT
                return whi[s], wlo[s]

        class Whole(Stream):

            def take(self):
                nc.sync.wait_ge(self.used, self.at() + self.used0)
                landed, count = self.load(self.at(), self.k0 + self.n)
                nc.tensor.wait_ge(landed, count)
                self.n += 1
                return self.raw[0], None

        stream = main = Split(raw, LEAD, raw_landed, unit_used)

        def take():
            return stream.take()

        def release(mm):
            mm.then_inc(stream.used, 1)
            return stream.taken()

        class Loop:

            def __init__(self, n, steps, units):
                self.n, self.steps, self.units = n, steps, units

            def __enter__(self):
                ring = len(stream.raw)
                assert self.units % RAW == 0 and self.units % SPLIT == 0
                self.old = [(x.base, x.count) for x in (pe, act, dve)]
                self.at = stream.base, stream.n, stream.k0, stream.rounds
                self.fori = nc.Fori(0, self.n)
                i = self.fori.__enter__()
                for x, k in zip((pe, act, dve), self.steps):
                    x.base, x.count = i * k + (x.base + x.count), 0
                rounds, k = divmod(stream.k0 + stream.n, ring)
                stream.rounds = i * (self.units // ring) + (stream.rounds + rounds)
                stream.base, stream.n, stream.k0 = i * self.units + stream.at(), 0, k
                return i

            def __exit__(self, *a):
                got = tuple(x.count for x in (pe, act, dve)) + (stream.n,)
                if a[0] is None:
                    assert got == tuple(self.steps) + (self.units,), ("steps and units of a pass", got)
                self.fori.__exit__(*a)
                for x, (b, c), k in zip((pe, act, dve), self.old, self.steps):
                    x.base, x.count = b, c + self.n * k
                stream.base, stream.n, stream.k0, stream.rounds = self.at
                stream.n += self.n * self.units

        n_loaded = 0

        def fetch(dst, src):
            nonlocal n_loaded
            nc.sync.dma_start(dst, src).then_inc(loaded, 16)
            n_loaded += 1

        def fetched():
            return Step(loaded, 16 * n_loaded)

        x_loaded = sem("x_loaded")
        nc.sync.dma_start(xT[:], io["xT"]).then_inc(x_loaded, 16)
        nc.sync.dma_start(v1[:], io["v1"]).then_inc(x_loaded, 16)
        dve.did(dve.next().memset(ones[:], 1.0))
        dve.did(dve.next().memset(zero[:], 0.0))
        dve.did(dve.next().memset(epsc[:], EPS))
        act.after(dve.now())
        pe.after(dve.now())
        for u in range(LEAD):
            main.prepare(u, u)
        fetch(v2[:], io["v2"])
        fetch(vx[:], io["vx"])
        fetch(selT[:], io["selT"])
        fetch(ident[:], io["ident"])
        fetch(selw[:], io["selw"])
        fetch(iota[:], io["iota"])
        for lane in (pe, act, dve):
            lane.after(Step(x_loaded, 32))

        def back(lane, n):
            return Step(lane.sem, lane.base + lane.count - n)

        def mm3(out, a_hi, a_lo, b_hi, b_lo, start, stop):
            if b_lo is None:
                nc.tensor.matmul(out, a_hi.bitcast(F32), b_hi, start=start, stop=False, skip_group_check=True)
                return nc.tensor.matmul(out, a_lo.bitcast(F32), b_hi, start=False, stop=stop,
                                        skip_group_check=True)
            nc.tensor.matmul(out, a_hi, b_hi, start=start, stop=False, skip_group_check=True)
            nc.tensor.matmul(out, a_hi, b_lo, start=False, stop=False, skip_group_check=True)
            return nc.tensor.matmul(out, a_lo, b_hi, start=False, stop=stop, skip_group_check=True)

        def split(hi, lo, src, *after):
            act.did(act.next(*after).activation(hi, src, ACT.Copy))
            return dve.did(dve.next(act.now(), *after).tensor_tensor(lo, src, hi.bitcast(F32), ALU.subtract))

        h_ready = [None] * (DK // 2)
        x_added = [None] * (DK // 2)

        def unit_T(bank, hi, lo, nk=DK, cols=UC, width=P, *after):
            w_hi, w_lo = take()
            claim(bank)
            pe.after(*after)
            wh = w_hi[:, 0:nk * cols].rearrange("p (k c) -> p k c", k=nk)
            wl = w_lo[:, 0:nk * cols].rearrange("p (k c) -> p k c", k=nk)
            for f in range(2):
                for k in range(nk):
                    if hi is hhi and k % 2 == 0 and h_ready[k // 2]:
                        pe.after(h_ready[k // 2])
                        h_ready[k // 2] = None
                    mm = mm3(PS[0:width, bank, f * S:(f + 1) * S], wh[:, k, f * width:(f + 1) * width],
                             wl[:, k, f * width:(f + 1) * width], hi[:, k, :], lo[:, k, :],
                             k == 0, k == nk - 1)
            return release(mm)

        def unit_tok(bank, hi, lo, *after):
            w_hi, w_lo = take()
            claim(bank)
            pe.after(*after)
            wh = w_hi[:].rearrange("p (k c) -> p k c", k=DK)
            wl = w_lo[:].rearrange("p (k c) -> p k c", k=DK)
            for t in range(NT):
                for k in range(DK):
                    ts = slice(t * P, (t + 1) * P)
                    mm = mm3(PS[:, bank, t * UC:(t + 1) * UC], hi[:, k, ts], lo[:, k, ts],
                             wh[:, k, :], wl[:, k, :], k == 0, k == DK - 1)
            return release(mm)

        fillers = []

        def fill(n=1):
            for _ in range(min(n, len(fillers))):
                fillers.pop(0)()

        SUMS = 6

        def group_rstd(src, nt, sel_of, rows_, scale, sq, *after):
            act.did(act.next(*after).activation(sq, src, ACT.Square))
            squared = act.now()
            fill()
            claim(SUMS)
            pe.after(squared)
            for t in range(nt):
                mm = nc.tensor.matmul(PS[0:rows_, SUMS, 0:S], sel_of(t), sq[:, t, :],
                                      start=t == 0, stop=t == nt - 1)
            pe.did(mm)
            act.did(act.next(pe.now(), dve.now()).activation(rs[0:rows_, :], PS[0:rows_, SUMS, 0:S], ACT.Sqrt,
                                                  bias=epsc[0:rows_, :], scale=scale))
            empty(SUMS, 1, act.now())
            dve.did(dve.next(act.now()).reciprocal(rs[0:rows_, :], rs[0:rows_, :]))
            spread_ready = dve.now()
            fill()
            pe.after(spread_ready)

        def apply_rstd(dst, src, nt, selT_of, rows_, gain, banks4):
            for t0 in range(0, nt, 2):
                b = banks4[(t0 // 2) % len(banks4)]
                n = min(2, nt - t0)
                claim(b)
                for t in range(t0, t0 + n):
                    mm = nc.tensor.matmul(PS[:, b, (t - t0) * S:(t - t0 + 1) * S], selT_of(t), rs[0:rows_, :],
                                          start=True, stop=True)
                pe.did(mm)
                for t in range(t0, t0 + n):
                    dve.did(dve.when(pe.now()).scalar_tensor_tensor(
                        out=dst[:, t, :], in0=src[:, t, :], scalar=gain(t),
                        in1=PS[:, b, (t - t0) * S:(t - t0 + 1) * S], op0=ALU.mult, op1=ALU.mult))
                empty(b, 1, dve.now())
            return dve.now()

        def whole_norm(gain, split_it=True):
            claim(SUMS)
            n = DK // 2
            for j in range(n):
                act.did(act.when(x_added[j]).activation(hT[:, 2 * j:2 * j + 2, :], xT[:, 2 * j:2 * j + 2, :],
                                                        ACT.Square))
                pe.after(act.now())
                for t in (2 * j, 2 * j + 1):
                    mm = nc.tensor.matmul(PS[:, SUMS, 0:S], ones[:], hT[:, t, :], start=t == 0, stop=t == DK - 1)
            pe.did(mm)
            act.did(act.next(pe.now(), dve.now()).activation(rstd, PS[:, SUMS, 0:S], ACT.Sqrt,
                                                             bias=epsc[:], scale=1.0 / D))
            empty(SUMS, 1, act.now())
            dve.did(dve.next(act.now()).reciprocal(rstd, rstd))
            dve.after(dve.now())
            halved = []
            for j in range(n + 1):
                if j < n:
                    for t in (2 * j, 2 * j + 1):
                        ins = nc.vector.scalar_tensor_tensor(out=hT[:, t, :], in0=xT[:, t, :], scalar=gain(t),
                                                             in1=rstd, op0=ALU.mult, op1=ALU.mult)
                    dve.did(ins)
                    if split_it:
                        act.did(act.when(dve.now()).activation(hhi[:, 2 * j:2 * j + 2, :],
                                                               hT[:, 2 * j:2 * j + 2, :], ACT.Copy))
                        halved.append(act.now())
                if j and split_it:
                    ts = slice(2 * j - 2, 2 * j)
                    h_ready[j - 1] = dve.did(dve.when(halved[j - 1]).tensor_tensor(
                        hlo[:, ts, :], hT[:, ts, :], hhi[:, ts, :].bitcast(F32), ALU.subtract))
            x_added[:] = [None] * n

        def pe_idle():
            return None if isinstance(stream.at(), int) and stream.at() == 0 else stream.taken()

        def settle():
            steps = [x.now() for x in (pe, act, dve)] + [pe_idle()]
            for lane in (pe, act, dve):
                lane.after(*steps)
            for b in range(8):
                emptied[b] = None
            h_ready[:] = x_added[:] = [None] * (DK // 2)

        def add_to_x(tile0, bank, step):
            out = xT[:, tile0:tile0 + 2, :].rearrange("p t s -> p (t s)")
            x_added[tile0 // 2] = dve.did(dve.next(step).tensor_tensor(out, out, PS[:, bank, :], ALU.add))
            return empty(bank, 1, dve.now())

        def project_to_x(hi, lo, ready):
            for j in range(DK // 2):
                step = unit_T(j, hi, lo, DK, UC, P, ready)
                add_to_x(2 * j, j, step)

        class Job:

            def __init__(self, pair, keys=S, bias=None, less=None, value=None, place=None, dst=None,
                         decay=None):
                self.pair = pair
                self.keys = keys
                self.decay = decay
                self.bias = bias
                self.less = less
                self.value = value
                self.place = place
                self.dst = dst

        PB = 4

        def attention(jobs, pbs, pts, stat, fill_every=1):
            N = len(jobs)
            turned, ready, scored, copied, used, buf, ptb = ([None] * N for _ in range(7))
            turns = [0]

            def score(n):
                j, b, pb, w = jobs[n], 2 * (n % 2), pbs[n % PB], jobs[n].keys
                sp = PS[:, b:b + 2, :].rearrange("p b (h k) -> p b h k", h=2)
                m, z = stat[:, n % PB, 0:4], stat[:, n % PB, 4:8]
                free = turned[n - PB + (jobs[n - PB].value is None)] if n >= PB else None
                claim(b, 2)
                for i in range(4):
                    q, k = j.pair(i)
                    out = sp[:, i // 2, i % 2, 0:w]
                    mm = nc.tensor.matmul(out, q, k, start=True, stop=j.decay is None)
                    if j.decay:
                        mm = nc.tensor.matmul(out, *j.decay(i), start=False, stop=True)
                pe.did(mm)
                dve.after(pe.now(), free)
                if j.bias:
                    for i in range(4):
                        column, mask = j.bias(i)
                        ins = nc.vector.scalar_tensor_tensor(
                            out=pb[:, i, 0:w], in0=sp[:, i // 2, i % 2, 0:w], scalar=column,
                            in1=mask, op0=ALU.add, op1=ALU.add)
                    dve.did(ins)
                    empty(b, 2, dve.now())
                    dve.did(dve.next().tensor_reduce(m, pb[:, :, 0:w], AX, ALU.max, negate=True))
                    src = lambda i: pb[:, i, 0:w]
                else:
                    dve.did(nc.vector.tensor_reduce(m.rearrange("p (b h) -> p b h", b=2), sp[:, :, :, 0:w],
                                                    AX, ALU.max, negate=True))
                    src = lambda i: sp[:, i // 2, i % 2, 0:w]
                act.after(dve.now(), free)
                for i in range(4):
                    ins = nc.scalar.activation(pb[:, i, 0:w], src(i), ACT.Exp, bias=m[:, i:i + 1],
                                               accum_out=z[:, i:i + 1])
                act.did(ins)
                scored[n] = act.now()
                if not j.bias:
                    empty(b, 2, act.now())

            def normalise(n):
                j, pb, w = jobs[n], pbs[n % PB], jobs[n].keys
                z = stat[:, n % PB, 4:8]
                dve.did(dve.when(scored[n]).reciprocal(z, z))
                dve.after(dve.now())
                for i in range(4):
                    ins = nc.vector.tensor_scalar(pb[:, i, 0:w], pb[:, i, 0:w], z[:, i:i + 1], None, ALU.mult)
                dve.did(ins)
                buf[n] = pb
                if j.less is not None:
                    buf[n] = pbs[(n - 1) % PB]
                    dve.did(dve.next().scalar_tensor_tensor(
                        out=buf[n][:], in0=pb[:], scalar=j.less, in1=buf[n][:], op0=ALU.mult, op1=ALU.add))
                ready[n] = dve.now()

            def turn(n):
                j, kb = jobs[n], jobs[n].keys // P
                tp = banks(4, 2).rearrange("p (h b q) -> p h b q", h=4, b=NT)
                claim(4, 2)
                pe.after(ready[n])
                for i in range(4):
                    for b in range(kb):
                        mm = nc.tensor.transpose(tp[:, i, b, :], buf[n][:, i, b * P:(b + 1) * P], ident[:])
                turned[n] = pe.did(mm)
                k = turns[0]
                ptb[n] = pts[k % 2]
                before = [x for x in used if x is not None]
                act.did(act.when(pe.now(), before[k - 2] if k >= 2 else None).activation(
                    ptb[n][:, :, 0:kb, :], tp[:, :, 0:kb, :], ACT.Copy))
                copied[n] = empty(4, 2, act.now())
                turns[0] += 1

            def weigh(n):
                j, kb = jobs[n], jobs[n].keys // P
                claim(6)
                pe.after(copied[n])
                for i in range(4):
                    lo, col = j.place(i)
                    for b in range(kb):
                        mm = nc.tensor.matmul(PS[lo:lo + HD, 6, col * P:(col + 1) * P], j.value(i, b),
                                              ptb[n][:, i, b, :], start=b == 0, stop=b == kb - 1,
                                              skip_group_check=True)
                used[n] = pe.did(mm)
                act.did(act.when(pe.now()).activation(
                    j.dst, PS[:, 6, 0:2 * P].rearrange("p (t q) -> p t q", t=2), ACT.Copy))
                empty(6, 1, act.now())

            for n in range(N + 2):
                if n < N:
                    score(n)
                if n >= 2 and jobs[n - 2].value:
                    weigh(n - 2)
                if n % fill_every == 0:
                    fill()
                if n < N:
                    normalise(n)
                if 1 <= n <= N and jobs[n - 1].value:
                    turn(n - 1)
            dve.after(act.now(), pe.now())

        c1 = Region(arena)
        tri = c1.put("tri", [P, NT, S])
        cmask = c1.put("cmask", [P, NT, S])
        bsum = c1.put("bsum", [P, NT, LEVELS * P])
        lmask = c1.put("lmask", [P, LEVELS, P])
        onehot = c1.put("onehot", [NH, NH, P])
        lbw = c1.put("lbw", [P, DEPTH, S])
        lbl = c1.put("lbl", [P, DEPTH, S])
        yT = c1.put("yT", [P, DK, S])
        rgs = c1.put("rgs", [P, 2, S])
        work1 = c1.top
        rw = Region(work1)
        cx = rw.put("cx", [P, 2, S])
        cb = rw.put("cb", [P, 2, S])
        cc1 = rw.put("cc1", [P, 2, S])
        cu = rw.put("cu", [P, 2, S + 2])
        rq = rw.put("rq", [P, 2, S])
        zf = rw.put("zf", [P, NT, S])
        ri = rw.put("ri", [P, NT, S])
        rd = Region(rw.top)
        rk = rd.put("rk", [P, 2, S])
        rkt = rd.put("rkt", [P, NT, S])
        lf = rd.put("lf", [P, NT, S])
        lf2 = rd.put("lf2", [P, NT, S])
        cy = rd.put("cy", [P, 2, S])
        ra = Region(rd.top)
        pb1 = [ra.put(f"pb1{i}", [P, 4, S]) for i in range(PB)]
        pt1 = [ra.put(f"pt1{i}", [P, 4, NT, P]) for i in range(2)]
        qkT = ra.put("qkT", [P, 8, S])
        vtok = ra.put("vtok", [P, NT, 512])
        nd = ra.put("nd", [NH, S])
        lsf = ra.put("lsf", [P, NT, NH])
        dq = ra.put("dq", [P, NT, NH])
        ft = ra.put("ft", [P, 3, NT * NH])
        rh = Region(rd.top)
        qe = [rh.put(f"qe{t}", [P, 2, LEVELS, P]) for t in range(NT)]
        ke = [rh.put(f"ke{t}", [P, 2, LEVELS, P]) for t in range(NT)]
        aT = rh.put("aT", [P, NT, 512])
        aX = hT[:, 2:4, :].rearrange("p t s -> p (t s)")
        am = hT[:, 0:2, :].rearrange("p t s -> p (t s)")
        ry = Region(rw.top)
        yhi = ry.put("yhi", [P, DK, S], F32R)
        ylo = ry.put("ylo", [P, DK, S], F32R)
        rf = Region(work1)
        sil = [rf.put(f"sil{i}", [P, 512]) for i in range(2)]
        ahi = [rf.put(f"ahi{i}", [P, 2, S], F32R) for i in range(2)]
        alo = [rf.put(f"alo{i}", [P, 2, S], F32R) for i in range(2)]
        fin = ra.top, rh.top, ry.top
        assert max(fin) <= nc.sbuf_usable_end, (fin, nc.sbuf_usable_end)
        for name in ("tri", "cmask", "bsum", "lmask", "onehot"):
            fetch(dict(tri=tri, cmask=cmask, bsum=bsum, lmask=lmask, onehot=onehot)[name][:], io[name])
        fetch(lbw[:], io["lbw"])

        def lower_bounds():
            a, b = lbw[:, 0, :], lbw[:, 1, :]
            m, t = pb1[0][:, 0, :], pb1[0][:, 1, :]
            v = lambda out, x, y, op: dve.did(dve.next().tensor_tensor(out, x, y, op))
            v(m, a, b, ALU.max)
            v(a, a, m, ALU.subtract)
            v(b, b, m, ALU.subtract)
            act.did(act.next(dve.now()).activation(lbw[:], lbw[:], ACT.Exp))
            dve.after(act.now())
            v(t, a, b, ALU.add)
            dve.did(dve.next().reciprocal(t, t))
            v(a, a, t, ALU.mult)
            v(b, b, t, ALU.mult)
            v(lbl[:, 0, :], a, a, ALU.subtract)
            v(t, a, b, ALU.add)
            v(lbl[:, 1, :], t, a, ALU.subtract)
            dve.did(dve.next().tensor_scalar(lbw[:], lbl[:], -1.0, 1.0, ALU.mult, ALU.add))

        def vec1(l, name):
            a, b = V1[name]
            return v1[:, l, a:b]

        def head_norm(buf, nt, gain, sq, *after):
            group_rstd(buf, nt, lambda t: selw[:, t, :], 16, 1.0 / HD, sq, *after)
            return apply_rstd(buf, buf, nt, lambda t: selT[:, t, :], 16, gain, [4, 5])

        def evacuate(dst, bank, step, scale=1.0, func=ACT.Copy, *after):
            act.did(act.when(step, *after).activation(dst, PS[:, bank, :], func, scale=scale))
            return empty(bank, 1, act.now())

        def pair(t, i):
            return t[:, 2 * i:2 * i + 2, :].rearrange("p t s -> p (t s)")

        def forget_decay(l):
            wf = vec1(l, "wf").rearrange("p (k h) -> p k h", k=DK)
            claim(6)
            pe.after(dve.now())
            for t in range(NT):
                for k in range(DK):
                    mm = nc.tensor.matmul(PS[:, 6, t * NH:(t + 1) * NH], hT[:, k, t * P:(t + 1) * P],
                                          wf[:, k, :], start=k == 0, stop=k == DK - 1)
            pe.did(mm)
            z, a, e = (ft[:, i, :].rearrange("p (t h) -> p t h", t=NT) for i in range(3))
            fb = vec1(l, "fbias").unsqueeze(1).to_broadcast([P, NT, NH])
            dve.did(dve.next(pe.now(), act.now()).tensor_tensor(
                z, PS[:, 6, 0:NT * NH].rearrange("p (t h) -> p t h", t=NT), fb, ALU.add))
            empty(6, 1, dve.now())
            act.did(act.next(dve.now()).activation(a, z, ACT.Abs))
            act.did(act.next().activation(e, a, ACT.Exp, scale=-1.0))
            act.did(act.next().activation(a, e, ACT.Ln, bias=1.0))
            dve.did(dve.next(act.now()).scalar_tensor_tensor(
                out=lsf[:], in0=z, scalar=0.0, in1=a, op0=ALU.min, op1=ALU.subtract))
            claim(6)
            claim(7)
            pe.after(dve.now())
            for t in range(NT):
                for b in range(t + 1):
                    nc.tensor.matmul(PS[:, 6, t * NH:(t + 1) * NH], tri[:, b, t * P:(t + 1) * P],
                                     lsf[:, b, :], start=b == 0, stop=b == t)
            for b in range(NT):
                mm = nc.tensor.matmul(PS[0:NH, 7, 0:S], lsf[:, b, :], tri[:, b, :],
                                      start=b == 0, stop=b == NT - 1)
            pe.did(mm)
            act.did(act.next(pe.now()).activation(dq[:], PS[:, 6, 0:NT * NH].rearrange(
                "p (t h) -> p t h", t=NT), ACT.Copy))
            act.did(act.next().activation(nd[:], PS[0:NH, 7, 0:S], ACT.Copy, scale=-1.0))
            empty(6, 2, act.now())

        def flat(t):
            return t[:].rearrange("p t s -> p (t s)")

        def by_unit(unit, dst, scale=1.0, func=ACT.Copy, then=None):
            def run():
                step = unit(7, hhi, hlo)
                act.did(act.when(step).activation(dst, PS[:, 7, :], func, scale=scale))
                empty(7, 1, act.now())
                if then:
                    then()
            fillers.append(run)

        def forgetting_attention(l):
            for i in range(4):
                evacuate(pair(qkT, i), 4 + i % 2, unit_T(4 + i % 2, hhi, hlo))
            for i in range(2):
                b = 4 + i
                step = unit_tok(b, hhi, hlo)
                act.did(act.when(step).activation(
                    vtok[:, :, i * UC:(i + 1) * UC], PS[:, b, :].rearrange("p (t c) -> p t c", t=NT), ACT.Copy))
                empty(b, 1, act.now())
            by_unit(unit_tok, flat(zf), then=lambda: decays(l))
            for dst in (cx, cb, cc1):
                by_unit(unit_T, flat(dst), then=(lambda: short_conv(l)) if dst is cc1 else None)
            by_unit(unit_T, flat(rq), func=ACT.Silu)
            by_unit(unit_tok, flat(ri))
            by_unit(unit_T, flat(rgs), func=ACT.Silu)
            qs = small[:, 500:501]
            dve.did(dve.next().tensor_scalar(qs, vec1(l, "qg"), HD ** -0.5, None, ALU.mult))
            dve.after(dve.now(), act.now())
            if l == 0:
                for lane in (pe, act, dve):
                    lane.after(fetched())
                lower_bounds()
            forget_decay(l)
            head_norm(qkT[:], 8, lambda t: qs if t < 4 else vec1(l, "kg"), hT[:], dve.now(), pe.now())
            pe.after(dve.now(), act.now())
            jobs = []
            for t in range(NT):
                for c in range(2):
                    def head(i, c=c):
                        return 4 * c + SLOT[i]

                    def operands(i, t=t, head=head):
                        h = head(i)
                        lo = HD * (h % 2)
                        return (qkT[lo:lo + HD, h // 2, t * P:(t + 1) * P],
                                qkT[lo:lo + HD, 4 + h // 2, 0:(t + 1) * P])
                    jobs.append(Job(
                        operands, keys=(t + 1) * P,
                        decay=lambda i, t=t, head=head: (onehot[:, head(i), :], nd[:, 0:(t + 1) * P]),
                        bias=lambda i, t=t, head=head: (dq[:, t, head(i):head(i) + 1], cmask[:, t, 0:(t + 1) * P]),
                        value=lambda i, b, head=head: vtok[:, b, head(i) * HD:(head(i) + 1) * HD],
                        place=lambda i: (HD * (SLOT[i] % 2), SLOT[i] // 2),
                        dst=yT[:, 2 * c:2 * c + 2, t * P:(t + 1) * P]))
            attention(jobs, pb1, pt1, stat)
            fill(len(fillers))

        def short_conv(l):
            w = vec1(l, "conv").rearrange("p (t j) -> p t j", t=2)
            dve.did(dve.next(act.now()).memset(cu[:, :, 0:2], 0.0))
            dve.did(dve.next().tensor_tensor(cu[:, :, 2:2 + S], cc1[:], cx[:], ALU.mult))
            for t in range(2):
                dve.did(dve.next().tensor_scalar(cy[:, t, :], cu[:, t, 0:S], w[:, t, 0:1], None, ALU.mult))
                for j in (1, 2):
                    dve.did(dve.next().scalar_tensor_tensor(
                        out=cy[:, t, :], in0=cu[:, t, j:j + S], scalar=w[:, t, j:j + 1],
                        in1=cy[:, t, :], op0=ALU.mult, op1=ALU.add))
            dve.did(dve.next().tensor_tensor(pair(yT, 2), flat(cb), flat(cy), ALU.mult))

        def decays(l):
            act.did(act.next().activation(flat(lf), flat(zf), ACT.Sigmoid))
            act.did(act.next().activation(flat(rkt), flat(zf), ACT.Sigmoid, scale=-1.0))
            lb = lbl[:, l, :].unsqueeze(1).to_broadcast([P, NT, S])
            om = lbw[:, l, :].unsqueeze(1).to_broadcast([P, NT, S])
            dve.did(dve.next(act.now()).tensor_tensor(lf[:], lf[:], om, ALU.mult))
            dve.did(dve.next().tensor_tensor(lf[:], lf[:], lb, ALU.add))
            dve.did(dve.next().tensor_tensor(rkt[:], rkt[:], om, ALU.mult))
            dve.did(dve.next().tensor_scalar(lf2[:], lf[:], TINY, 1.0 / LN_CUT, ALU.max, ALU.mult))
            dve.did(dve.next().tensor_scalar(lf2[:], lf2[:], 1.0, None, ALU.min))
            dve.did(dve.next().tensor_scalar(lf[:], lf[:], LN_CUT, None, ALU.max))
            act.did(act.next(dve.now()).activation(lf[:], lf[:], ACT.Ln))
            act.did(act.next().activation(lf2[:], lf2[:], ACT.Ln))
            dve.did(dve.next(act.now()).tensor_tensor(lf[:], lf[:], lf2[:], ALU.add))

        def hgrn(l):
            claim(6)
            pe.after(dve.now())
            kp = PS[:, 6, :].rearrange("p (g s) -> p g s", g=2)
            for g in range(2):
                for t in range(NT):
                    mm = nc.tensor.transpose(kp[:, g, t * P:(t + 1) * P], rkt[:, t, g * P:(g + 1) * P], ident[:])
            pe.did(mm)
            act.did(act.next(pe.now()).activation(flat(rk), PS[:, 6, :], ACT.Copy))
            empty(6, 1, act.now())
            for t in range(NT):
                b = 4 * t
                claim(b, 4)
                pe.after(dve.now())
                for g in range(2):
                    for c in range(2):
                        mm = nc.tensor.matmul(PS[:, b + 2 * g + c, :], lf[:, t, g * P:(g + 1) * P],
                                              bsum[:, t, c * 512:(c + 1) * 512], start=True, stop=True)
                pe.did(mm)
                act.did(act.next(pe.now(), dve.now()).activation(
                    qe[t][:].rearrange("p g l s -> p (g l s)"), banks(b, 4), ACT.Exp))
                empty(b, 4, act.now())

            def decayed(t, *after):
                dve.after(*after)
                for g in range(2):
                    over = lambda x: x[:, g, t * P:(t + 1) * P].unsqueeze(1).to_broadcast([P, LEVELS, P])
                    dve.did(dve.engine.tensor_tensor(ke[t][:, g], qe[t][:, g], over(rk), ALU.mult))
                    dve.did(dve.next().tensor_tensor(qe[t][:, g], qe[t][:, g], over(rq), ALU.mult))
                return dve.now()

            exps = back(act, 1), act.now()
            ready = [decayed(0, exps[0]), None]
            for t in range(NT):
                for v in range(LEVELS):
                    b = v % 4 * 2
                    claim(b, 2)
                    pe.after(ready[t])
                    for h in range(4):
                        lo, g = HD * (h % 2), h // 2
                        ks = ke[t][lo:lo + HD, g, v, :] if v < LEVELS - 1 else rk[lo:lo + HD, g, t * P:(t + 1) * P]
                        qs = qe[t][lo:lo + HD, g, v, :] if v < LEVELS - 1 else rq[lo:lo + HD, g, t * P:(t + 1) * P]
                        mm = nc.tensor.matmul(PS[:, b + h % 2, g * P:(g + 1) * P], ks, qs, start=True, stop=True)
                    pe.did(mm)
                    mask = lmask[:, v, :].unsqueeze(1).unsqueeze(1).to_broadcast([P, 2, 2, P])
                    dst = aT[:, t, :] if v == 0 else am
                    dve.did(dve.next(pe.now()).tensor_tensor(
                        dst.rearrange("p (b g s) -> p b g s", b=2, g=2),
                        PS[:, b:b + 2, 0:2 * P].rearrange("p b (g s) -> p b g s", g=2), mask, ALU.mult))
                    empty(b, 2, dve.now())
                    if v:
                        dve.did(dve.next().tensor_tensor(aT[:, t, :], aT[:, t, :], am[:], ALU.add))
                    if t == 0 and v == 1:
                        ready[1] = decayed(1, exps[1])
            claim(0, 2)
            for h in range(4):
                lo, g = HD * (h % 2), h // 2
                mm = nc.tensor.matmul(PS[:, h % 2, g * P:(g + 1) * P], ke[0][lo:lo + HD, g, LEVELS - 1, :],
                                      qe[1][lo:lo + HD, g, LEVELS - 1, :], start=True, stop=True)
            pe.did(mm)
            act.did(act.next(pe.now()).activation(aX.rearrange("p (b s) -> p b s", b=2),
                                                  PS[:, 0:2, 0:2 * P], ACT.Copy))
            empty(0, 2, act.now())
            claim(5)
            pe.after(dve.now(), act.now())
            for h in range(4):
                lo = HD * (h % 2)
                for t in range(NT):
                    out = PS[lo:lo + HD, 5, (h // 2) * S + t * P:(h // 2) * S + (t + 1) * P]
                    hs = slice((h % 2 * 2 + h // 2) * P, (h % 2 * 2 + h // 2 + 1) * P)
                    vs = slice(h * HD, (h + 1) * HD)
                    if t:
                        nc.tensor.matmul(out, ri[:, 0, vs], aX[:, hs], start=True, stop=False,
                                         skip_group_check=True)
                    mm = nc.tensor.matmul(out, ri[:, t, vs], aT[:, t, hs], start=t == 0, stop=True,
                                          skip_group_check=True)
            pe.did(mm)
            evacuate(pair(yT, 3), 5, pe.now())

        def mixer_out(l):
            g = vec1(l, "mix_gain")
            head_norm(yT[:], DK, lambda t: g[:, t:t + 1], hT[:], dve.now())
            dve.did(dve.next().tensor_tensor(pair(yT, 3), pair(yT, 3), rgs[:].rearrange("p t s -> p (t s)"), ALU.mult))
            ready = split(yhi[:], ylo[:], yT[:], dve.now(), pe.now())
            project_to_x(yhi, ylo, ready)

        def open_sums():
            claim(0, 4)
            for b in range(4):
                mm = nc.tensor.matmul(PS[:, b, :], zero[:, 0:P], zero[:], start=True, stop=False,
                                      skip_group_check=True)
            pe.did(mm)

        def down(a_hi, a_lo, ready):
            w_hi, w_lo = take()
            pe.after(ready)
            for f in range(2):
                for d in range(DK):
                    cs = slice(f * D + d * P, f * D + (d + 1) * P)
                    mm = mm3(PS[:, d // 2, (d % 2) * S:(d % 2 + 1) * S], w_hi[:, cs], w_lo[:, cs],
                             a_hi[:, f, :], a_lo[:, f, :], False, False)
            return release(mm)

        def close_sums(step):
            for b in range(4):
                add_to_x(2 * b, b, step)

        used_a = [None, None, None]

        def swiglu_up(i):
            bg, bu = 4 + 2 * i, 5 + 2 * i
            g_step = unit_T(bg, hhi, hlo)
            u_step = unit_T(bu, hhi, hlo)
            act.did(act.next(g_step, dve.now()).activation(sil[i][:], PS[:, bg, :], ACT.Silu))
            empty(bg, 1, act.now())
            dve.did(dve.next(u_step, act.now()).tensor_tensor(sil[i][:], sil[i][:], PS[:, bu, :], ALU.mult))
            empty(bu, 1, dve.now())
            src = sil[i][:].rearrange("p (t s) -> p t s", t=2)
            return split(ahi[i][:], alo[i][:], src, dve.now(), used_a[i])

        def swiglu(groups, steps):
            open_sums()
            ready = swiglu_up(0)
            emptied[6] = emptied[7] = None
            n = (groups - 2) // 2
            with Loop(n, steps, 6) as i:
                settled = [pe_idle(), act.now(), dve.now()]
                for b in range(4, 8):
                    emptied[b] = None
                emptied[4] = settled[1]
                emptied[6], emptied[7] = settled[1], settled[2]
                emptied[5] = settled[2]
                used_a[0] = used_a[1] = None
                r1 = swiglu_up(1)
                used_a[0] = down(ahi[0], alo[0], settled[2])
                swiglu_up(0)
                used_a[1] = down(ahi[1], alo[1], r1)
            done = pe_idle()
            used_a[0] = used_a[1] = done
            for b in range(4, 8):
                emptied[b] = dve.now()
            r1 = swiglu_up(1)
            down(ahi[0], alo[0], r1)
            close_sums(down(ahi[1], alo[1], r1))

        def router():
            wr = vx[:, 8:72].rearrange("p (k e) -> p k e", k=DK)
            claim(4)
            pe.after(dve.now())
            for t in range(NT):
                for k in range(DK):
                    mm = nc.tensor.matmul(PS[:, 4, t * NE:(t + 1) * NE], hT[:, k, t * P:(t + 1) * P],
                                          wr[:, k, :], start=k == 0, stop=k == DK - 1)
            pe.did(mm)
            lg = small[:, 0:16].rearrange("p (t e) -> p t e", t=NT)
            m = small[:, 16:18]
            ex = small[:, 32:48].rearrange("p (t e) -> p t e", t=NT)
            rank = small[:, 48:64].rearrange("p (t e) -> p t e", t=NT)
            gt = small[:, 64:192].rearrange("p (t e j) -> p t e j", t=NT, e=NE)
            eq = small[:, 192:320].rearrange("p (t e j) -> p t e j", t=NT, e=NE)
            before = vx[:, 80:144].rearrange("p (e j) -> p e j", e=NE)
            vv = lambda *a: dve.did(dve.next().tensor_tensor(*a))
            rb = vx[:, 72:80].unsqueeze(1).to_broadcast([P, NT, NE])
            dve.after(pe.now())
            vv(lg, PS[:, 4, 0:16].rearrange("p (t e) -> p t e", t=NT), rb, ALU.add)
            empty(4, 1, dve.now())
            for t in range(NT):
                mine = lg[:, t, :].unsqueeze(2).to_broadcast([P, NE, NE])
                other = lg[:, t, :].unsqueeze(1).to_broadcast([P, NE, NE])
                vv(gt[:, t], other, mine, ALU.is_gt)
                vv(eq[:, t], other, mine, ALU.is_equal)
                vv(eq[:, t], eq[:, t], before, ALU.mult)
                vv(gt[:, t], gt[:, t], eq[:, t], ALU.add)
            dve.did(dve.next().tensor_reduce(rank, gt, AX, ALU.add))
            dve.did(dve.next().tensor_scalar(rank, rank, 1.5, None, ALU.is_lt))
            dve.did(dve.next().tensor_reduce(m, lg, AX, ALU.max))
            vv(ex, lg, m.unsqueeze(2).to_broadcast([P, NT, NE]), ALU.subtract)
            act.did(act.next(dve.now()).activation(ex, ex, ACT.Exp))
            dve.after(act.now())
            vv(ex, ex, rank, ALU.mult)
            dve.did(dve.next().tensor_reduce(m, ex, AX, ALU.add))
            dve.did(dve.next().reciprocal(m, m))
            vv(ex, ex, m.unsqueeze(2).to_broadcast([P, NT, NE]), ALU.mult)
            claim(5)
            pe.after(dve.now())
            for t in range(NT):
                for b in range(t + 1):
                    nc.tensor.matmul(PS[:, 5, t * NE:(t + 1) * NE], tri[:, b, t * P:(t + 1) * P],
                                     rank[:, b, :], start=b == 0, stop=b == t)
            for t in range(NT):
                mm = nc.tensor.matmul(PS[0:1, 5, 32:32 + NE], ones[:, 0:1], rank[:, t, :],
                                      start=t == 0, stop=t == NT - 1)
            pe.did(mm)
            cnt = PS[:, 5, 0:NT * NE].rearrange("p (t e) -> p t e", t=NT)
            dve.after(pe.now())
            vv(slots.rearrange("p (t e) -> p t e", t=NT), cnt, rank, ALU.mult)
            dve.did(dve.next().tensor_scalar(slots, slots, -1.0, None, ALU.add))
            dve.did(dve.next().tensor_reduce(m[0:1, 0:1], PS[0:1, 5, 32:32 + NE], AX, ALU.max))
            dve.did(dve.next().tensor_scalar(overflow[:], m[0:1, 0:1], float(P), None, ALU.is_gt))
            empty(5, 1, dve.now())

        slots = small[:, 384:400]
        gates = small[:, 32:48]
        GF = 512
        GE = D_FF // GF
        rm = Region(arena)
        xghi = rm.put("xghi", [P, NE, DK, P], F32R)
        xglo = rm.put("xglo", [P, NE, DK, P], F32R)
        pm = rm.put("pm", [P, NE, S], F32R)
        xshi = rm.put("xshi", [P, DK, P], F32R)
        xslo = rm.put("xslo", [P, DK, P], F32R)
        msil = rm.put("msil", [P, GF])
        mact = rm.put("mact", [P, GF])
        mahi = rm.put("mahi", [P, GF // P, P], F32R)
        malo = rm.put("malo", [P, GF // P, P], F32R)
        at_pt = rm.top
        pt = rm.put("pt", [P, NT, NE, P], F32R)
        r = Region(at_pt)
        ohi = r.put("ohi", [P, D], F32R)
        olo = r.put("olo", [P, D], F32R)
        assert rm.top <= nc.sbuf_usable_end, (rm.top, nc.sbuf_usable_end)
        htkhi = at("htkhi", [P, NT, D], at_hhi, F32R)
        htklo = at("htklo", [P, NT, D], at_hlo, F32R)
        gsl = small[:, 400:408]
        gs1 = small[:, 408:409]

        def tokens_to_rows():
            for src, dst, b, lane in ((hhi, htkhi, 0, act), (hlo, htklo, 4, dve)):
                claim(b, 4)
                pe.after(dve.now(), act.now())
                for t in range(NT):
                    for k in range(DK):
                        mm = nc.tensor.transpose(banks(b, 4)[:, t * D + k * P:t * D + (k + 1) * P],
                                                 src[:, k, t * P:(t + 1) * P].bitcast(F32), ident[:])
                pe.did(mm)
            act.did(act.next(pe.now()).activation(htkhi[:].rearrange("p t d -> p (t d)"), banks(0, 4), ACT.Copy))
            dve.did(dve.next(pe.now()).tensor_copy(htklo[:].rearrange("p t d -> p (t d)"), banks(4, 4)))
            empty(0, 4, act.now())
            empty(4, 4, dve.now())

        def gather(r):
            sl = small[:, 416:432]
            dve.did(dve.next(act.now(), pe.now()).tensor_scalar(sl, slots, float(-P * r), None, ALU.add))
            dve.did(dve.next().tensor_tensor(
                pt[:].rearrange("p t e s -> p (t e) s"), iota[:].unsqueeze(1).to_broadcast([P, NT * NE, P]),
                sl.unsqueeze(2).to_broadcast([P, NT * NE, P]), ALU.is_equal))
            pe.after(dve.now(), act.now())
            i = 0
            for half in range(2):
                es = slice(4 * half, 4 * half + 4)
                for k in range(DK):
                    b = i % 4 * 2
                    claim(b, 2)
                    for j, src in enumerate((htkhi, htklo)):
                        for t in range(NT):
                            mm = nc.tensor.matmul(PS[:, b + j, :], src[:, t, k * P:(k + 1) * P],
                                                  pt[:, t, es, :], start=t == 0, stop=t == NT - 1)
                    pe.did(mm)
                    v = PS[:, b:b + 2, :].rearrange("p b (e s) -> p b e s", e=4)
                    act.did(act.next(pe.now()).activation(xghi[:, es, k, :], v[:, 0], ACT.Copy))
                    dve.did(dve.next(pe.now()).tensor_copy(xglo[:, es, k, :], v[:, 1]))
                    empty(b, 1, act.now())
                    empty(b + 1, 1, dve.now())
                    i += 1
            claim(0, 5)
            for e in range(NE):
                for t in range(NT):
                    nc.tensor.transpose(banks(0, 4)[:, e * S + t * P:e * S + (t + 1) * P],
                                        pt[:, t, e, :].bitcast(F32), ident[:])
                for t in range(NT):
                    mm = nc.tensor.matmul(PS[:, 4, e:e + 1], pt[:, t, e, :].bitcast(F32),
                                          gates[:, t * NE + e:t * NE + e + 1], start=t == 0, stop=t == NT - 1)
            pe.did(mm)
            act.did(act.next(pe.now()).activation(pm[:].rearrange("p e s -> p (e s)"), banks(0, 4), ACT.Copy))
            dve.did(dve.next(pe.now()).tensor_copy(gsl, PS[:, 4, 0:NE]))
            empty(0, 4, act.now())
            empty(4, 1, dve.now())

        ACC, GATE, UP = 0, 4, 5
        OUT = (2, 3, 6, 7)

        def expert_tokens(e):
            flat = lambda x: x.rearrange("p a k s -> p (a k s)")
            act.did(act.next(pe.now(), pe_idle(), dve.now()).activation(
                xshi[:].rearrange("p k s -> p (k s)"), flat(xghi[:, bass.ds(e, 1), :, :]).bitcast(F32), ACT.Copy))
            dve.did(dve.next(pe.now(), pe_idle()).tensor_copy(
                xslo[:].rearrange("p k s -> p (k s)"), flat(xglo[:, bass.ds(e, 1), :, :]).bitcast(F32)))
            dve.did(dve.next().tensor_copy(gs1, gsl[:, bass.ds(e, 1)]))

        def expert_places(e):
            act.did(act.next(pe.now(), pe_idle()).activation(
                pms[:], pm[:, bass.ds(e, 1), :].rearrange("p a s -> p (a s)").bitcast(F32), ACT.Copy))

        def group_up(gate_free, up_free, sil_free):
            steps = []
            for b, free in ((GATE, gate_free), (UP, up_free)):
                for half in range(2):
                    w_hi, w_lo = take()
                    if half == 0:
                        pe.after(*free)
                    for k in range(4):
                        cs = slice(k * GF, (k + 1) * GF)
                        kk = 4 * half + k
                        mm = mm3(PS[:, b, :], xshi[:, kk, :], xslo[:, kk, :], w_hi[:, cs],
                                 None if w_lo is None else w_lo[:, cs], kk == 0, kk == 7)
                    step = release(mm)
                steps.append(step)
            act.did(act.next(steps[0], sil_free).activation(msil[:], PS[:, GATE, :], ACT.Silu))
            dve.did(dve.next(act.now(), steps[1]).scalar_tensor_tensor(
                out=mact[:], in0=msil[:], scalar=gs1, in1=PS[:, UP, :], op0=ALU.mult, op1=ALU.mult))
            return dve.now()

        def group_turn(ready):
            pe.after(ready)
            for f in range(GF // P):
                mm = nc.tensor.transpose(PS[:, UP, f * P:(f + 1) * P], mact[:, f * P:(f + 1) * P], ident[:])
            pe.did(mm)
            src = PS[:, UP, :].rearrange("p (f s) -> p f s", s=P)
            act.did(act.next(pe.now()).activation(mahi[:], src, ACT.Copy))
            dve.did(dve.next(act.now(), pe.now()).tensor_tensor(malo[:], src, mahi[:].bitcast(F32), ALU.subtract))

        def group_down(ready_act, ready_dve):
            for half in range(2):
                w_hi, w_lo = take()
                if half == 0:
                    pe.after(ready_act, ready_dve)
                for f in range(2):
                    for c in range(2):
                        cs = slice(f * D + c * 512, f * D + (c + 1) * 512)
                        mm = mm3(PS[:, ACC + c, :], mahi[:, 2 * half + f, :], malo[:, 2 * half + f, :],
                                 w_hi[:, cs], None if w_lo is None else w_lo[:, cs], False, False)
                step = release(mm)
            return step

        def open_acc():
            for c in range(2):
                mm = nc.tensor.matmul(PS[:, ACC + c, :], zero[:, 0:P].bitcast(F32R), zero[:].bitcast(F32R),
                                      start=True, stop=False, skip_group_check=True)
            return mm

        def take_out(step):
            act.did(act.next(step).activation(ohi[:], banks(ACC, 2), ACT.Copy))
            dve.did(dve.next(act.now(), step).tensor_tensor(olo[:], banks(ACC, 2), ohi[:].bitcast(F32), ALU.subtract))

        def scatter(out_act, out_dve):
            pe.after(out_act, out_dve)
            for q, b in enumerate(OUT):
                for f in range(2):
                    cs = slice((2 * q + f) * P, (2 * q + f + 1) * P)
                    out = PS[:, b, f * S:(f + 1) * S]
                    nc.tensor.matmul(out, ohi[:, cs], pms[:], start=True, stop=False)
                    mm = nc.tensor.matmul(out, olo[:, cs], pms[:], start=False, stop=True)
                pe.did(mm)
                dst = xT[:, 2 * q:2 * q + 2, :].rearrange("p t s -> p (t s)")
                dve.did(dve.next(pe.now()).tensor_tensor(dst, dst, PS[:, b, :], ALU.add))

        def groups_of_expert():
            with Loop(GE - 1, (1, 2, 2), 6):
                ready = act.now(), dve.now()
                up = group_up([back(act, 1)], ready, dve.now())
                group_down(*ready)
                group_turn(up)

        def experts():
            expert_tokens(0)
            expert_places(0)
            pe.after(act.now(), dve.now())
            pe.did(open_acc())
            group_turn(group_up([], [], None))
            with Loop(NE - 1, EXPERT_STEPS, 6 * (GE - 1) + 6) as e:
                groups_of_expert()
                ready = act.now(), dve.now()
                expert_tokens(e + 1)
                tokens = act.now(), dve.now()
                take_out(group_down(*ready))
                out = act.now(), dve.now()
                up = group_up(tokens, ready, out[1])
                scatter(*out)
                expert_places(e + 1)
                open_acc()
                group_turn(up)
            groups_of_expert()
            take_out(group_down(act.now(), dve.now()))
            scatter(act.now(), dve.now())

        def routed_ffn():
            nonlocal stream
            settle()
            tokens_to_rows()
            gather(0)
            moe_start = main.at()
            experts()
            settle()
            for engine in (nc.sync, nc.gpsimd):
                engine.wait_ge(dve.sem, dve.base + dve.count)
            flag = nc.values_load(overflow[0:1, 0:1], min_val=0, max_val=1,
                                  skip_runtime_bounds_check_because="it is the result of a comparison")
            with nc.If(flag > 0):
                kept = [(x.sem, x.base, x.count) for x in (pe, act, dve)]
                for x, name in zip((pe, act, dve), ("pe", "act", "dve")):
                    x.sem, x.base, x.count = sem(f"overflow_{name}_steps"), 0, 0
                stream = Whole([slow_raw], 0, [sem("overflow_landed")], sem("overflow_used"),
                               first_unit=moe_start, used0=1)
                open_acc().then_inc(stream.used, 1)
                pe.did(open_acc())
                act.did(act.next(pe.now()).activation(small[:, 440:441], gates[:, 0:1], ACT.Copy))
                dve.did(dve.next(act.now()).tensor_copy(small[:, 441:442], gates[:, 0:1]))
                gather(1)
                experts()
                settle()
                nc.sync.wait_ge(dve.sem, dve.base + dve.count)
                stream = main
                for x, (a, b, c) in zip((pe, act, dve), kept):
                    x.sem, x.base, x.count = a, b, c
            settle()

        def vec1_of(l, name):
            g = vec1(l, name)
            return lambda t: g[:, t:t + 1]

        for l in range(DEPTH):
            whole_norm(vec1_of(l, "norm_mix"))
            forgetting_attention(l)
            pe.after(act.now(), dve.now())
            act.after(pe.now())
            dve.after(pe.now(), act.now())
            hgrn(l)
            dve.after(act.now())
            mixer_out(l)
            whole_norm(vec1_of(l, "norm_ffn"))
            if l % 2 == 0:
                swiglu(G1, (0, 4, 4))
            else:
                router()
                routed_ffn()

        settle()
        c2 = Region(arena)
        rope_in = {n: c2.put(n, io[n].shape) for n in ("cosA", "sinA", "rotA", "cosB", "sinB", "rotB",
                                                        "cosC", "sinC", "rotC", "selC", "selCT")}
        vl = c2.put("vl", [P, V2N])
        nlam = c2.put("nlam", [P, 4])
        y2 = c2.put("y2", [P, 12, S])
        sg = c2.put("sg", [P, 24, S])
        soft = c2.top
        rp = Region(soft)
        pb2 = [rp.put(f"pb2{i}", [P, 4, S]) for i in range(PB)]
        pt2 = [rp.put(f"pt2{i}", [P, 4, NT, P]) for i in range(2)]
        r = Region(soft)
        chi = r.put("chi", [P, 5, S], F32R)
        clo = r.put("clo", [P, 5, S], F32R)
        r = Region(soft)
        y2hi = r.put("y2hi", [P, 12, S], F32R)
        y2lo = r.put("y2lo", [P, 12, S], F32R)
        r = Region(rp.top)
        cc = r.put("cc", [P, 6, S])
        vc = r.put("vc", [P, NT, 512])
        qk = r.top
        qa = r.put("qa", [P, 6, S])
        va = r.put("va", [P, NT, P])
        qkb = r.put("qkb", [P, 8, S])
        vb = r.put("vb", [P, NT, 512])
        end2 = r.top
        r = Region(qk)
        qc = r.put("qc", [P, NH, S])
        kc = r.put("kc", [P, NH, S])
        r = Region(rp.top)
        mg = r.put("mg", [P, DK, S])
        mhi = r.put("mhi", [P, DK, S], F32R)
        mlo = r.put("mlo", [P, DK, S], F32R)
        gs = [r.put(f"gs{i}", [P, 512]) for i in range(2)]
        end2 = max(end2, r.top)
        r = Region(soft)
        rl = [r.put(f"rl{i}", [P, 512]) for i in range(3)]
        bhi = [r.put(f"bhi{i}", [P, 2, S], F32R) for i in range(3)]
        blo = [r.put(f"blo{i}", [P, 2, S], F32R) for i in range(3)]
        assert max(end2, r.top) <= nc.sbuf_usable_end, (end2, r.top)
        loaded2 = sem("second_loaded")
        for n, t in rope_in.items():
            nc.scalar.dma_start(t[:], io[n]).then_inc(loaded2, 16)
        tables = Step(loaded2, 16 * len(rope_in))

        def vec2(name):
            return vl[:, V2[name][0]:V2[name][1]]

        def column(name, n=1):
            return lambda t: vec2(name)[:, (t if n > 1 else 0):(t if n > 1 else 0) + 1]

        def rope(buf, nt, n, which, tmp):
            rot, cos, sin = (rope_in[x + which] for x in ("rot", "cos", "sin"))
            k = (nt + 1) // 2
            ready = dve.now(), act.now()
            fill()
            claim(0, k)
            pe.after(*ready)
            out = banks(0, k).rearrange("p (t s) -> p t s", s=S)
            for t in range(nt):
                mm = nc.tensor.matmul(out[0:n, t, :], rot[0:n, 0:n], buf[:, t, :], start=True, stop=True)
            turned = pe.did(mm)
            fill()
            wide = lambda x: x[0:n, :].unsqueeze(1).to_broadcast([n, nt, S])
            dve.did(dve.next(turned).tensor_tensor(tmp, out[0:n, 0:nt, :], wide(sin), ALU.mult))
            empty(0, k, dve.now())
            dve.did(dve.next().tensor_tensor(buf, buf, wide(cos), ALU.mult))
            dve.did(dve.next().tensor_tensor(buf, buf, tmp, ALU.add))

        def four_heads(t, c, operands, value, y_tiles, **more):
            return Job(lambda i: operands(4 * c + SLOT[i], t), value=lambda i, b: value(4 * c + SLOT[i], b),
                       place=lambda i: (HD * (SLOT[i] % 2), SLOT[i] // 2),
                       dst=y2[:, y_tiles + 2 * c:y_tiles + 2 * c + 2, t * P:(t + 1) * P], **more)

        def branch_a():
            for i in range(3):
                evacuate(pair(qa, i), 4 + i % 2, unit_T(4 + i % 2, hhi, hlo))
            for i in range(4):
                by_unit(unit_T, pair(qkb, i), scale=32 ** -0.5 if i < 2 else 1.0)
            for i in range(2):
                def values(i=i):
                    step = unit_tok(7, hhi, hlo)
                    act.did(act.when(step).activation(
                        vb[:, :, i * UC:(i + 1) * UC], PS[:, 7, :].rearrange("p (t c) -> p t c", t=NT), ACT.Copy))
                    empty(7, 1, act.now())
                fillers.append(values)
            for i in range(3):
                by_unit(unit_T, pair(cc, i))
            for i in range(12):
                by_unit(unit_T, pair(sg, i), func=ACT.Sigmoid)
            pe.after(tables)
            dve.after(tables)
            lam = vec2("lam").rearrange("p (a b d) -> p a b d", a=2, b=2)
            pr = small[:, 64:128].rearrange("p (a d) -> p a d", a=2)
            dve.did(dve.next().tensor_tensor(pr, lam[:, :, 0, :], lam[:, :, 1, :], ALU.mult))
            dve.did(dve.next().tensor_reduce(nlam[:, 0:2], pr, AX, ALU.add))
            act.did(act.next(dve.now()).activation(nlam[:, 0:2], nlam[:, 0:2], ACT.Exp))
            dve.did(dve.next(act.now()).tensor_tensor(nlam[:, 2:3], nlam[:, 1:2], nlam[:, 0:1], ALU.subtract))
            dve.did(dve.next().tensor_tensor(nlam[:, 2:3], nlam[:, 2:3], vec2("lam_init"), ALU.subtract))
            qs = nlam[:, 3:4]
            dve.did(dve.next(act.now()).tensor_scalar(qs, vec2("aq"), HD ** -0.5, None, ALU.mult))
            head_norm(qa[:, 0:5, :], 5, lambda t: qs if t < 4 else vec2("ak"), hT[:, 0:5, :], dve.now())
            rope(qa[:, 0:5, :], 5, P, "A", hT[:, 0:5, :])
            claim(4)
            pe.after(act.now(), dve.now())
            for t in range(NT):
                mm = nc.tensor.transpose(PS[:, 4, t * P:(t + 1) * P], qa[:, 5, t * P:(t + 1) * P], ident[:])
            pe.did(mm)
            act.did(act.when(pe.now()).activation(va[:].rearrange("p t c -> p (t c)"), PS[:, 4, 0:S], ACT.Copy))
            empty(4, 1, act.now())
            jobs = []
            for t in range(NT):
                for c in range(2):
                    def head(i, c=c):
                        return 4 * (i // 2) + 2 * c + i % 2

                    def operands(i, t=t, head=head):
                        h, lo = head(i), HD * (i // 2)
                        return qa[lo:lo + HD, h % 4, t * P:(t + 1) * P], qa[lo:lo + HD, 4, :]
                    jobs.append(Job(operands,
                                    value=lambda i, b: va[:, b, i // 2 * HD:(i // 2 + 1) * HD],
                                    place=lambda i: (HD * (i % 2), i // 2),
                                    dst=y2[:, c:4:2, t * P:(t + 1) * P]))
            attention(jobs, pb2, pt2, stat)

        def branch_b():
            fill(max(0, len(fillers) - 15))
            pe.after(act.now())
            dve.after(act.now())
            rope(qkb[:], 8, P, "B", hT[:])
            pe.after(dve.now())
            jobs = []
            for t in range(NT):
                for c in range(2):
                    for part in range(2):
                        def operands(h, t, part=part):
                            lo = HD * (h % 2) + 32 * part
                            return qkb[lo:lo + 32, h // 2, t * P:(t + 1) * P], qkb[lo:lo + 32, 4 + h // 2, :]
                        j = four_heads(t, c, operands, lambda h, b: vb[:, b, h * HD:(h + 1) * HD], 4,
                                       less=nlam[:, 2:3] if part else None)
                        if part == 0:
                            j.value = None
                        jobs.append(j)
            attention(jobs, pb2, pt2, stat, fill_every=2)
            g = nlam[:, 3:4]
            dve.did(dve.next(act.now()).tensor_scalar(g, vec2("lam_init"), -1.0, 1.0, ALU.mult, ALU.add))
            dve.did(dve.next().tensor_tensor(g, g, vec2("bsub"), ALU.mult))
            head_norm(y2[:, 4:8, :], 4, lambda t: g, hT[:, 0:4, :], dve.now())

        NOPE, ROT = 64, 32
        QW = NOPE + ROT

        def branch_c():
            fill(max(0, len(fillers) - 12))
            sel_c, sel_ct = rope_in["selC"], rope_in["selCT"]
            lat = cc[:, 0:5, :]
            group_rstd(lat, 5, lambda t: sel_c[:, t, :], 16, 1.0, hT[:, 0:5, :], dve.now(), act.now())
            gains = lambda t: column("cq", 3)(t) if t < 3 else column("ckv", 2)(t - 3)
            apply_rstd(lat, lat, 5, lambda t: sel_ct[:, t, :], 16, gains, [4, 5])
            ready = split(chi[:], clo[:], lat, dve.now())
            rope(cc[0:QW, 5:6, :], 1, QW, "C", hT[0:QW, 0:1, :])
            act.did(act.next(dve.now()).activation(
                kc[NOPE:QW, :, :], cc[NOPE:QW, 5:6, :].to_broadcast([ROT, NH, S]), ACT.Copy))
            fill(len(fillers))
            for i in range(2):
                w_hi, w_lo = take()
                claim(4 + 2 * i, 2)
                pe.after(ready)
                wh, wl = (w[:, 0:3 * 4 * QW].rearrange("p (k c) -> p k c", k=3) for w in (w_hi, w_lo))
                out = banks(4 + 2 * i, 2).rearrange("p (h s) -> p h s", s=S)
                for h in range(4):
                    cs = slice(h * QW, (h + 1) * QW)
                    for k in range(3):
                        mm = mm3(out[0:QW, h, :], wh[:, k, cs], wl[:, k, cs], chi[:, k, :], clo[:, k, :],
                                 k == 0, k == 2)
                step = release(mm)
                act.did(act.when(step).activation(qc[0:QW, 4 * i:4 * i + 4, :], out[0:QW, :, :], ACT.Copy,
                                                  scale=QW ** -0.5))
                empty(4 + 2 * i, 2, act.now())
            w_hi, w_lo = take()
            wh, wl = (w[:].rearrange("p (k c) -> p k c", k=2) for w in (w_hi, w_lo))
            claim(0, 8)
            out = banks(4, 4).rearrange("p (h s) -> p h s", s=S)
            for h in range(NH):
                for k in range(2):
                    mm3(out[:, h, :], wh[:, k, h * P:(h + 1) * P], wl[:, k, h * P:(h + 1) * P],
                        chi[:, 3 + k, :], clo[:, 3 + k, :], k == 0, k == 1)
            for t in range(NT):
                ts = slice(t * P, (t + 1) * P)
                for k in range(2):
                    vh, vl_ = (w[:, k, :].rearrange("p (h c) -> p h c", h=NH)[:, :, NOPE:] for w in (wh, wl))
                    mm = mm3(PS[:, t, :], chi[:, 3 + k, ts], clo[:, 3 + k, ts], vh, vl_, k == 0, k == 1)
            step = release(mm)
            act.did(act.when(step).activation(kc[0:NOPE, :, :], out[0:NOPE, :, :], ACT.Copy))
            act.did(act.when().activation(vc[:].rearrange("p t c -> p (t c)"), banks(0, 2), ACT.Copy))
            empty(0, 8, act.now())
            dve.after(act.now())
            rope(qc[0:QW, :, :], NH, QW, "C", hT[0:QW, :, :])
            pe.after(dve.now(), act.now())
            jobs = [four_heads(t, c, lambda h, t: (qc[0:QW, h, t * P:(t + 1) * P], kc[0:QW, h, :]),
                               lambda h, b: vc[:, b, h * HD:(h + 1) * HD], 8)
                    for t in range(NT) for c in range(2)]
            attention(jobs, pb2, pt2, stat)

        def merge():
            ready = split(y2hi[:], y2lo[:], y2[:], act.now(), pe.now())
            for jj in range(2):
                for n in range(3):
                    b = 4 + 2 * ((3 * jj + n) % 2)
                    w_hi, w_lo = take()
                    claim(b, 2)
                    pe.after(ready)
                    wh, wl = (w[:].rearrange("p (k c) -> p k c", k=4) for w in (w_hi, w_lo))
                    for f in range(4):
                        for k in range(4):
                            mm = mm3(PS[:, b + f // 2, f % 2 * S:(f % 2 + 1) * S],
                                     wh[:, k, f * P:(f + 1) * P], wl[:, k, f * P:(f + 1) * P],
                                     y2hi[:, 4 * n + k, :], y2lo[:, 4 * n + k, :], k == 0, k == 3)
                    step = release(mm)
                    for i in range(2):
                        dst = pair(mg, 2 * jj + i)
                        dve.did(dve.next(step).tensor_tensor(
                            dst if n == 0 else gs[i][:], pair(sg, 4 * n + 2 * jj + i), PS[:, b + i, :], ALU.mult))
                        empty(b + i, 1, dve.now())
                        if n:
                            dve.did(dve.next().tensor_tensor(dst, dst, gs[i][:], ALU.add))
            project_to_x(mhi, mlo, split(mhi[:], mlo[:], mg[:], dve.now(), pe.now()))

        used_b = [None] * 3

        def relu_up(i):
            step = unit_T(4 + i, hhi, hlo)
            act.did(act.next(step, dve.now()).activation(rl[i][:], PS[:, 4 + i, :], ACT.Relu))
            empty(4 + i, 1, act.now())
            dve.did(dve.next(act.now()).tensor_tensor(rl[i][:], rl[i][:], rl[i][:], ALU.mult))
            return split(bhi[i][:], blo[i][:], rl[i][:].rearrange("p (t s) -> p t s", t=2), dve.now(), used_b[i])

        def relu_ffn(steps):
            open_sums()
            ready = relu_up(0)
            with Loop((G2 - 1) // 3, steps, 6):
                before_act, before_dve = act.now(), dve.now()
                for b in range(4, 7):
                    emptied[b] = before_act
                for j in range(3):
                    used_b[j] = None
                r = before_dve
                for j in range(3):
                    r2 = relu_up((j + 1) % 3)
                    used_b[j] = down(bhi[j], blo[j], r)
                    r = r2
            close_sums(down(bhi[0], blo[0], dve.now()))

        def layer2(l):
            settle()
            src = v2[:, bass.ds(l, 1), :].rearrange("p a c -> p (a c)")
            dve.did(dve.next().tensor_copy(vl[:], src))
            whole_norm(column("ln1", 8))
            branch_a()
            branch_b()
            branch_c()
            merge()
            whole_norm(column("ln2", 8))
            relu_ffn((0, 6, 6))

        with Loop(DEPTH, LAYER_STEPS, U_BLK2) as l:
            layer2(l)
        settle()
        whole_norm(lambda t: vx[:, t:t + 1], split_it=False)
        nc.sync.wait_ge(dve.sem, dve.base + dve.count)
        nc.sync.dma_start(io["out"], hT[:]).then_inc(stored, 16)
        nc.sync.wait_ge(stored, 16)


def constants():
    f = np.float32
    s, t = np.arange(P)[:, None], np.arange(S)[None, :]
    c = {}
    c["tri"] = np.stack([(s + b * P <= t) for b in range(NT)], 1).astype(f)
    c["cmask"] = np.stack([np.where(t <= s + b * P, 0.0, NEG) for b in range(NT)], 1).astype(f)
    tt = np.arange(P)[None, :]
    bsum = np.zeros((P, NT, LEVELS, P), f)
    lmask = np.zeros((P, LEVELS, P), f)
    for v in range(LEVELS - 1):
        n = 1 << v
        mid = tt // (2 * n) * (2 * n) + n - 1
        m = np.where(tt > mid, (s > mid) & (s <= tt), (s > tt) & (s <= mid))
        bsum[:, :, v, :] = m[:, None, :]
        lmask[:, v, :] = (s // (2 * n) == tt // (2 * n)) & (s // n % 2 == 0) & (tt // n % 2 == 1)
    bsum[:, 0, LEVELS - 1, :] = s > tt
    bsum[:, 1, LEVELS - 1, :] = s <= tt
    lmask[:, LEVELS - 1, :] = s == tt
    c["bsum"], c["lmask"] = bsum.reshape(P, NT, -1), lmask
    def angles(pos, dim, theta):
        inv = (f(theta) ** (-np.arange(0, dim, 2, dtype=f) / f(dim))).astype(f)
        return (pos.astype(f)[:, None] * inv[None, :]).astype(f).T

    def rotary(n, spans):
        cos, sin, rot = np.ones((n, S), f), np.zeros((n, S), f), np.zeros((n, n), f)
        for a, ang in spans:
            h = len(ang)
            for i in (0, h):
                cos[a + i:a + i + h], sin[a + i:a + i + h] = np.cos(ang), np.sin(ang)
            for i in range(h):
                rot[a + h + i, a + i], rot[a + i, a + h + i] = -1, 1
        return cos, sin, rot

    pos = np.arange(S)
    row, col = angles(pos // 64, 32, 10000.0), angles(pos % 64, 32, 10000.0)
    spans = dict(A=(P, [(a + o, g) for a in (0, 64) for o, g in ((0, row), (32, col))]),
                 B=(P, [(a, angles(pos, 8, 500000.0)) for a in range(0, P, 32)]),
                 C=(96, [(64, angles(pos, 32, 10000.0))]))
    for which, (n, sp) in spans.items():
        c["cos" + which], c["sin" + which], c["rot" + which] = rotary(n, sp)
    sel_c = np.zeros((P, 5, 16), f)
    sel_c[:, 0:3, 0] = 1 / 384
    sel_c[:, 3:5, 1] = 1 / 256
    c["selC"] = sel_c
    c["selCT"] = np.ascontiguousarray((sel_c != 0).astype(f).transpose(2, 1, 0))
    c["onehot"] = np.repeat(np.eye(NH, dtype=f)[:, :, None], P, 2)
    c["ident"] = np.eye(P, dtype=f)
    c["iota"] = np.broadcast_to(np.arange(P, dtype=f), (P, P)).copy()
    half = np.arange(P) // HD
    selw = np.zeros((P, DK, 16), f)
    for k in range(DK):
        selw[np.arange(P), k, 2 * k + half] = 1
    c["selw"] = selw
    c["selT"] = np.ascontiguousarray(selw.transpose(2, 1, 0))
    return c


def by_part(v):
    return np.moveaxis(v.reshape(*v.shape[:-1], -1, P), -1, 0)


def k_units(w, cols=UC):
    K, N = w.shape
    return w.reshape(K // P, P, N // cols, cols).transpose(2, 1, 0, 3).reshape(N // cols, P, -1)


def down_units(w):
    return w.reshape(-1, 2, P, w.shape[1]).transpose(0, 2, 1, 3).reshape(-1, P, 2 * w.shape[1])


def pipelined(up, dn):
    out = [up[0]]
    for g in range(len(up) - 1):
        out += [up[g + 1], dn[g:g + 1]]
    return out + [dn[-1:]]


def pack(inp):
    f = np.float32
    units = []
    w_in, w_out = inp["w_in"], inp["w_out"]
    for l in range(DEPTH):
        w = w_in[l]
        units.append(k_units(w[:, 0:1536]))
        rest = k_units(w[:, 1544:1544 + 1792])
        units.append(rest[[4, 0, 1, 2, 3, 5, 6]])
        units.append(k_units(w_out[l]))
        if l == 0:
            a = np.stack([k_units(inp["ffn_w_gate"][0]), k_units(inp["ffn_w_up"][0])], 1)
            units += pipelined(a, down_units(inp["ffn_w_down"][0]))
        else:
            wide = lambda w: w.reshape(NE, 2, 4, P, 7, 512).transpose(0, 4, 1, 3, 2, 5).reshape(NE, 7, 2, P, UNIT)
            gu = np.concatenate([wide(inp["moe_w_gate"][0]), wide(inp["moe_w_up"][0])], 2)
            dn = inp["moe_w_down"][0].reshape(NE, 7, 2, 2, P, D).transpose(0, 1, 2, 4, 3, 5).reshape(NE, 7, 2, P, UNIT)
            units.append(gu[0, 0])
            for e in range(NE):
                for g in range(6):
                    units += [gu[e, g + 1], dn[e, g]]
                units.append(dn[e, 6])
                if e + 1 < NE:
                    units.append(gu[e + 1, 0])
            del gu, dn
    for l in range(DEPTH):
        w = inp["w_in_2"][l]
        perm = [h * HD + d for t in range(4) for h in (t, t + 4) for d in range(HD)]
        units.append(k_units(w[:, 0:512][:, perm]))
        units.append(k_units(w[:, 512:768]))
        units.append(k_units(w[:, 768:2304]))
        lat = np.zeros((D, 768), f)
        lat[:, 0:640] = w[:, 2304:2944]
        lat[:, 640 + 64:640 + 96] = w[:, 2944:2976]
        units.append(k_units(lat))
        units.append(k_units(w[:, 2976:]))
        uq = k_units(inp["c_w_uq_2"][l], 384)
        units.append(np.concatenate([uq, np.zeros((2, P, UNIT - uq.shape[2]), f)], 2))
        units.append(k_units(inp["c_w_ukv_2"][l], 1024))
        for jj in range(2):
            for n in range(3):
                units.append(k_units(inp["w_branch_2"][l][n][:, jj * 512:(jj + 1) * 512], 512))
        units.append(k_units(inp["w_out_2"][l]))
        units += pipelined(k_units(inp["w_ff1_2"][l])[:, None], down_units(inp["w_ff2_2"][l]))
    units.append(np.zeros((LEAD, P, UNIT), f))
    arrays = {"ws": np.concatenate(units, 0)}
    arrays["xT"] = by_part(np.ascontiguousarray(inp["x"][0])).transpose(0, 2, 1)
    rep = lambda v: np.broadcast_to(v, (P,) + v.shape)
    two = lambda v: np.concatenate([v, v])[:, None]
    v1 = []
    for l in range(DEPTH):
        wf = w_in[l][:, 1536:1544].reshape(DK, P, NH).transpose(1, 0, 2).reshape(P, -1)
        conv = inp["conv_w"][l].reshape(3, 2, P).transpose(2, 1, 0).reshape(P, 6)
        v1.append(np.concatenate([by_part(inp["norm_mix"][l]), by_part(inp["norm_ffn"][l]),
                                  by_part(inp["mix_out_gain"][l]), two(inp["q_norm_gain"][l]),
                                  two(inp["k_norm_gain"][l]), conv, rep(inp["attn_f_bias"][l]), wf], 1))
    arrays["v1"] = np.stack(v1, 1)
    v2 = []
    for l in range(DEPTH):
        v2.append(np.concatenate([by_part(inp["ln1_g_2"][l]), by_part(inp["ln2_g_2"][l]),
                                  two(inp["a_q_norm_2"][l]), two(inp["a_k_norm_2"][l]),
                                  two(inp["b_subln_2"][l]), by_part(inp["c_q_norm_2"][l]),
                                  by_part(inp["c_kv_norm_2"][l]), rep(inp["b_lambda_2"][l].reshape(-1)),
                                  np.full((P, 1), LAMBDA_INIT[l], f)], 1))
    arrays["v2"] = np.stack(v2, 1)
    wr = inp["moe_router_w"][0].reshape(DK, P, NE).transpose(1, 0, 2).reshape(P, -1)
    arrays["vx"] = np.concatenate([by_part(inp["final_g_2"]), wr, rep(inp["moe_router_b"][0]),
                                   rep(np.tril(np.ones((NE, NE), np.float32), -1).reshape(-1))], 1)
    arrays["lbw"] = rep(inp["hgrn_lb_logits"])
    arrays.update(constants())
    return {k: np.ascontiguousarray(v) for k, v in arrays.items()}


def kernel(**inputs):
    import concourse.bacc as bacc
    from concourse.bass_utils import run_bass_kernel_spmd as run

    arrays = pack({k: np.asarray(v) for k, v in inputs.items()})
    nc = bacc.Bacc("TRN2", target_bir_lowering=False, num_devices=1, dynamic_dma_scratch_size=1024)
    io = {k: nc.dram_tensor(f"in_{k}", a.shape, F32, kind="ExternalInput").ap() for k, a in arrays.items()}
    io["out"] = nc.dram_tensor("out_T", (P, DK, S), F32, kind="ExternalOutput").ap()
    build(nc, io)
    r = run(nc, [{f"in_{k}": a for k, a in arrays.items()}], core_ids=[0])
    out = r.results[0]["out_T"]
    return np.ascontiguousarray(out.transpose(2, 1, 0)).reshape(1, S, D)
```
